# Optimizing a Trainium2 kernel written in Bass

```python
import math
import jax, jax.numpy as jnp
from jax import lax
import numpy as np

D_MODEL = 2048
BATCH = 1
SEQ = 256
DEPTH = 2

N_MEM = 256
MEM_HEADS = 4
MEM_HEAD_DIM = 128
MEM_WIDTH = MEM_HEADS * MEM_HEAD_DIM
MIX_WIDTH = D_MODEL
TOKEN_WIDTH = MIX_WIDTH - MEM_WIDTH

POOL_GROUPS = 4
POOL_WINDOWS = (2, 4, 8, 16)
POOL_GROUP_DIM = TOKEN_WIDTH // POOL_GROUPS

MLA_HEADS = 12
QK_NOPE_DIM = 128
QK_ROPE_DIM = 64
V_HEAD_DIM = 128
Q_LORA_RANK = 512
KV_LORA_RANK = 512
ROPE_THETA = 10000.0
Q_BLOCK = 128
MLA_SCALE = (QK_NOPE_DIM + QK_ROPE_DIM) ** -0.5
MLA_IN_WIDTH = Q_LORA_RANK + KV_LORA_RANK + QK_ROPE_DIM + MEM_WIDTH
MLA_OUT_WIDTH = MLA_HEADS * V_HEAD_DIM + MEM_WIDTH

D_FF = 5632
CONV_WIDTH = 3

N_POOL_LAYERS = (DEPTH + 1) // 2
N_MLA_LAYERS = DEPTH // 2

ALPHA = (2 * DEPTH) ** 0.25
BETA = (8 * DEPTH) ** -0.25

LN_EPS = 1e-5
RMS_EPS = 1e-6

kernel_name = "hybrid_pool_mla_memory_encoder"

def layer_norm(u, g, b):
    uf = u.astype(jnp.float32)
    mu = jnp.mean(uf, axis=-1, keepdims=True)
    var = jnp.mean(jnp.square(uf - mu), axis=-1, keepdims=True)
    y = (uf - mu) * lax.rsqrt(var + LN_EPS)
    return (y * g.astype(jnp.float32) + b.astype(jnp.float32)).astype(u.dtype)

def rms_norm(u, g):
    uf = u.astype(jnp.float32)
    y = uf * lax.rsqrt(jnp.mean(jnp.square(uf), axis=-1, keepdims=True) + RMS_EPS)
    return (y * g.astype(jnp.float32)).astype(u.dtype)

def rotary_tables(positions):
    inv_freq = ROPE_THETA ** (-jnp.arange(0, QK_ROPE_DIM, 2, dtype=jnp.float32) / QK_ROPE_DIM)
    ang = positions.astype(jnp.float32)[..., None] * inv_freq
    return jnp.cos(ang), jnp.sin(ang)

def apply_rotary(u, cos, sin):
    uf = u.astype(jnp.float32)
    half = QK_ROPE_DIM // 2
    u1, u2 = uf[..., :half], uf[..., half:]
    out = jnp.concatenate([u1 * cos - u2 * sin, u2 * cos + u1 * sin], axis=-1)
    return out.astype(u.dtype)

def centred_window_mean(u, w):
    B, S, C = u.shape
    uf = u.astype(jnp.float32)
    cs = jnp.concatenate([jnp.zeros((B, 1, C), jnp.float32), jnp.cumsum(uf, axis=1)], axis=1)
    t = jnp.arange(S)
    lo = jnp.clip(t - w // 2, 0, S)
    hi = jnp.clip(t + w // 2, 0, S)
    total = jnp.take(cs, hi, axis=1) - jnp.take(cs, lo, axis=1)
    count = (hi - lo).astype(jnp.float32)
    return total / count[None, :, None]

def pool_mixer(u, group_w, scale):
    B, S, _ = u.shape
    g = u.reshape(B, S, POOL_GROUPS, POOL_GROUP_DIM)
    pooled = jnp.stack(
        [centred_window_mean(g[:, :, k], POOL_WINDOWS[k]) - g[:, :, k].astype(jnp.float32)
         for k in range(POOL_GROUPS)], axis=2).astype(u.dtype)
    y = jnp.einsum('bsgc,gcd->bsgd', pooled, group_w).reshape(B, S, TOKEN_WIDTH)
    return y * scale

def memory_attention(q, mem, w_kv):
    B, S, _ = q.shape
    kv = mem @ w_kv
    k = kv[..., :MEM_WIDTH].reshape(B, N_MEM, MEM_HEADS, MEM_HEAD_DIM)
    v = kv[..., MEM_WIDTH:].reshape(B, N_MEM, MEM_HEADS, MEM_HEAD_DIM)
    qh = q.reshape(B, S, MEM_HEADS, MEM_HEAD_DIM)
    s = jnp.einsum('bshd,bmhd->bhsm', qh, k).astype(jnp.float32) * (MEM_HEAD_DIM ** -0.5)
    p = jax.nn.softmax(s, axis=-1).astype(v.dtype)
    return jnp.einsum('bhsm,bmhd->bshd', p, v).reshape(B, S, MEM_WIDTH)

def mla_attention(q_nope, q_rope, k_nope, k_rope, v):
    B, S, H, _ = q_nope.shape
    nblk = S // Q_BLOCK

    def to_blocks(t):
        return jnp.moveaxis(t.reshape(B, nblk, Q_BLOCK, *t.shape[2:]), 1, 0)

    def attend(blk):
        qn, qr = blk
        s = (jnp.einsum('bqhd,bkhd->bhqk', qn, k_nope)
             + jnp.einsum('bqhr,bkr->bhqk', qr, k_rope))
        p = jax.nn.softmax(s.astype(jnp.float32) * MLA_SCALE, axis=-1).astype(v.dtype)
        return jnp.einsum('bhqk,bkhd->bqhd', p, v)

    o = lax.map(attend, (to_blocks(q_nope), to_blocks(q_rope)))
    return jnp.moveaxis(o, 0, 1).reshape(B, S, H * V_HEAD_DIM)

def pool_layer_mix(x, mem, w_in, group_w, scale, w_out, w_mem_kv):
    z = x @ w_in
    u_pool, q_mem = z[..., :TOKEN_WIDTH], z[..., TOKEN_WIDTH:]
    y_tok = pool_mixer(u_pool, group_w, scale)
    y_mem = memory_attention(q_mem, mem, w_mem_kv)
    return jnp.concatenate([y_tok, y_mem], axis=-1) @ w_out

def mla_layer_mix(x, mem, cos, sin, w_in, q_norm_g, kv_norm_g, w_uq, w_uk, w_uv, w_out, w_mem_kv):
    B, S, _ = x.shape
    z = x @ w_in
    o1 = Q_LORA_RANK
    o2 = o1 + KV_LORA_RANK
    o3 = o2 + QK_ROPE_DIM
    q_lat, kv_lat, k_rope, q_mem = z[..., :o1], z[..., o1:o2], z[..., o2:o3], z[..., o3:]
    q = (rms_norm(q_lat, q_norm_g) @ w_uq).reshape(B, S, MLA_HEADS, QK_NOPE_DIM + QK_ROPE_DIM)
    q_nope = q[..., :QK_NOPE_DIM]
    q_rope = apply_rotary(q[..., QK_NOPE_DIM:], cos[:, :, None, :], sin[:, :, None, :])
    c_kv = rms_norm(kv_lat, kv_norm_g)
    k_nope = (c_kv @ w_uk).reshape(B, S, MLA_HEADS, QK_NOPE_DIM)
    v = (c_kv @ w_uv).reshape(B, S, MLA_HEADS, V_HEAD_DIM)
    k_rope = apply_rotary(k_rope, cos, sin)
    y_tok = mla_attention(q_nope, q_rope, k_nope, k_rope, v)
    y_mem = memory_attention(q_mem, mem, w_mem_kv)
    return jnp.concatenate([y_tok, y_mem], axis=-1) @ w_out

def conv_ffn(x, w_up, conv_w, conv_b, w_down):
    h = x @ w_up
    c = h.shape[-1]
    h = lax.conv_general_dilated(
        h, conv_w[:, None, :], window_strides=(1,), padding=((CONV_WIDTH // 2, CONV_WIDTH // 2),),
        dimension_numbers=('NWC', 'WIO', 'NWC'), feature_group_count=c) + conv_b
    gate, val = h[..., :D_FF], h[..., D_FF:]
    return (jax.nn.silu(gate) * val) @ w_down

def setup_inputs(seed: int = 0) -> dict:
    key = jax.random.key(seed)
    ks = jax.random.split(key, 32)
    f32 = jnp.float32

    def nrm(k, shape, scale):
        return jax.random.normal(k, shape, f32) * scale

    x = nrm(ks[0], (BATCH, SEQ, D_MODEL), 1.0)
    mem = nrm(ks[1], (BATCH, N_MEM, D_MODEL), 1.0)
    offset = jax.random.randint(ks[2], (BATCH, 1), 0, 4096, dtype=jnp.int32)
    positions = offset + jnp.arange(SEQ, dtype=jnp.int32)[None, :]

    pool_w_in = nrm(ks[3], (N_POOL_LAYERS, D_MODEL, MIX_WIDTH), D_MODEL ** -0.5)
    pool_group_w = nrm(ks[4], (N_POOL_LAYERS, POOL_GROUPS, POOL_GROUP_DIM, POOL_GROUP_DIM), POOL_GROUP_DIM ** -0.5)
    pool_scale = 1.0 + nrm(ks[5], (N_POOL_LAYERS, TOKEN_WIDTH), 0.1)
    pool_w_out = nrm(ks[6], (N_POOL_LAYERS, MIX_WIDTH, D_MODEL), BETA * MIX_WIDTH ** -0.5)

    mla_w_in = nrm(ks[7], (N_MLA_LAYERS, D_MODEL, MLA_IN_WIDTH), D_MODEL ** -0.5)
    mla_q_norm_g = 1.0 + nrm(ks[8], (N_MLA_LAYERS, Q_LORA_RANK), 0.02)
    mla_kv_norm_g = 1.0 + nrm(ks[9], (N_MLA_LAYERS, KV_LORA_RANK), 0.02)
    mla_w_uq = nrm(ks[10], (N_MLA_LAYERS, Q_LORA_RANK, MLA_HEADS * (QK_NOPE_DIM + QK_ROPE_DIM)), Q_LORA_RANK ** -0.5)
    mla_w_uk = nrm(ks[11], (N_MLA_LAYERS, KV_LORA_RANK, MLA_HEADS * QK_NOPE_DIM), KV_LORA_RANK ** -0.5)
    mla_w_uv = nrm(ks[12], (N_MLA_LAYERS, KV_LORA_RANK, MLA_HEADS * V_HEAD_DIM), BETA * KV_LORA_RANK ** -0.5)
    mla_w_out = nrm(ks[13], (N_MLA_LAYERS, MLA_OUT_WIDTH, D_MODEL), BETA * MLA_OUT_WIDTH ** -0.5)

    mem_k = nrm(ks[14], (DEPTH, D_MODEL, MEM_WIDTH), D_MODEL ** -0.5)
    mem_v = nrm(ks[15], (DEPTH, D_MODEL, MEM_WIDTH), BETA * D_MODEL ** -0.5)
    mem_w_kv = jnp.concatenate([mem_k, mem_v], axis=-1)

    ln1_g = 1.0 + nrm(ks[16], (DEPTH, D_MODEL), 0.02)
    ln1_b = nrm(ks[17], (DEPTH, D_MODEL), 0.02)
    ln2_g = 1.0 + nrm(ks[18], (DEPTH, D_MODEL), 0.02)
    ln2_b = nrm(ks[19], (DEPTH, D_MODEL), 0.02)

    ffn_w_up = nrm(ks[20], (DEPTH, D_MODEL, 2 * D_FF), BETA * D_MODEL ** -0.5)
    ffn_conv_w = nrm(ks[21], (DEPTH, CONV_WIDTH, 2 * D_FF), CONV_WIDTH ** -0.5)
    ffn_conv_b = nrm(ks[22], (DEPTH, 2 * D_FF), 0.02)
    ffn_w_down = nrm(ks[23], (DEPTH, D_FF, D_MODEL), BETA * D_FF ** -0.5)

    return {
        "x": x, "mem": mem, "positions": positions,
        "pool_w_in": pool_w_in, "pool_group_w": pool_group_w, "pool_scale": pool_scale, "pool_w_out": pool_w_out,
        "mla_w_in": mla_w_in, "mla_q_norm_g": mla_q_norm_g, "mla_kv_norm_g": mla_kv_norm_g,
        "mla_w_uq": mla_w_uq, "mla_w_uk": mla_w_uk, "mla_w_uv": mla_w_uv, "mla_w_out": mla_w_out,
        "mem_w_kv": mem_w_kv,
        "ln1_g": ln1_g, "ln1_b": ln1_b, "ln2_g": ln2_g, "ln2_b": ln2_b,
        "ffn_w_up": ffn_w_up, "ffn_conv_w": ffn_conv_w, "ffn_conv_b": ffn_conv_b, "ffn_w_down": ffn_w_down,
    }

def reference(x, mem, positions,
              pool_w_in, pool_group_w, pool_scale, pool_w_out,
              mla_w_in, mla_q_norm_g, mla_kv_norm_g, mla_w_uq, mla_w_uk, mla_w_uv, mla_w_out,
              mem_w_kv,
              ln1_g, ln1_b, ln2_g, ln2_b,
              ffn_w_up, ffn_conv_w, ffn_conv_b, ffn_w_down):
    cos, sin = rotary_tables(positions)
    for i in range(DEPTH):
        j = i // 2
        if i % 2 == 0:
            h = pool_layer_mix(x, mem, pool_w_in[j], pool_group_w[j], pool_scale[j], pool_w_out[j], mem_w_kv[i])
        else:
            h = mla_layer_mix(x, mem, cos, sin, mla_w_in[j], mla_q_norm_g[j], mla_kv_norm_g[j],
                              mla_w_uq[j], mla_w_uk[j], mla_w_uv[j], mla_w_out[j], mem_w_kv[i])
        x = layer_norm(ALPHA * x + h, ln1_g[i], ln1_b[i])
        f = conv_ffn(x, ffn_w_up[i], ffn_conv_w[i], ffn_conv_b[i], ffn_w_down[i])
        x = layer_norm(ALPHA * x + f, ln2_g[i], ln2_b[i])
    return x


_drawn_inputs = setup_inputs


def setup_inputs(seed=0):
    import zlib

    import numpy as np

    out = dict(_drawn_inputs(seed))
    spreads = {}
    factors = {'mem': 4.546,
     'mla_w_in': 3.002,
     'mla_q_norm_g': 8.0,
     'mla_kv_norm_g': 8.0,
     'mla_w_uq': 4.097,
     'mla_w_uk': 4.547,
     'mla_w_uv': 3.342,
     'mla_w_out': 2.928,
     'mem_w_kv': 3.81,
     'ffn_conv_b': 8.0}
    for name, (base, spread) in spreads.items():
        noise = np.random.default_rng([zlib.crc32(name.encode()), seed]).standard_normal(out[name].shape)
        drawn = base * np.exp(spread * noise) if base else spread * noise
        out[name] = __import__('jax').numpy.asarray(drawn.astype(out[name].dtype))
    for name, factor in factors.items():
        out[name] = (out[name] * factor).astype(out[name].dtype)
    return out
```

```python
from contextlib import ExitStack

import concourse.bass as bass
from concourse import mybir

P = 128
F32 = mybir.dt.float32
F32R = mybir.dt.float32r
I32 = mybir.dt.int32
ALU = mybir.AluOpType
ACT = mybir.ActivationFunctionType
AX_X = mybir.AxisListType.X

RING = 4
UNIT = 1024
BANK = 512
HEAD = 128
ROPE = 64
WINDOWS = (2, 4, 8, 16)
PAD = 8
MAGIC = 1.5 * 2.0 ** 23
TWO_PI_PARTS = (6.28125, 1.9350051879882812e-03, 3.0199159819e-07)


class Steps:

    def __init__(self, engine, sem):
        self.engine, self.sem, self.n, self.turn = engine, sem, 0, 0

    def done(self, instruction):
        instruction.then_inc(self.sem, 1)
        self.n += 1
        return self.n

    def wait(self, n=None):
        self.engine.wait_ge(self.sem, (self.n if n is None else n) + self.turn)

    def loop(self, i, per_turn):
        self.first, self.per_turn = self.n, per_turn
        self.turn = i * per_turn

    def end_loop(self, turns):
        assert self.n - self.first == self.per_turn, (self.n - self.first, self.per_turn)
        self.turn = 0
        self.n = self.first + self.per_turn * turns


def encoder_trunk(nc, x, mem, positions, pool_w_in, pool_group_w, pool_scale, pool_w_out, mla_w_in,
                  mla_q_norm_g, mla_kv_norm_g, mla_w_uq, mla_w_uk, mla_w_uv, mla_w_out, mem_w_kv,
                  ln1_g, ln1_b, ln2_g, ln2_b, ffn_w_up, ffn_conv_w, ffn_conv_b, ffn_w_down, inv_freq, out):
    _, S, D = x.shape
    DEPTH = ffn_w_up.shape[0]
    FF = ffn_w_down.shape[1]
    KC = D // P
    FC = FF // P
    TB = S // P
    MEM_HEADS = mem_w_kv.shape[2] // (2 * HEAD)
    MLA_HEADS = mla_w_uk.shape[2] // HEAD
    QL = mla_w_uq.shape[1]
    LC = QL // P
    POOL_CH = D - MEM_HEADS * HEAD
    POOL_CHUNKS = POOL_CH // P
    GC = POOL_CHUNKS // len(WINDOWS)
    ALPHA = (2 * DEPTH) ** 0.25
    MEM_SCALE = HEAD ** -0.5
    MLA_SCALE = (HEAD + ROPE) ** -0.5
    assert (S, D, DEPTH, FC, MEM_HEADS, MLA_HEADS, LC) == (256, 2048, 2, 44, 4, 12, 4)

    UG = KC // 2
    DG = FC // 2
    FG = FC // 4
    U_MEM = 0
    U_IN0 = U_MEM + 4 * UG
    U_GW = U_IN0 + 4 * UG
    U_OUT = [U_GW + 6, 0]
    U_UP = [U_OUT[0] + 4 * UG, 0]
    U_DOWN = [U_UP[0] + 2 * FG * UG, 0]
    U_IN1 = U_DOWN[0] + 4 * DG
    U_UQ = U_IN1 + 3 * UG + 2
    U_QR = U_UQ + 6
    U_UK = U_QR + 3
    U_UV = U_UK + 6
    U_OUT[1] = U_UV + 6
    U_UP[1] = U_OUT[1] + 4 * UG
    U_DOWN[1] = U_UP[1] + 2 * FG * UG
    U_END = U_DOWN[1] + 4 * DG
    G_IN0, G_GW, G_OUT0 = 4, 8, 11
    G_UP0 = G_OUT0 + 4
    G_DOWN0 = G_UP0 + 2 * FG
    G_IN1 = G_DOWN0 + 4
    G_UQ = G_IN1 + 4
    G_QR = G_UQ + 3
    G_UK = G_QR + 2
    G_UV = G_UK + 3
    G_OUT1 = G_UV + 3
    G_OUT = [G_OUT0, G_OUT1]
    G_UP = [G_UP0, G_OUT1 + 4]
    G_DOWN = [G_DOWN0, G_OUT1 + 4 + 2 * FG]
    H_MEM, H_IN0 = 0, 2
    H_GW = H_IN0 + 4
    H_OUT = [H_GW + 3, 0]
    H_UP = [H_OUT[0] + 4, 0]
    H_DOWN = [H_UP[0] + 2 * FG, 0]
    H_IN1 = H_DOWN[0] + 4
    H_UQ = H_IN1 + 4
    H_QR = H_UQ + 3
    H_UK = H_QR + 2
    H_OUT[1] = H_UK + 3
    H_UP[1] = H_OUT[1] + 4
    H_DOWN[1] = H_UP[1] + 2 * FG

    kv_scratch = nc.dram_tensor("kv_scratch", (P, 8 * S), F32, kind="Internal").ap()

    with ExitStack() as ctx:
        def sb(name, shape, dt=F32):
            return ctx.enter_context(nc.sbuf_tensor(name, shape, dt))

        def sem(name):
            return ctx.enter_context(nc.semaphore(name))

        raw = sb("raw", [P, RING, UNIT])
        w_hi = sb("w_hi", [P, RING, UNIT], F32R)
        w_lo = sb("w_lo", [P, RING, UNIT], F32R)
        res = sb("res", [P, KC, S])
        KB = 1024

        base0 = nc.sbuf_base
        sb("xy_region", [P, KC * 2 * S])
        sb("act_region", [P, FC * 2 * S])
        sb("tmp_region", [P, 3088])
        XY = base0
        AR = XY + KC * 2 * S * 4
        TR = AR + FC * 2 * S * 4
        assert nc.sbuf_base == TR + 3088 * 4, (nc.sbuf_base, TR)

        def at(name, shape, offset, dt=F32):
            return nc.alloc_sbuf_tensor_at(name, shape, dt, offset=offset)

        xy = at("xy", [P, KC, 2 * S], XY, F32R)
        act_hl = at("act_hl", [P, FC, 2 * S], AR, F32R)
        first_half = [at(f"first_half{k}", [P, 4, S], o) for k, o in ((0, AR + 32 * KB), (1, XY), (2, AR), (3, XY))]
        squares = [at(f"squares{k}", [P, 4, S], o + 4 * KB) for k, o in ((0, AR + 32 * KB), (1, XY), (2, AR), (3, XY))]
        sum_d = [at(f"sum_d{k}", [P, 4, S], o + 8 * KB) for k, o in ((0, AR + 32 * KB), (1, XY), (2, AR), (3, XY))]
        sum_dd = [at(f"sum_dd{k}", [P, 4, S], o + 12 * KB) for k, o in ((0, AR + 32 * KB), (1, XY), (2, AR), (3, XY))]
        mem_hl = at("mem_hl", [P, KC, 2 * S], AR, F32R)
        mem_rows = at("mem_rows", [P, TB, D], AR + 32 * KB)
        kv_mem = [at(f"kv_mem{l}", [P, 2, 4 * S], o) for l, o in ((0, AR + 48 * KB), (1, AR + 56 * KB))]
        x_rows = at("x_rows", [P, TB, D], AR + 64 * KB)
        conv_rows = at("conv_rows", [FC * 2, DEPTH, 4, P], AR + 80 * KB)
        ln_rows = at("ln_rows", [P, P], AR + 84 * KB)
        misc_rows = at("misc_rows", [POOL_CHUNKS + 2 * LC, P], AR + 84 * KB + 512)
        pos_i = at("pos_i", [P, S], AR + 85 * KB, I32)
        angle = at("angle", [P, S], AR + 86 * KB)
        turns = at("turns", [P, S], AR + 87 * KB)
        q_mem = [at("q_mem0", [P, 4, S], AR), at("q_mem1", [P, 4, S], AR + 74 * KB)]
        inv_count = at("inv_count", [P, len(WINDOWS), S], AR + 4 * KB)
        u_pad = at("u_pad", [P, POOL_CHUNKS, S + 2 * PAD], AR + 8 * KB)
        win = [at(f"win{k}", [P, GC, S + 2 * PAD], AR + 8 * KB + 13056 + 3264 * k) for k in range(2)]
        y_pool = at("y_pool", [P, 4, S], AR + 28 * KB)
        pooled = at("pooled", [P, POOL_CHUNKS, 2 * S], AR + 64 * KB, F32R)
        qn_hl = at("qn_hl", [P, LC, 2 * S], AR, F32R)
        kvn_hl = at("kvn_hl", [P, LC, 2 * S], AR + 8 * KB, F32R)
        latent = at("latent", [P, LC, S], AR + 16 * KB)
        latent_sq = at("latent_sq", [P, LC, S], AR + 20 * KB)
        k_rope = at("k_rope", [P, 1, S], AR + 24 * KB)
        k_swap = at("k_swap", [P, 1, S], AR + 25 * KB)
        q_rope = at("q_rope", [P, MLA_HEADS // 2, S], AR + 26 * KB)
        q_swap = at("q_swap", [P, MLA_HEADS // 2, S], AR + 32 * KB)
        q_nope = at("q_nope", [P, MLA_HEADS, S], AR + 38 * KB)
        k_nope = at("k_nope", [P, MLA_HEADS, S], AR + 50 * KB)
        v_mla = at("v_mla", [P, TB, MLA_HEADS * HEAD], AR + 62 * KB)
        kv_back = at("kv_back", [P, 2, 4 * S], AR + 78 * KB)
        out_rows = at("out_rows", [P, TB, D], AR)
        h_pad = at("h_pad", [P, 4, S + 2], TR)
        gate = at("gate", [P, 4, S], TR + 4128)
        val = at("val", [P, 4, S], TR + 4128 + 4 * KB)
        probs = [at(f"probs{k}", [P, TB, S], TR + 2 * KB * k) for k in range(3)]
        probs_t = [at(f"probs_t{k}", [P, TB, S], TR + 6 * KB + 2 * KB * k) for k in range(2)]
        soft = at("soft", [P, 4, 2 * 16], TR + 10 * KB)
        shift, mean, var, std, rstd, mean_rstd, fold_a = [at(n, [P, S], TR + KB * k) for k, n in enumerate(
            ["shift", "mean", "var", "std", "rstd", "mean_rstd", "fold_a"])]
        fold_b = at("fold_b", [P, 2, S], TR + 7 * KB)
        conv_col = sb("conv_col", [P, DEPTH, 4, 2 * FC])
        ln_col = sb("ln_col", [P, 4, DEPTH, KC])
        misc_col = sb("misc_col", [P, POOL_CHUNKS + 2 * LC])
        ident = sb("ident", [P, P])
        ones = sb("ones", [P, P])
        cos_t = sb("cos_t", [P, 1, S])
        sin_t = sb("sin_t", [P, 1, S])
        sign = sb("sign", [P, 1])
        freq = sb("freq", [P, 1])
        halfpi = sb("halfpi", [P, 1])

        ps = ctx.enter_context(nc.psum_tensor("ps", [P, 8, BANK], F32))

        raw_landed = [sem(f"raw_landed{s}") for s in range(RING)]
        hi_ready = sem("hi_ready")
        lo_ready = sem("lo_ready")
        units_done = sem("units_done")
        halves = sem("halves")
        evacuated = sem("evacuated")
        mem_landed = [sem(f"mem_landed{q}") for q in range(4)]
        x_landed = sem("x_landed")
        params_landed = sem("params_landed")
        pos_landed = sem("pos_landed")
        consts_ready = sem("consts_ready")
        mem_turned = sem("mem_turned")
        mem_hi = sem("mem_hi")
        mem_ready = sem("mem_ready")
        x_turned = sem("x_turned")
        x_hi = sem("x_hi")
        x_ready = sem("x_ready")
        params_turned = sem("params_turned")
        params_ready = sem("params_ready")
        trig = sem("trig")
        trig_done = sem("trig_done")
        kv_saved = sem("kv_saved")
        kv_loaded = sem("kv_loaded")
        pads_ready = sem("pads_ready")
        windowed = sem("windowed")
        pool_diff = sem("pool_diff")
        pool_hi = sem("pool_hi")
        pooled_ready = sem("pooled_ready")
        pool_y_hi = sem("pool_y_hi")
        pool_y_ready = sem("pool_y_ready")
        scores_ready = sem("scores_ready")
        neg_max = sem("neg_max")
        exps = sem("exps")
        probs_ready = sem("probs_ready")
        probs_turned = sem("probs_turned")
        probs_t_ready = sem("probs_t_ready")
        heads_out = sem("heads_out")
        y_hi = sem("y_hi")
        y_ready = sem("y_ready")
        col_sum = sem("col_sum")
        stat_done = sem("stat_done")
        shift_ready = sem("shift_ready")
        shifted = sem("shifted")
        squared = sem("squared")
        sums_ready = sem("sums_ready")
        mean_ready = sem("mean_ready")
        var_ready = sem("var_ready")
        std_ready = sem("std_ready")
        normed = sem("normed")
        affine = sem("affine")
        conv_gate = sem("conv_gate")
        silu_done = sem("silu_done")
        product = sem("product")
        act_hi = sem("act_hi")
        act_ready = sem("act_ready")
        pad_zero = sem("pad_zero")
        sq_used = sem("sq_used")
        lat_sq = sem("lat_sq")
        lat_sum = sem("lat_sum")
        lat_stat = sem("lat_stat")
        lat_var = sem("lat_var")
        lat_std = sem("lat_std")
        lat_normed = sem("lat_normed")
        lat_hi = sem("lat_hi")
        latent_ready = sem("latent_ready")
        swapped = sem("swapped")
        rope_ready = sem("rope_ready")
        final_turned = sem("final_turned")
        out_copied = sem("out_copied")
        out_saved = sem("out_saved")
        act_step = sem("act_step")
        dve_step = sem("dve_step")
        pool_step = sem("pool_step")

        block = ctx.enter_context(nc.Block())

        def bank_set(g):
            return (g % 2) * 4

        def first_cols(g, nb=4):
            return ps[:, bank_set(g):bank_set(g) + nb, 0:S]

        def second_cols(g, nb=4):
            return ps[:, bank_set(g):bank_set(g) + nb, S:2 * S]

        def wide(t, n):
            return t.to_broadcast([P, n, S])

        def n_loads(u):
            if U_QR <= u < U_QR + 3:
                return LC
            return 2 if U_GW <= u < U_GW + 6 or U_IN1 + 2 * UG <= u < U_IN1 + 2 * UG + 2 or U_UQ <= u < U_QR else 1

        def landed(u):
            return 16 * sum(n_loads(v) for v in range(u % RING, u + 1, RING))

        @block.sync
        def _(sp):
            def load(u, src, turn=0):
                s = u % RING
                if u >= RING:
                    sp.wait_ge(lo_ready, u - RING + 1 + turn)
                sp.dma_start(raw[:, s, :].rearrange("p (a b) -> p a b", a=2), src).then_inc(raw_landed[s], 16)

            def load_parts(u, parts):
                s = u % RING
                assert len(parts) == n_loads(u)
                sp.wait_ge(lo_ready, u - RING + 1)
                for cols, n, src in parts:
                    if cols is None:
                        dst = raw[:, s, :].rearrange("p (c w) -> p c w", c=8)[:, :, n * ROPE:(n + 1) * ROPE]
                    else:
                        dst = raw[:, s, cols].rearrange("p (a b) -> p a b", a=n)
                    sp.dma_start(dst, src).then_inc(raw_landed[s], 16)

            def rows(w):
                return w.rearrange("(c p) n -> p c n", p=P)

            def load_groups(u0, w, cols, n_units):
                for g, c in enumerate(cols):
                    for j in range(n_units):
                        load(u0 + g * n_units + j, rows(w)[:, 2 * j:2 * j + 2, c:c + 512])

            def load_group_loop(u0, w, n_groups, n_units, stride=512):
                with sp.Fori(0, n_groups // 2) as i:
                    for g in range(2):
                        for j in range(n_units):
                            load(u0 + g * n_units + j,
                                 rows(w)[:, 2 * j:2 * j + 2, bass.ds(i * (2 * stride) + g * stride, 512)],
                                 i * (2 * n_units))

            for q in range(4):
                sp.dma_start(mem_rows[:, :, q * 512:(q + 1) * 512],
                             mem[0].rearrange("(t p) d -> p t d", p=P)[:, :, q * 512:(q + 1) * 512]) \
                    .then_inc(mem_landed[q], 16)
            load_groups(0, mem_w_kv[0], (0,), UG // 2)
            sp.dma_start(pos_i[:], positions.to_broadcast([P, S])).then_inc(pos_landed, 16)
            sp.dma_start(freq[:], inv_freq).then_inc(pos_landed, 16)
            sp.dma_start(x_rows[:], x[0].rearrange("(t p) d -> p t d", p=P)).then_inc(x_landed, 16)
            for l in range(DEPTH):
                for t in range(3):
                    sp.dma_start(conv_rows[:, l, t, :], ffn_conv_w[l, t].rearrange("(c p) -> c p", p=P)) \
                        .then_inc(params_landed, 16)
                sp.dma_start(conv_rows[:, l, 3, :], ffn_conv_b[l].rearrange("(c p) -> c p", p=P)) \
                    .then_inc(params_landed, 16)
            for k, w in enumerate((ln1_g, ln1_b, ln2_g, ln2_b)):
                sp.dma_start(ln_rows[32 * k:32 * k + 32, :], w.rearrange("l (c p) -> (l c) p", p=P)) \
                    .then_inc(params_landed, 16)
            for r0, w in ((0, pool_scale), (POOL_CHUNKS, mla_q_norm_g), (POOL_CHUNKS + LC, mla_kv_norm_g)):
                sp.dma_start(misc_rows[r0:r0 + w.shape[1] // P, :], w[0].rearrange("(c p) -> c p", p=P)) \
                    .then_inc(params_landed, 16)

            for j in range(UG // 2, UG):
                load(j, rows(mem_w_kv[0])[:, 2 * j:2 * j + 2, 0:512])
            load_groups(UG, mem_w_kv[0], (512,), UG)
            load_groups(2 * UG, mem_w_kv[1], (0, 512), UG)
            load_groups(U_IN0, pool_w_in[0], (POOL_CH,), UG)
            sp.wait_ge(evacuated, 4)
            sp.dma_start(kv_scratch, kv_mem[1][:].rearrange("p a b -> p (a b)")).then_inc(kv_saved, 16)
            load_groups(U_IN0 + UG, pool_w_in[0], (0, 512, 1024), UG)
            for r in range(6):
                blocks = [divmod(2 * r + h, GC) for h in range(2)]
                load_parts(U_GW + r, [(slice(h * GC * P, (h + 1) * GC * P), GC,
                                       rows(pool_group_w[0, w])[:, :, b * P:(b + 1) * P])
                                      for h, (w, b) in enumerate(blocks)])
            load_group_loop(U_OUT[0], pool_w_out[0], 4, UG)

            def load_ffn(l):
                with sp.Fori(0, FG) as i:
                    for h in range(2):
                        for j in range(UG):
                            load(U_UP[l] + h * UG + j,
                                 rows(ffn_w_up[l])[:, 2 * j:2 * j + 2, bass.ds(i * 512 + h * FF, 512)], i * (2 * UG))
                load_group_loop(U_DOWN[l], ffn_w_down[l], 4, DG)

            load_ffn(0)
            o_rope = 2 * QL
            load_groups(U_IN1, mla_w_in[0], (0,), UG)
            sp.wait_ge(units_done, U_IN1)
            sp.wait_ge(kv_saved, 16)
            sp.dma_start(kv_back[:].rearrange("p a b -> p (a b)"), kv_scratch).then_inc(kv_loaded, 16)
            load_groups(U_IN1 + UG, mla_w_in[0], (QL,), UG)
            for r in range(2):
                w_rope = rows(mla_w_in[0])[:, 8 * r:8 * r + 8, o_rope:o_rope + ROPE]
                load_parts(U_IN1 + 2 * UG + r, [(None, h, w_rope) for h in range(2)])
            load_groups(U_IN1 + 2 * UG + 2, mla_w_in[0], (o_rope + ROPE,), UG)
            per_head = mla_w_uq[0].rearrange("(c p) (h w) -> p c h w", p=P, w=HEAD + ROPE)
            for g in range(3):
                for j in range(2):
                    load_parts(U_UQ + 2 * g + j, [(slice(c * 512, (c + 1) * 512), 4,
                                                   per_head[:, 2 * j + c, 4 * g:4 * g + 4, 0:HEAD]) for c in range(2)])
            for r in range(3):
                load_parts(U_QR + r, [(slice(c * 256, (c + 1) * 256), 4,
                                       per_head[:, c, 4 * r:4 * r + 4, HEAD:HEAD + ROPE]) for c in range(LC)])
            load_groups(U_UK, mla_w_uk[0], (0, 512, 1024), 2)
            load_groups(U_UV, mla_w_uv[0], (0, 512, 1024), 2)
            load_group_loop(U_OUT[1], mla_w_out[0], 4, UG)
            load_ffn(1)
            for q in range(4):
                sp.wait_ge(out_copied, 2 * (q + 1))
                sp.dma_start(out[0].rearrange("(t p) d -> p t d", p=P)[:, :, q * 512:(q + 1) * 512],
                             out_rows[:, :, q * 512:(q + 1) * 512]).then_inc(out_saved, 16)
            sp.wait_ge(out_saved, 16 * 4)

        def walk(eng, split):
            state = [0]

            def to(n):
                n = min(n, U_END)
                while state[0] < n:
                    u = state[0]
                    turns = (n - u) // RING
                    calm = all(landed(v + RING * (turns - 1)) - landed(v) == 16 * (turns - 1) for v in range(u, u + RING)) \
                        if turns > 1 else False
                    if turns > 1 and calm and u >= RING:
                        with eng.Fori(0, turns) as i:
                            for j in range(RING):
                                split(u + j, i * RING, i * 16)
                        state[0] += RING * turns
                    else:
                        split(u, 0, 0)
                        state[0] += 1

            def skip(n):
                state[0] = n

            return to, skip

        LN_AT = [(0, 0, U_OUT[0], UG, G_OUT[0], H_OUT[0]), (0, 1, U_DOWN[0], DG, G_DOWN[0], H_DOWN[0]),
                 (1, 0, U_OUT[1], UG, G_OUT[1], H_OUT[1]), (1, 1, U_DOWN[1], DG, G_DOWN[1], H_DOWN[1])]
        HEADS = [[("mem", h) for h in range(MEM_HEADS)],
                 [("mla", h) for h in range(MLA_HEADS)] + [("mem", h) for h in range(MEM_HEADS)]]
        HEAD0 = [0, MEM_HEADS]

        def y_chunk(l, n):
            return POOL_CHUNKS + n if l == 0 else n

        @block.scalar
        def _(act):
            step = Steps(act, act_step)

            def split(u, turn, turn16):
                s = u % RING
                act.wait_ge(raw_landed[s], landed(u) + turn16)
                if u >= RING:
                    act.wait_ge(units_done, u - RING + 1 + turn)
                act.activation(w_hi[:, s, :], raw[:, s, :], ACT.Copy).then_inc(hi_ready, 1)

            split_to, skip_to = walk(act, split)

            def half_out(e, g, dst, nb=4):
                split_to(e + RING)
                act.wait_ge(units_done, e)
                act.activation(dst, first_cols(g, nb), ACT.Copy).then_inc(halves, 1)

            for j in range(KC // 2):
                act.wait_ge(mem_turned, j + 1)
                act.activation(mem_hl[:, 2 * j:2 * j + 2, 0:S], ps[:, j, :].rearrange("p (a b) -> p a b", a=2),
                               ACT.Copy).then_inc(mem_hi, 1)
            split_to(RING)
            act.wait_ge(trig, 1)
            act.activation(sin_t[:, 0, :], angle[:], ACT.Sin).then_inc(trig_done, 1)
            act.wait_ge(trig, 2)
            act.activation(cos_t[:, 0, :], turns[:], ACT.Sin).then_inc(trig_done, 1)
            half_out(UG, 0, kv_mem[0][:, 0, :].rearrange("p (a b) -> p a b", a=4))
            half_out(3 * UG, 2, kv_mem[1][:, 0, :].rearrange("p (a b) -> p a b", a=4))
            split_to(U_IN0 + RING)
            for j in range(KC // 2):
                act.wait_ge(x_turned, j + 1)
                bank = ps[:, j % 4, :].rearrange("p (a b) -> p a b", a=2)
                act.activation(res[:, 2 * j:2 * j + 2, :], bank, ACT.Copy)
                act.activation(xy[:, 2 * j:2 * j + 2, 0:S], bank, ACT.Copy).then_inc(x_hi, 1)

            def attention(l):
                heads, h0 = HEADS[l], HEAD0[l]
                n = len(heads)
                for s in range(n + 3):
                    if s < n:
                        scale = MEM_SCALE if heads[s][0] == "mem" else MLA_SCALE
                        act.wait_ge(neg_max, h0 + s + 1)
                        if s >= 3:
                            act.wait_ge(probs_turned, h0 + s - 2)
                        for t in range(TB):
                            ins = act.activation(probs[s % 3][:, t, :], ps[:, s % 3, t * S:(t + 1) * S], ACT.Exp,
                                                 bias=soft[:, 1, 2 * s + t:2 * s + t + 1], scale=scale,
                                                 accum_out=soft[:, 2, 2 * s + t:2 * s + t + 1])
                        ins.then_inc(exps, 1)
                    if 2 <= s < n + 2:
                        h = s - 2
                        act.wait_ge(probs_turned, h0 + h + 1)
                        if h >= 2:
                            act.wait_ge(heads_out, h0 + h - 1)
                        act.activation(probs_t[h % 2][:].rearrange("p a b -> p (a b)"), ps[:, 3 + h % 3, :],
                                       ACT.Copy).then_inc(probs_t_ready, 1)
                    if s >= 3:
                        h = s - 3
                        act.wait_ge(heads_out, h0 + h + 1)
                        act.activation(xy[:, y_chunk(l, h), 0:S], ps[:, 6 + h % 2, 0:S], ACT.Copy).then_inc(y_hi, 1)

            def layer_norm(k):
                l, which, u0, n_units, g0, _ = LN_AT[k]
                for g in range(4):
                    if g:
                        act.wait_ge(evacuated, g0 + g)
                    half_out(u0 + (g + 1) * n_units, g0 + g, first_half[k][:])
                    if g == 1:
                        act.wait_ge(stat_done, 2 * k + 1)
                        act.activation(shift[:], ps[:, bank_set(g0), 0:S], ACT.Copy, scale=1.0 / 512) \
                            .then_inc(shift_ready, 1)
                    if g >= 1:
                        for gg in ([0, 1] if g == 1 else [g]):
                            act.wait_ge(shifted, 4 * k + gg + 1)
                            dst = sum_dd[k] if gg == 0 else squares[k]
                            if gg >= 2:
                                act.wait_ge(sq_used, 3 * k + gg - 1)
                            act.activation(dst[:], res[:, 4 * gg:4 * gg + 4, :], ACT.Square).then_inc(squared, 1)
                act.wait_ge(stat_done, 2 * k + 2)
                act.activation(mean[:], ps[:, bank_set(g0), 0:S], ACT.Copy, scale=1.0 / D).then_inc(mean_ready, 1)
                act.wait_ge(var_ready, k + 1)
                act.activation(std[:], var[:], ACT.Sqrt).then_inc(std_ready, 1)
                for j in range(KC // 2):
                    act.wait_ge(normed, 8 * k + j + 1)
                    for c in (2 * j, 2 * j + 1):
                        ins = act.activation(res[:, c, :], res[:, c, :], ACT.Identity,
                                             scale=ln_col[:, 2 * which, l, c:c + 1],
                                             bias=ln_col[:, 2 * which + 1, l, c:c + 1])
                        if k < 3:
                            step.done(ins)
                    if k < 3:
                        step.wait()
                        act.activation(xy[:, 2 * j:2 * j + 2, 0:S], res[:, 2 * j:2 * j + 2, :], ACT.Copy) \
                            .then_inc(x_hi, 1)
                    else:
                        ins.then_inc(affine, 1)

            def ffn(l):
                u0 = U_UP[l]
                act.wait_ge(pad_zero, l + 1)
                with act.Fori(0, FG) as i:
                    def ahead(a, b):
                        for j in range(a, b):
                            split(u0 + RING + j, i * (2 * UG), i * (2 * UG // RING * 16))

                    ahead(0, UG)
                    act.wait_ge(units_done, i * (2 * UG) + (u0 + UG))
                    act.activation(h_pad[:, :, 1:S + 1], first_cols(G_UP[l]), ACT.Copy).then_inc(halves, 1)
                    ahead(UG, UG + RING)
                    act.wait_ge(conv_gate, i + (FG * l + 1))
                    act.activation(gate[:], gate[:], ACT.Silu).then_inc(silu_done, 1)
                    ahead(UG + RING, 2 * UG)
                    act.wait_ge(units_done, i * (2 * UG) + (u0 + 2 * UG))
                    act.activation(h_pad[:, :, 1:S + 1], first_cols(G_UP[l] + 1), ACT.Copy).then_inc(halves, 1)
                    act.wait_ge(product, i + (FG * l + 1))
                    act.activation(act_hl[:, bass.ds(i * 4, 4), 0:S], val[:], ACT.Copy).then_inc(act_hi, 1)
                skip_to(u0 + RING + 2 * FG * UG)

            half_out(U_IN0 + UG, G_IN0, q_mem[0][:])
            act.wait_ge(pads_ready, 1)
            for g in range(3):
                half_out(U_IN0 + (2 + g) * UG, G_IN0 + 1 + g, u_pad[:, 4 * g:4 * g + 4, PAD:PAD + S])
            attention(0)
            for k in range(len(WINDOWS)):
                act.wait_ge(pool_diff, k + 1)
                act.activation(pooled[:, GC * k:GC * k + GC, 0:S], u_pad[:, GC * k:GC * k + GC, PAD:PAD + S],
                               ACT.Copy).then_inc(pool_hi, 1)
            for g in range(3):
                if g:
                    act.wait_ge(pool_y_ready, g)
                half_out(U_GW + 2 * (g + 1), G_GW + g, y_pool[:])
                act.wait_ge(evacuated, G_GW + g + 1)
                for b in range(4):
                    step.done(act.activation(y_pool[:, b, :], y_pool[:, b, :], ACT.Copy,
                                             scale=misc_col[:, 4 * g + b:4 * g + b + 1]))
                step.wait()
                act.activation(xy[:, 4 * g:4 * g + 4, 0:S], y_pool[:], ACT.Copy).then_inc(pool_y_hi, 1)
            layer_norm(0)
            ffn(0)
            layer_norm(1)

            def latent_norm(n, e, g, gains):
                if n:
                    act.wait_ge(latent_ready, n)
                half_out(e, g, latent[:])
                act.wait_ge(evacuated, g + 1)
                act.activation(latent_sq[:], latent[:], ACT.Square).then_inc(lat_sq, 1)
                act.wait_ge(lat_var, n + 1)
                act.activation(std[:], var[:], ACT.Sqrt).then_inc(lat_std, 1)
                act.wait_ge(lat_normed, n + 1)
                for c in range(LC):
                    step.done(act.activation(latent[:, c, :], latent[:, c, :], ACT.Copy,
                                             scale=misc_col[:, gains + c:gains + c + 1]))
                step.wait()
                act.activation((qn_hl, kvn_hl)[n][:, :, 0:S], latent[:], ACT.Copy).then_inc(lat_hi, 1)

            def swap_halves(g, src, dst):
                act.wait_ge(evacuated, g + 1)
                for q in range(4):
                    r, w = 32 * (q ^ 1), 32 * q
                    ins = act.activation(dst[w:w + 32, :, :], src[r:r + 32, :, :], ACT.Copy)
                ins.then_inc(swapped, 1)

            e = U_IN1
            latent_norm(0, e + UG, G_IN1, POOL_CHUNKS)
            latent_norm(1, e + 2 * UG, G_IN1 + 1, POOL_CHUNKS + LC)
            half_out(e + 2 * UG + 2, G_IN1 + 2, k_rope[:], 1)
            swap_halves(G_IN1 + 2, k_rope, k_swap)
            half_out(U_UQ, G_IN1 + 3, q_mem[1][:])
            for g in range(3):
                half_out(U_UQ + 2 * (g + 1), G_UQ + g, q_nope[:, 4 * g:4 * g + 4, :])
            half_out(U_QR + 2, G_QR, q_rope[:, 0:4, :])
            half_out(U_QR + 3, G_QR + 1, q_rope[:, 4:6, :], 2)
            swap_halves(G_QR + 1, q_rope, q_swap)
            for g in range(3):
                half_out(U_UK + 2 * (g + 1), G_UK + g, k_nope[:, 4 * g:4 * g + 4, :])
            split_to(U_OUT[1] + RING)
            attention(1)
            layer_norm(2)
            ffn(1)
            layer_norm(3)
            for j in range(KC // 2):
                act.wait_ge(final_turned, j + 1)
                act.activation(out_rows[:, :, 2 * j * P:(2 * j + 2) * P],
                               ps[:, j, :].rearrange("p (t b) -> p t b", t=2), ACT.Copy).then_inc(out_copied, 1)

        @block.vector
        def _(dve):
            step = Steps(dve, dve_step)

            def split(u, turn, turn16):
                s = u % RING
                dve.wait_ge(hi_ready, u + 1 + turn)
                dve.tensor_tensor(w_lo[:, s, :], raw[:, s, :], w_hi[:, s, :], ALU.subtract).then_inc(lo_ready, 1)

            split_to, skip_to = walk(dve, split)

            def add_half(e, g, h, dst, nb=4):
                split_to(e + RING)
                dve.wait_ge(halves, h + 1)
                dve.tensor_tensor(dst, dst, second_cols(g, nb), ALU.add).then_inc(evacuated, 1)

            def rows_out(e, g, dst):
                split_to(e + RING)
                dve.wait_ge(units_done, e)
                b = bank_set(g)
                dve.tensor_copy(dst, ps[:, b:b + TB, :]).then_inc(evacuated, 1)

            for j in range(KC // 2):
                dve.wait_ge(mem_hi, j + 1)
                dve.tensor_tensor(mem_hl[:, 2 * j:2 * j + 2, S:2 * S], ps[:, j, :].rearrange("p (a b) -> p a b", a=2),
                                  mem_hl[:, 2 * j:2 * j + 2, 0:S], ALU.subtract).then_inc(mem_ready, 1)
            split_to(RING)

            dve.wait_ge(pos_landed, 32)
            for q in range(4):
                step.done(dve.memset(sign[32 * q:32 * q + 32, :], -1.0 if q % 2 == 0 else 1.0))
            step.done(dve.tensor_copy(turns[:], pos_i[:]))
            step.wait()
            step.done(dve.tensor_scalar(angle[:], turns[:], freq[:, 0:1], None, ALU.mult))
            step.wait()
            step.done(dve.tensor_scalar(turns[:], angle[:], 1.0 / 6.283185307179586, MAGIC, ALU.mult, ALU.add))
            step.wait()
            step.done(dve.tensor_scalar(turns[:], turns[:], MAGIC, None, ALU.subtract))
            for part in TWO_PI_PARTS:
                step.wait()
                step.done(dve.scalar_tensor_tensor(out=angle[:], in0=turns[:], scalar=-part, in1=angle[:],
                                                   op0=ALU.mult, op1=ALU.add))
            step.wait()
            step.done(dve.tensor_scalar(angle[:], angle[:], 3.1415925, -3.1415925, ALU.min, ALU.max))
            step.wait()
            step.done(dve.scalar_tensor_tensor(out=turns[:], in0=angle[:], scalar=-1.0, in1=angle[:],
                                               op0=ALU.mult, op1=ALU.max))
            step.wait()
            dve.tensor_scalar(angle[:], angle[:], sign[:, 0:1], None, ALU.mult).then_inc(trig, 1)
            dve.tensor_scalar(turns[:], turns[:], -1.0, 1.5707964, ALU.mult, ALU.add).then_inc(trig, 1)

            def heads_of(t):
                return t.rearrange("p (a b) -> p a b", a=4)

            for l in range(DEPTH):
                add_half((2 * l + 1) * UG, 2 * l, H_MEM + l, heads_of(kv_mem[l][:, 0, :]))
                rows_out((2 * l + 2) * UG, 2 * l + 1, kv_mem[l][:, 1, :].rearrange("p (a b) -> p a b", a=TB))

            def x_lo(j, bank=None):
                src = res[:, 2 * j:2 * j + 2, :] if bank is None else bank
                dve.tensor_tensor(xy[:, 2 * j:2 * j + 2, S:2 * S], src, xy[:, 2 * j:2 * j + 2, 0:S],
                                  ALU.subtract).then_inc(x_ready, 1)

            for j in range(KC // 2):
                dve.wait_ge(x_hi, j + 1)
                x_lo(j, ps[:, j % 4, :].rearrange("p (a b) -> p a b", a=2))
            for l in range(DEPTH):
                dve.wait_ge(params_turned, l + 1)
                dve.tensor_copy(conv_col[:, l, :, :].rearrange("p a b -> p (a b)"), ps[:, l, 0:8 * FC]) \
                    .then_inc(params_ready, 1)
            dve.wait_ge(params_turned, 3)
            dve.tensor_copy(ln_col[:].rearrange("p a b c -> p (a b c)"), ps[:, 2, 0:P]).then_inc(params_ready, 1)
            dve.tensor_copy(misc_col[:], ps[:, 2, P:P + POOL_CHUNKS + 2 * LC]).then_inc(params_ready, 1)

            def attention(l):
                heads, h0 = HEADS[l], HEAD0[l]
                n = len(heads)
                for s in range(n + 3):
                    if s < n:
                        scale = MEM_SCALE if heads[s][0] == "mem" else MLA_SCALE
                        c = slice(2 * s, 2 * s + TB)
                        dve.wait_ge(scores_ready, h0 + s + 1)
                        step.done(dve.tensor_reduce(soft[:, 0, c], ps[:, s % 3, :].rearrange("p (a b) -> p a b", a=TB),
                                                    AX_X, ALU.max))
                        step.wait()
                        dve.tensor_scalar(soft[:, 1, c], soft[:, 0, c], -scale, None, ALU.mult).then_inc(neg_max, 1)
                    if s >= 3:
                        h = s - 3
                        dve.wait_ge(y_hi, h0 + h + 1)
                        y = xy[:, y_chunk(l, h), :]
                        dve.tensor_tensor(y[:, S:2 * S], ps[:, 6 + h % 2, 0:S], y[:, 0:S], ALU.subtract) \
                            .then_inc(y_ready, 1)
                    if s < n:
                        dve.wait_ge(exps, h0 + s + 1)
                        step.done(dve.reciprocal(soft[:, 3, c], soft[:, 2, c]))
                        step.wait()
                        for t in range(TB):
                            ins = dve.tensor_scalar(probs[s % 3][:, t, :], probs[s % 3][:, t, :],
                                                    soft[:, 3, 2 * s + t:2 * s + t + 1], None, ALU.mult)
                        ins.then_inc(probs_ready, 1)

            def layer_norm(k):
                l, which, u0, n_units, g0, h0 = LN_AT[k]

                def chunks(g):
                    return res[:, 4 * g:4 * g + 4, :]

                for g in range(4):
                    e = u0 + (g + 1) * n_units
                    split_to(e + RING)
                    dve.wait_ge(halves, h0 + g + 1)
                    step.done(dve.scalar_tensor_tensor(out=chunks(g), in0=chunks(g), scalar=ALPHA,
                                                       in1=second_cols(g0 + g), op0=ALU.mult, op1=ALU.add))
                    step.wait()
                    dve.tensor_tensor(chunks(g), chunks(g), first_half[k][:], ALU.add).then_inc(evacuated, 1)
                    dve.wait_ge(evacuated, g0 + g + 1)
                    if g == 0:
                        step.done(dve.tensor_tensor(fold_b[:], res[:, 0:2, :], res[:, 2:4, :], ALU.add))
                        step.wait()
                        dve.tensor_tensor(fold_a[:], fold_b[:, 0, :], fold_b[:, 1, :], ALU.add).then_inc(col_sum, 1)
                        continue
                    if g == 1:
                        dve.wait_ge(shift_ready, k + 1)
                        dve.tensor_tensor(chunks(0), chunks(0), wide(shift[:].unsqueeze(1), 4), ALU.subtract) \
                            .then_inc(shifted, 1)
                    dve.tensor_tensor(chunks(g), chunks(g), wide(shift[:].unsqueeze(1), 4), ALU.subtract) \
                        .then_inc(shifted, 1)
                    dve.wait_ge(shifted, 4 * k + g + 1)
                    if g == 1:
                        step.done(dve.tensor_tensor(sum_d[k][:], chunks(0), chunks(1), ALU.add))
                    else:
                        step.wait()
                        step.done(dve.tensor_tensor(sum_d[k][:], sum_d[k][:], chunks(g), ALU.add))
                step.wait()
                step.done(dve.tensor_tensor(fold_b[:], sum_d[k][:, 0:2, :], sum_d[k][:, 2:4, :], ALU.add))
                step.wait()
                dve.tensor_tensor(fold_a[:], fold_b[:, 0, :], fold_b[:, 1, :], ALU.add).then_inc(sums_ready, 1)
                dve.wait_ge(sums_ready, 2 * k + 1)
                dve.wait_ge(sq_used, 3 * k + 3)
                step.done(dve.tensor_tensor(fold_b[:], sum_dd[k][:, 0:2, :], sum_dd[k][:, 2:4, :], ALU.add))
                step.wait()
                dve.tensor_tensor(sum_dd[k][:, 0, :], fold_b[:, 0, :], fold_b[:, 1, :], ALU.add) \
                    .then_inc(sums_ready, 1)
                dve.wait_ge(stat_done, 2 * k + 2)
                step.done(dve.tensor_scalar(var[:], ps[:, bank_set(g0) + 1, 0:S], 1.0 / D, LN_EPS, ALU.mult, ALU.add))
                dve.wait_ge(mean_ready, k + 1)
                step.done(dve.tensor_tensor(mean_rstd[:], mean[:], mean[:], ALU.mult))
                step.wait()
                dve.tensor_tensor(var[:], var[:], mean_rstd[:], ALU.subtract).then_inc(var_ready, 1)
                dve.wait_ge(std_ready, k + 1)
                step.done(dve.reciprocal(rstd[:], std[:]))
                step.wait()
                step.done(dve.tensor_tensor(mean_rstd[:], mean[:], rstd[:], ALU.mult))
                for j in range(KC // 2 + 1):
                    if j < KC // 2:
                        pair = res[:, 2 * j:2 * j + 2, :]
                        step.wait()
                        step.done(dve.tensor_tensor(pair, pair, wide(rstd[:].unsqueeze(1), 2), ALU.mult))
                        step.wait()
                        dve.tensor_tensor(pair, pair, wide(mean_rstd[:].unsqueeze(1), 2), ALU.subtract) \
                            .then_inc(normed, 1)
                    if j >= 1 and k < 3:
                        dve.wait_ge(x_hi, 8 * (k + 1) + j)
                        x_lo(j - 1)

            def ffn(l):
                u0 = U_UP[l]
                dve.memset(h_pad[:, :, 0:1], 0.0)
                dve.memset(h_pad[:, :, S + 1:S + 2], 0.0).then_inc(pad_zero, 1)

                def convolve(dst, chunk):
                    def col(t, b):
                        return conv_col[:, l, t, bass.ds(chunk + b, 1)]

                    done = [step.done(dve.tensor_scalar(dst[:, b, :], h_pad[:, b, 1:S + 1], col(1, b), col(3, b),
                                                        ALU.mult, ALU.add)) for b in range(4)]
                    for t in (0, 2):
                        for b in range(4):
                            step.wait(done[b])
                            done[b] = step.done(dve.scalar_tensor_tensor(
                                out=dst[:, b, :], in0=h_pad[:, b, t:t + S], scalar=col(t, b), in1=dst[:, b, :],
                                op0=ALU.mult, op1=ALU.add))

                with dve.Fori(0, FG) as i:
                    step.loop(i, 26)

                    def ahead(a, b):
                        for j in range(a, b):
                            split(u0 + RING + j, i * (2 * UG), 0)

                    def hidden(half):
                        g = G_UP[l] + half
                        dve.wait_ge(halves, i * 2 + (H_UP[l] + half + 1))
                        dve.tensor_tensor(h_pad[:, :, 1:S + 1], h_pad[:, :, 1:S + 1], second_cols(g), ALU.add) \
                            .then_inc(evacuated, 1)
                        dve.wait_ge(evacuated, i * 2 + (g + 1))

                    ahead(0, UG)
                    hidden(0)
                    convolve(gate, i * 4)
                    step.wait()
                    dve.sem_inc(conv_gate, 1)
                    ahead(UG, 2 * UG)
                    hidden(1)
                    convolve(val, i * 4 + FC)
                    dve.wait_ge(silu_done, i + (FG * l + 1))
                    step.wait()
                    dve.tensor_tensor(val[:], val[:], gate[:], ALU.mult).then_inc(product, 1)
                    dve.wait_ge(act_hi, i + (FG * l + 1))
                    a = act_hl[:, bass.ds(i * 4, 4), :]
                    dve.tensor_tensor(a[:, :, S:2 * S], val[:], a[:, :, 0:S], ALU.subtract).then_inc(act_ready, 1)
                    step.done(dve.memset(h_pad[:, :, 0:1], 0.0))
                    step.done(dve.memset(h_pad[:, :, S + 1:S + 2], 0.0))
                step.end_loop(FG)
                skip_to(u0 + RING + 2 * FG * UG)

            add_half(U_IN0 + UG, G_IN0, H_IN0, q_mem[0][:])
            for g in range(3):
                add_half(U_IN0 + (2 + g) * UG, G_IN0 + 1 + g, H_IN0 + 1 + g, u_pad[:, 4 * g:4 * g + 4, PAD:PAD + S])
            attention(0)
            for k in range(len(WINDOWS)):
                u = u_pad[:, GC * k:GC * k + GC, PAD:PAD + S]
                dve.wait_ge(windowed, k + 1)
                dve.tensor_tensor(u, win[(k + 1) % 2][:, :, PAD:PAD + S], u, ALU.subtract).then_inc(pool_diff, 1)
            for k in range(len(WINDOWS)):
                dve.wait_ge(pool_hi, k + 1)
                p = pooled[:, GC * k:GC * k + GC, :]
                dve.tensor_tensor(p[:, :, S:2 * S], u_pad[:, GC * k:GC * k + GC, PAD:PAD + S], p[:, :, 0:S],
                                  ALU.subtract).then_inc(pooled_ready, 1)
            for g in range(3):
                add_half(U_GW + 2 * (g + 1), G_GW + g, H_GW + g, y_pool[:])
                dve.wait_ge(pool_y_hi, g + 1)
                y = xy[:, 4 * g:4 * g + 4, :]
                dve.tensor_tensor(y[:, :, S:2 * S], y_pool[:], y[:, :, 0:S], ALU.subtract).then_inc(pool_y_ready, 1)
            layer_norm(0)
            ffn(0)
            layer_norm(1)

            def latent_norm(n, e, g, h):
                add_half(e, g, h, latent[:])
                dve.wait_ge(lat_sq, n + 1)
                sq = latent_sq
                step.done(dve.tensor_tensor(sq[:, 0:2, :], sq[:, 0:2, :], sq[:, 2:4, :], ALU.add))
                step.wait()
                dve.tensor_tensor(sq[:, 0, :], sq[:, 0, :], sq[:, 1, :], ALU.add).then_inc(lat_sum, 1)
                dve.wait_ge(lat_stat, n + 1)
                dve.tensor_scalar(var[:], ps[:, bank_set(g), 0:S], 1.0 / QL, RMS_EPS, ALU.mult, ALU.add) \
                    .then_inc(lat_var, 1)
                dve.wait_ge(lat_std, n + 1)
                step.done(dve.reciprocal(rstd[:], std[:]))
                step.wait()
                dve.tensor_tensor(latent[:], latent[:], wide(rstd[:].unsqueeze(1), LC), ALU.mult) \
                    .then_inc(lat_normed, 1)
                dve.wait_ge(lat_hi, n + 1)
                hl = (qn_hl, kvn_hl)[n]
                dve.tensor_tensor(hl[:, :, S:2 * S], latent[:], hl[:, :, 0:S], ALU.subtract).then_inc(latent_ready, 1)

            def rotate(n, t, swap, width):
                dve.wait_ge(swapped, n)
                step.done(dve.tensor_tensor(t[:], t[:], cos_t[:].to_broadcast([P, width, S]), ALU.mult))
                step.done(dve.tensor_tensor(swap[:], swap[:], sin_t[:].to_broadcast([P, width, S]), ALU.mult))
                step.wait()
                dve.tensor_tensor(t[:], t[:], swap[:], ALU.add).then_inc(rope_ready, 1)

            latent_norm(0, U_IN1 + UG, G_IN1, H_IN1)
            latent_norm(1, U_IN1 + 2 * UG, G_IN1 + 1, H_IN1 + 1)
            add_half(U_IN1 + 2 * UG + 2, G_IN1 + 2, H_IN1 + 2, k_rope[:], 1)
            dve.wait_ge(trig_done, 2)
            rotate(1, k_rope, k_swap, 1)
            add_half(U_UQ, G_IN1 + 3, H_IN1 + 3, q_mem[1][:])
            for g in range(3):
                add_half(U_UQ + 2 * (g + 1), G_UQ + g, H_UQ + g, q_nope[:, 4 * g:4 * g + 4, :])
            add_half(U_QR + 2, G_QR, H_QR, q_rope[:, 0:4, :])
            add_half(U_QR + 3, G_QR + 1, H_QR + 1, q_rope[:, 4:6, :], 2)
            rotate(2, q_rope, q_swap, MLA_HEADS // 2)
            for g in range(3):
                add_half(U_UK + 2 * (g + 1), G_UK + g, H_UK + g, k_nope[:, 4 * g:4 * g + 4, :])
            for g in range(3):
                rows_out(U_UV + 2 * (g + 1), G_UV + g, v_mla[:, :, 512 * g:512 * g + 512])
            attention(1)
            layer_norm(2)
            ffn(1)
            layer_norm(3)

        @block.gpsimd
        def _(pool):
            step = Steps(pool, pool_step)
            step.done(pool.memset(ident[:], 0.0))
            step.wait()
            step.done(pool.affine_select(out=ident[:], in_=ident[:], compare_op=ALU.not_equal, fill=1.0, base=0,
                                         pattern=[[-1, P]], channel_multiplier=1))
            step.wait()
            pool.memset(ones[:], 1.0).then_inc(consts_ready, 1)

            pool.wait_ge(units_done, U_IN0)
            pool.memset(u_pad[:, :, 0:PAD], 0.0)
            pool.memset(u_pad[:, :, PAD + S:], 0.0).then_inc(pads_ready, 1)
            pool.wait_ge(pads_ready, 1)
            for k, w in enumerate(WINDOWS):
                h = w // 2
                pool.memset(inv_count[:, k, h:S - h + 1], 1.0 / w)
                for t in range(h):
                    pool.memset(inv_count[:, k, t:t + 1], 1.0 / (t + h))
                for t in range(S - h + 1, S):
                    ins = pool.memset(inv_count[:, k, t:t + 1], 1.0 / (S - t + h))
            step.done(ins)
            step.wait()
            for k, w in enumerate(WINDOWS):
                pool.wait_ge(evacuated, G_IN0 + 1 + (1, 2, 3, 3)[k])
                src = u_pad[:, GC * k:GC * k + GC, :]
                n = 0
                for m in range(k + 1):
                    back, ahead_ = (1, 0) if m == 0 else (2 ** (m - 1), 2 ** (m - 1))
                    reach = w // 2 - 2 ** m
                    a, b = PAD - reach, PAD + S + reach
                    dst = win[(k + m) % 2 if False else (k - m) % 2][:, :, a:b]
                    if k >= 1 and m < 2:
                        pool.wait_ge(pool_diff, k)
                    step.done(pool.tensor_tensor(dst, src[:, :, a - back:b - back],
                                                 src[:, :, a + ahead_:b + ahead_], ALU.add))
                    step.wait()
                    src = win[(k - m) % 2]
                assert src is win[0]
                pool.tensor_tensor(win[(k + 1) % 2][:, :, PAD:PAD + S], src[:, :, PAD:PAD + S],
                                   wide(inv_count[:, k:k + 1, :], GC), ALU.mult).then_inc(windowed, 1)

            for k in range(4):
                for g in range(1, 4):
                    pool.wait_ge(squared, 4 * k + g + 1)
                    if g > 1:
                        pool.wait_ge(sq_used, 3 * k + g - 1)
                    pool.tensor_tensor(sum_dd[k][:], sum_dd[k][:], squares[k][:], ALU.add).then_inc(sq_used, 1)

        @block.tensor
        def _(pe):
            def multiply(u, g, rhs, chunks, nb=4, width=512, first=False, last=False, turn=0):
                s, b0 = u % RING, bank_set(g)
                pe.wait_ge(lo_ready, u + 1 + turn)
                for c in range(chunks):
                    x_hl = rhs(c)
                    end = last and c == chunks - 1
                    for b in range(nb):
                        at_ = c * width + b * P
                        hi, lo = w_hi[:, s, at_:at_ + P], w_lo[:, s, at_:at_ + P]
                        bank = ps[:, b0 + b, :]
                        if end:
                            pe.matmul(bank[:, S:2 * S], lo, x_hl[:, 0:S], start=False, stop=False)
                            ins = pe.matmul(bank, hi, x_hl, start=False, stop=True)
                        else:
                            pe.matmul(bank, hi, x_hl, start=first and c == 0, stop=False)
                            ins = pe.matmul(bank[:, S:2 * S], lo, x_hl[:, 0:S], start=False, stop=False)
                ins.then_inc(units_done, 1)

            def multiply_rows(u, g, lhs, chunks, first=False, last=False):
                s, b0 = u % RING, bank_set(g)
                pe.wait_ge(lo_ready, u + 1)
                for c in range(chunks):
                    x_hl = lhs(c)
                    hi, lo = w_hi[:, s, c * 512:(c + 1) * 512], w_lo[:, s, c * 512:(c + 1) * 512]
                    for t in range(TB):
                        x_hi_, x_lo_ = x_hl[:, t * P:(t + 1) * P], x_hl[:, S + t * P:S + (t + 1) * P]
                        end = last and c == chunks - 1
                        pe.matmul(ps[:, b0 + t, :], x_hi_, hi, start=first and c == 0, stop=False)
                        pe.matmul(ps[:, b0 + t, :], x_lo_, hi, start=False, stop=False)
                        ins = pe.matmul(ps[:, b0 + t, :], x_hi_, lo, start=False, stop=end)
                ins.then_inc(units_done, 1)

            def banks_free(g, turn=0):
                pe.wait_ge(evacuated, g - 1 + turn)

            def xy_chunk(j):
                return lambda c: xy[:, 2 * j + c, :]

            def column_sums(bank, src):
                return pe.matmul(ps[:, bank, 0:S], ones[:], src, start=True, stop=True)

            pe.wait_ge(consts_ready, 1)
            for j in range(KC // 2):
                pe.wait_ge(mem_landed[j // 2], 16)
                for c in range(2):
                    for t in range(TB):
                        ins = pe.transpose(ps[:, j, c * S + t * P:c * S + (t + 1) * P],
                                           mem_rows[:, t, (2 * j + c) * P:(2 * j + c + 1) * P], ident[:])
                ins.then_inc(mem_turned, 1)
            for l in range(DEPTH):
                for kind in range(2):
                    g = 2 * l + kind
                    if g < 2:
                        pe.wait_ge(mem_ready, 4 * (g + 1))
                    else:
                        banks_free(g)
                    for j in range(UG):
                        pe.wait_ge(mem_ready, j + 1)
                        (multiply, multiply_rows)[kind](g * UG + j, g, lambda c: mem_hl[:, 2 * j + c, :], 2,
                                                        first=j == 0, last=j == UG - 1)

            pe.wait_ge(evacuated, 3)
            pe.wait_ge(x_landed, 16)
            for j in range(KC // 2):
                if j >= 4:
                    pe.wait_ge(x_ready, j - 3)
                for c in range(2):
                    for t in range(TB):
                        ins = pe.transpose(ps[:, j % 4, c * S + t * P:c * S + (t + 1) * P],
                                           x_rows[:, t, (2 * j + c) * P:(2 * j + c + 1) * P], ident[:])
                ins.then_inc(x_turned, 1)
            pe.wait_ge(params_landed, 16 * (4 * DEPTH + 7))
            for l in range(DEPTH):
                pe.wait_ge(x_ready, 5 + l)
                for t in range(4):
                    ins = pe.transpose(ps[:, l, t * 2 * FC:(t + 1) * 2 * FC], conv_rows[:, l, t, :],
                                       ident[0:2 * FC, 0:2 * FC])
                ins.then_inc(params_turned, 1)
            pe.wait_ge(x_ready, 7)
            n_misc = POOL_CHUNKS + 2 * LC
            pe.transpose(ps[:, 2, 0:P], ln_rows[:], ident[:])
            pe.transpose(ps[:, 2, P:P + n_misc], misc_rows[:], ident[0:n_misc, 0:n_misc]).then_inc(params_turned, 1)

            def attention(l):
                heads, h0 = HEADS[l], HEAD0[l]
                n = len(heads)
                kv = (kv_mem[0], kv_back)[l]
                for s in range(n + 3):
                    if s < n:
                        kind, h = heads[s]
                        if s >= 3:
                            pe.wait_ge(exps, h0 + s - 2)
                        q = q_mem[l][:, h, :] if kind == "mem" else q_nope[:, h, :]
                        k = kv[:, 0, h * S:(h + 1) * S] if kind == "mem" else k_nope[:, h, :]
                        for t in range(TB):
                            bank = ps[:, s % 3, t * S:(t + 1) * S]
                            rot = kind == "mla"
                            ins = pe.matmul(bank, q[:, t * P:(t + 1) * P], k, start=True, stop=not rot)
                            if rot:
                                r = ROPE * (h % 2)
                                ins = pe.matmul(bank, q_rope[r:r + ROPE, h // 2, t * P:(t + 1) * P],
                                                k_rope[r:r + ROPE, 0, :], start=False, stop=True)
                        ins.then_inc(scores_ready, 1)
                    if 2 <= s < n + 2:
                        h = s - 2
                        pe.wait_ge(probs_ready, h0 + h + 1)
                        if h >= 3:
                            pe.wait_ge(probs_t_ready, h0 + h - 2)
                        for m in range(TB):
                            for t in range(TB):
                                ins = pe.transpose(ps[:, 3 + h % 3, m * S + t * P:m * S + (t + 1) * P],
                                                   probs[h % 3][:, t, m * P:(m + 1) * P], ident[:])
                        ins.then_inc(probs_turned, 1)
                    if s >= 3:
                        n_, (kind, h) = s - 3, heads[s - 3]
                        pe.wait_ge(probs_t_ready, h0 + n_ + 1)
                        if n_ >= 2:
                            pe.wait_ge(y_ready, h0 + n_ - 1)
                        for m in range(TB):
                            v = kv[:, 1, m * 512 + h * HEAD:m * 512 + (h + 1) * HEAD] if kind == "mem" \
                                else v_mla[:, m, h * HEAD:(h + 1) * HEAD]
                            ins = pe.matmul(ps[:, 6 + n_ % 2, 0:S], v, probs_t[n_ % 2][:, m, :],
                                            start=m == 0, stop=m == TB - 1)
                        ins.then_inc(heads_out, 1)

            def stat_products(k):
                b = bank_set(LN_AT[k][4])
                pe.wait_ge(sums_ready, 2 * k + 1)
                column_sums(b, fold_a[:])
                pe.wait_ge(sums_ready, 2 * k + 2)
                column_sums(b + 1, sum_dd[k][:, 0, :]).then_inc(stat_done, 1)

            def mix_out(l):
                k = 2 * l
                for g in range(4):
                    gg = G_OUT[l] + g
                    if g >= 2 or l == 1:
                        banks_free(gg)
                    for j in range(UG):
                        if g == 0 and l == 0 and j < POOL_CHUNKS // 2:
                            pe.wait_ge(pool_y_ready, j // 2 + 1)
                        if g == 1 and j == 4:
                            pe.wait_ge(col_sum, k + 1)
                            column_sums(bank_set(G_OUT[l]), fold_a[:]).then_inc(stat_done, 1)
                        if g == 2 and j == 0:
                            pe.wait_ge(shift_ready, k + 1)
                        multiply(U_OUT[l] + g * UG + j, gg, xy_chunk(j), 2, first=j == 0, last=j == UG - 1)
                stat_products(k)

            def ffn(l):
                k = 2 * l + 1
                with pe.Fori(0, FG) as i:
                    for h in range(2):
                        g = G_UP[l] + h
                        banks_free(g, i * 2)
                        if h == 0:
                            pe.wait_ge(var_ready, 2 * l + 1)
                        for j in range(UG):
                            if h == 0:
                                pe.wait_ge(x_ready, 8 * (2 * l + 1) + j + 1)
                            multiply(U_UP[l] + h * UG + j, g, xy_chunk(j), 2, first=j == 0, last=j == UG - 1,
                                     turn=i * (2 * UG))
                flat = act_hl[:].rearrange("p a b -> p (a b)")
                loops = (DG - 6) // RING
                for g in range(4):
                    gg, u = G_DOWN[l] + g, U_DOWN[l] + g * DG
                    banks_free(gg)
                    if g == 2:
                        pe.wait_ge(shift_ready, k + 1)
                    for j in range(2):
                        pe.wait_ge(act_ready, FG * l + 1)
                        multiply(u + j, gg, lambda c: act_hl[:, 2 * j + c, :], 2, first=j == 0)
                    pe.wait_ge(act_ready, FG * l + FG - 2)
                    with pe.Fori(0, loops) as i:
                        for j in range(RING):
                            multiply(u + 2 + j, gg,
                                     lambda c: flat[:, bass.ds(i * (2 * RING * 2 * S) + (4 + 2 * j + c) * 2 * S, 2 * S)],
                                     2, turn=i * RING)
                    if g == 1:
                        pe.wait_ge(col_sum, k + 1)
                        column_sums(bank_set(G_DOWN[l]), fold_a[:]).then_inc(stat_done, 1)
                    pe.wait_ge(act_ready, FG * l + FG)
                    for j in range(DG - RING, DG):
                        multiply(u + j, gg, lambda c: act_hl[:, 2 * j + c, :], 2, last=j == DG - 1)
                stat_products(k)

            pe.wait_ge(params_ready, 4)
            for g in range(4):
                banks_free(G_IN0 + g)
                for j in range(UG):
                    if g == 0:
                        pe.wait_ge(x_ready, j + 1)
                        if j == 0:
                            pe.wait_ge(x_ready, 8)
                    multiply(U_IN0 + g * UG + j, G_IN0 + g, xy_chunk(j), 2, first=j == 0, last=j == UG - 1)
            pe.wait_ge(evacuated, G_GW)
            attention(0)
            pe.wait_ge(y_ready, HEAD0[1])
            for r in range(6):
                u, g = U_GW + r, G_GW + r // 2
                s = u % RING
                if r % 2 == 0 and r >= 4:
                    banks_free(g)
                pe.wait_ge(lo_ready, u + 1)
                for h in range(2):
                    w, b = divmod(2 * r + h, GC)
                    pe.wait_ge(pooled_ready, w + 1)
                    bank = ps[:, bank_set(g) + 2 * (r % 2) + h, :]
                    for c in range(GC):
                        at_ = (h * GC + c) * P
                        pc = pooled[:, GC * w + c, :]
                        hi, lo = w_hi[:, s, at_:at_ + P], w_lo[:, s, at_:at_ + P]
                        if c == GC - 1:
                            pe.matmul(bank[:, S:2 * S], lo, pc[:, 0:S], start=False, stop=False)
                            ins = pe.matmul(bank, hi, pc, start=False, stop=True)
                        else:
                            pe.matmul(bank, hi, pc, start=c == 0, stop=False)
                            pe.matmul(bank[:, S:2 * S], lo, pc[:, 0:S], start=False, stop=False)
                ins.then_inc(units_done, 1)
            banks_free(G_OUT[0])
            banks_free(G_OUT[0] + 1)
            mix_out(0)
            ffn(0)

            g = G_IN1
            pe.wait_ge(var_ready, 2)
            for n in range(2):
                banks_free(g + n)
                for j in range(UG):
                    if n == 1 and j == 4:
                        pe.wait_ge(lat_sum, 1)
                        column_sums(bank_set(g), latent_sq[:, 0, :]).then_inc(lat_stat, 1)
                    pe.wait_ge(x_ready, 8 * 2 + j + 1)
                    multiply(U_IN1 + n * UG + j, g + n, xy_chunk(j), 2, first=j == 0, last=j == UG - 1)
            pe.wait_ge(lat_var, 1)
            banks_free(g + 2)
            for r in range(2):
                multiply(U_IN1 + 2 * UG + r, g + 2, lambda c: xy[:, 8 * r + c, :], 8, nb=1, width=P,
                         first=r == 0, last=r == 1)
            pe.wait_ge(lat_sum, 2)
            column_sums(bank_set(g + 1), latent_sq[:, 0, :]).then_inc(lat_stat, 1)
            pe.wait_ge(lat_var, 2)
            banks_free(g + 3)
            for j in range(UG):
                multiply(U_IN1 + 2 * UG + 2 + j, g + 3, xy_chunk(j), 2, first=j == 0, last=j == UG - 1)
            pe.wait_ge(latent_ready, 1)
            for n in range(3):
                banks_free(G_UQ + n)
                for j in range(2):
                    multiply(U_UQ + 2 * n + j, G_UQ + n, lambda c: qn_hl[:, 2 * j + c, :], 2, first=j == 0, last=j == 1)
            for r in range(3):
                gg = G_QR + r // 2
                if r != 1:
                    banks_free(gg)
                s, b0 = (U_QR + r) % RING, bank_set(gg) + 2 * (r % 2)
                pe.wait_ge(lo_ready, U_QR + r + 1)
                for b in range(2):
                    for c in range(LC):
                        at_ = c * 256 + b * P
                        hi, lo = w_hi[:, s, at_:at_ + P], w_lo[:, s, at_:at_ + P]
                        bank, xc = ps[:, b0 + b, :], qn_hl[:, c, :]
                        if c == LC - 1:
                            pe.matmul(bank[:, S:2 * S], lo, xc[:, 0:S], start=False, stop=False)
                            ins = pe.matmul(bank, hi, xc, start=False, stop=True)
                        else:
                            pe.matmul(bank, hi, xc, start=c == 0, stop=False)
                            pe.matmul(bank[:, S:2 * S], lo, xc[:, 0:S], start=False, stop=False)
                ins.then_inc(units_done, 1)
            pe.wait_ge(latent_ready, 2)
            for n in range(3):
                banks_free(G_UK + n)
                for j in range(2):
                    multiply(U_UK + 2 * n + j, G_UK + n, lambda c: kvn_hl[:, 2 * j + c, :], 2, first=j == 0, last=j == 1)
            for n in range(3):
                banks_free(G_UV + n)
                for j in range(2):
                    multiply_rows(U_UV + 2 * n + j, G_UV + n, lambda c: kvn_hl[:, 2 * j + c, :], 2,
                                  first=j == 0, last=j == 1)
            pe.wait_ge(evacuated, G_OUT[1])
            pe.wait_ge(rope_ready, 2)
            pe.wait_ge(kv_loaded, 16)
            attention(1)
            pe.wait_ge(y_ready, HEAD0[1] + len(HEADS[1]))
            mix_out(1)
            ffn(1)
            pe.wait_ge(var_ready, 4)
            pe.wait_ge(evacuated, G_DOWN[1] + 4)
            for j in range(KC // 2):
                pe.wait_ge(affine, j + 1)
                for t in range(TB):
                    for c in range(2):
                        ins = pe.transpose(ps[:, j, t * 2 * P + c * P:t * 2 * P + (c + 1) * P],
                                           res[:, 2 * j + c, t * P:(t + 1) * P], ident[:])
                ins.then_inc(final_turned, 1)


LN_EPS = 1e-5
RMS_EPS = 1e-6
_INS = ["x", "mem", "positions", "pool_w_in", "pool_group_w", "pool_scale", "pool_w_out", "mla_w_in", "mla_q_norm_g",
        "mla_kv_norm_g", "mla_w_uq", "mla_w_uk", "mla_w_uv", "mla_w_out", "mem_w_kv", "ln1_g", "ln1_b", "ln2_g",
        "ln2_b", "ffn_w_up", "ffn_conv_w", "ffn_conv_b", "ffn_w_down"]


def kernel(**inputs):
    import numpy as _np
    import concourse.bacc as _bacc
    from concourse import mybir as _mybir
    from concourse.bass_utils import run_bass_kernel_spmd as _run

    nc = _bacc.Bacc("TRN2", target_bir_lowering=False, num_devices=1)
    arrays, args = {}, []
    for name in _INS:
        a = _np.ascontiguousarray(inputs[name])
        arrays[f"in_{name}_dram"] = a
        args.append(nc.dram_tensor(f"in_{name}_dram", a.shape, _mybir.dt.from_np(a.dtype), kind="ExternalInput").ap())
    half = ROPE // 2
    freqs = _np.float32(10000.0) ** (-_np.arange(0, ROPE, 2, dtype=_np.float32) / _np.float32(ROPE))
    arrays["rotary_freq"] = _np.ascontiguousarray(_np.tile(freqs, P // half).reshape(P, 1).astype(_np.float32))
    args.append(nc.dram_tensor("rotary_freq", (P, 1), _mybir.dt.float32, kind="ExternalInput").ap())
    shape = inputs["x"].shape
    args.append(nc.dram_tensor("out_0_dram", shape, _mybir.dt.float32, kind="ExternalOutput").ap())
    encoder_trunk(nc, *args)
    r = _run(nc, [arrays], core_ids=[0])
    return r.results[0]["out_0_dram"]
```

```python
from contextlib import ExitStack

import concourse.bass as bass
from concourse import mybir

P = 128
F32 = mybir.dt.float32
F32R = mybir.dt.float32r
I32 = mybir.dt.int32
ALU = mybir.AluOpType
ACT = mybir.ActivationFunctionType
AX_X = mybir.AxisListType.X

RING = 4
UNIT = 1024
BANK = 512
HEAD = 128
ROPE = 64
WINDOWS = (2, 4, 8, 16)
PAD = 8
MAGIC = 1.5 * 2.0 ** 23
TWO_PI_PARTS = (6.28125, 1.9350051879882812e-03, 3.0199159819e-07)


class Steps:

    def __init__(self, engine, sem):
        self.engine, self.sem, self.n, self.turn = engine, sem, 0, 0

    def done(self, instruction):
        instruction.then_inc(self.sem, 1)
        self.n += 1
        return self.n

    def wait(self, n=None):
        self.engine.wait_ge(self.sem, (self.n if n is None else n) + self.turn)

    def loop(self, i, per_turn):
        self.first, self.per_turn = self.n, per_turn
        self.turn = i * per_turn

    def end_loop(self, turns):
        assert self.n - self.first == self.per_turn, (self.n - self.first, self.per_turn)
        self.turn = 0
        self.n = self.first + self.per_turn * turns


def encoder_trunk(nc, x, mem, positions, pool_w_in, pool_group_w, pool_scale, pool_w_out, mla_w_in,
                  mla_q_norm_g, mla_kv_norm_g, mla_w_uq, mla_w_uk, mla_w_uv, mla_w_out, mem_w_kv,
                  ln1_g, ln1_b, ln2_g, ln2_b, ffn_w_up, ffn_conv_w, ffn_conv_b, ffn_w_down, inv_freq, out):
    _, S, D = x.shape
    DEPTH = ffn_w_up.shape[0]
    FF = ffn_w_down.shape[1]
    KC = D // P
    FC = FF // P
    TB = S // P
    MEM_HEADS = mem_w_kv.shape[2] // (2 * HEAD)
    MLA_HEADS = mla_w_uk.shape[2] // HEAD
    QL = mla_w_uq.shape[1]
    LC = QL // P
    POOL_CH = D - MEM_HEADS * HEAD
    POOL_CHUNKS = POOL_CH // P
    GC = POOL_CHUNKS // len(WINDOWS)
    ALPHA = (2 * DEPTH) ** 0.25
    MEM_SCALE = HEAD ** -0.5
    MLA_SCALE = (HEAD + ROPE) ** -0.5
    assert (S, D, DEPTH, FC, MEM_HEADS, MLA_HEADS, LC) == (256, 2048, 2, 44, 4, 12, 4)

    UG = KC // 2
    DG = FC // 2
    FG = FC // 4
    U_IN0 = 2 * UG
    U_MEM = [0, U_IN0 + 4 * UG]
    U_GW = U_MEM[1] + 2 * UG
    U_OUT = [U_GW + 6, 0]
    U_UP = [U_OUT[0] + 4 * UG, 0]
    U_DOWN = [U_UP[0] + 2 * FG * UG, 0]
    U_IN1 = U_DOWN[0] + 4 * DG
    U_UQ = U_IN1 + 3 * UG + 2
    U_QR = U_UQ + 6
    U_UK = U_QR + 3
    U_UV = U_UK + 6
    U_OUT[1] = U_UV + 6
    U_UP[1] = U_OUT[1] + 4 * UG
    U_DOWN[1] = U_UP[1] + 2 * FG * UG
    U_END = U_DOWN[1] + 4 * DG
    G_MEM, G_IN0, G_GW, G_OUT0 = [0, 6], 2, 8, 11
    G_UP0 = G_OUT0 + 4
    G_DOWN0 = G_UP0 + 2 * FG
    G_IN1 = G_DOWN0 + 4
    G_UQ = G_IN1 + 4
    G_QR = G_UQ + 3
    G_UK = G_QR + 2
    G_UV = G_UK + 3
    G_OUT1 = G_UV + 3
    G_OUT = [G_OUT0, G_OUT1]
    G_UP = [G_UP0, G_OUT1 + 4]
    G_DOWN = [G_DOWN0, G_OUT1 + 4 + 2 * FG]
    H_MEM, H_IN0 = [0, 5], 1
    H_GW = H_MEM[1] + 1
    H_OUT = [H_GW + 3, 0]
    H_UP = [H_OUT[0] + 3, 0]
    H_DOWN = [H_UP[0] + 2 * FG, 0]
    H_IN1 = H_DOWN[0] + 3
    H_UQ = H_IN1 + 4
    H_QR = H_UQ + 3
    H_UK = H_QR + 2
    H_OUT[1] = H_UK + 3
    H_UP[1] = H_OUT[1] + 3
    H_DOWN[1] = H_UP[1] + 2 * FG

    kv_scratch = nc.dram_tensor("kv_scratch", (P, 8 * S), F32, kind="Internal").ap()

    with ExitStack() as ctx:
        def sb(name, shape, dt=F32):
            return ctx.enter_context(nc.sbuf_tensor(name, shape, dt))

        def sem(name):
            return ctx.enter_context(nc.semaphore(name))

        raw = sb("raw", [P, RING, UNIT])
        w_hi = sb("w_hi", [P, RING, UNIT], F32R)
        w_lo = sb("w_lo", [P, RING, UNIT], F32R)
        res = sb("res", [P, KC, S])
        KB = 1024

        base0 = nc.sbuf_base
        sb("xy_region", [P, KC * 2 * S])
        sb("act_region", [P, FC * 2 * S])
        sb("tmp_region", [P, 3088])
        XY = base0
        AR = XY + KC * 2 * S * 4
        TR = AR + FC * 2 * S * 4
        assert nc.sbuf_base == TR + 3088 * 4, (nc.sbuf_base, TR)

        def at(name, shape, offset, dt=F32):
            return nc.alloc_sbuf_tensor_at(name, shape, dt, offset=offset)

        xy = at("xy", [P, KC, 2 * S], XY, F32R)
        act_hl = at("act_hl", [P, FC, 2 * S], AR, F32R)
        first_half = [at(f"first_half{k}", [P, 4, S], o) for k, o in ((0, AR + 32 * KB), (1, XY), (2, AR), (3, XY))]
        squares = [at(f"squares{k}", [P, 4, S], o + 4 * KB) for k, o in ((0, AR + 32 * KB), (1, XY), (2, AR), (3, XY))]
        sum_d = [at(f"sum_d{k}", [P, 4, S], o + 8 * KB) for k, o in ((0, AR + 32 * KB), (1, XY), (2, AR), (3, XY))]
        sum_dd = [at(f"sum_dd{k}", [P, 4, S], o + 12 * KB) for k, o in ((0, AR + 32 * KB), (1, XY), (2, AR), (3, XY))]
        mem_hl = at("mem_hl", [P, KC, 2 * S], AR, F32R)
        mem_rows = at("mem_rows", [P, TB, D], AR + 32 * KB)
        kv_mem = [at(f"kv_mem{l}", [P, 2, 4 * S], o) for l, o in ((0, AR + 49 * KB), (1, AR + 57 * KB))]
        x_rows = at("x_rows", [P, TB, D], AR + 65 * KB)
        conv_rows = at("conv_rows", [FC * 2, DEPTH, 4, P], AR + 81 * KB)
        ln_rows = at("ln_rows", [P, P], AR + 85 * KB)
        misc_rows = at("misc_rows", [POOL_CHUNKS + 2 * LC, P], AR + 85 * KB + 512)
        pos_i = at("pos_i", [P, S], AR + 86 * KB, I32)
        angle = at("angle", [P, S], AR + 87 * KB)
        turns = at("turns", [P, S], TR + 8 * KB)
        q_mem = [at("q_mem0", [P, 4, S], AR + 32 * KB + 13056), at("q_mem1", [P, 4, S], AR + 74 * KB)]
        u_pad = at("u_pad", [P, POOL_CHUNKS, S + 2 * PAD], AR + 32 * KB)
        win = [at(f"win{k}", [P, GC, S + 2 * PAD], TR + KB + 3264 * k) for k in range(2)]
        y_pool = at("y_pool", [P, 4, S], AR)
        pooled = at("pooled", [P, POOL_CHUNKS, 2 * S], AR + 65 * KB, F32R)
        qn_hl = at("qn_hl", [P, LC, 2 * S], AR, F32R)
        kvn_hl = at("kvn_hl", [P, LC, 2 * S], AR + 8 * KB, F32R)
        latent = at("latent", [P, LC, S], AR + 16 * KB)
        latent_sq = at("latent_sq", [P, LC, S], AR + 20 * KB)
        k_rope = at("k_rope", [P, 1, S], AR + 24 * KB)
        k_swap = at("k_swap", [P, 1, S], AR + 25 * KB)
        q_rope = at("q_rope", [P, MLA_HEADS // 2, S], AR + 26 * KB)
        q_swap = at("q_swap", [P, MLA_HEADS // 2, S], AR + 32 * KB)
        q_nope = at("q_nope", [P, MLA_HEADS, S], AR + 38 * KB)
        k_nope = at("k_nope", [P, MLA_HEADS, S], AR + 50 * KB)
        v_mla = at("v_mla", [P, TB, MLA_HEADS * HEAD], AR + 62 * KB)
        kv_back = at("kv_back", [P, 2, 4 * S], AR + 78 * KB)
        out_rows = at("out_rows", [P, TB, D], AR)
        h_pad = at("h_pad", [P, 4, S + 2], TR)
        gate = at("gate", [P, 4, S], TR + 4128)
        val = at("val", [P, 4, S], TR + 4128 + 4 * KB)
        probs = [at(f"probs{k}", [P, TB, S], TR + KB + 2 * KB * k) for k in range(3)]
        probs_t = [at(f"probs_t{k}", [P, TB, S], TR + 7 * KB + 2 * KB * k) for k in range(2)]
        soft = at("soft", [P, 4, 2 * 16], TR + 11 * KB)
        shift, mean, var, std, rstd, mean_rstd, fold_a = [at(n, [P, S], TR + KB * k) for k, n in enumerate(
            ["shift", "mean", "var", "std", "rstd", "mean_rstd", "fold_a"])]
        fold_b = at("fold_b", [P, 2, S], TR + 7 * KB)
        conv_col = sb("conv_col", [P, DEPTH, 4, 2 * FC])
        ln_col = sb("ln_col", [P, 4, DEPTH, KC])
        misc_col = sb("misc_col", [P, POOL_CHUNKS + 2 * LC])
        ident = sb("ident", [P, P])
        ones = sb("ones", [P, P])
        cos_t = sb("cos_t", [P, 1, S])
        sin_t = sb("sin_t", [P, 1, S])
        sign = sb("sign", [P, 1])
        freq = sb("freq", [P, 1])
        eps = sb("eps", [P, 1])
        inv_count = sb("inv_count", [P, len(WINDOWS), S])
        sqrt_warm = sb("sqrt_warm", [P, 1])

        ps = ctx.enter_context(nc.psum_tensor("ps", [P, 8, BANK], F32))

        raw_landed = [sem(f"raw_landed{s}") for s in range(RING)]
        hi_ready = sem("hi_ready")
        lo_ready = sem("lo_ready")
        units_done = sem("units_done")
        halves = sem("halves")
        evacuated = sem("evacuated")
        mem_landed = [sem(f"mem_landed{q}") for q in range(4)]
        x_landed = sem("x_landed")
        params_landed = sem("params_landed")
        pos_landed = sem("pos_landed")
        consts_ready = sem("consts_ready")
        mem_turned = sem("mem_turned")
        mem_hi = sem("mem_hi")
        mem_ready = sem("mem_ready")
        x_turned = sem("x_turned")
        x_hi = sem("x_hi")
        x_ready = sem("x_ready")
        params_turned = sem("params_turned")
        params_ready = sem("params_ready")
        trig = sem("trig")
        trig_done = sem("trig_done")
        kv_saved = sem("kv_saved")
        kv_loaded = sem("kv_loaded")
        pads_ready = sem("pads_ready")
        windowed = sem("windowed")
        pool_diff = sem("pool_diff")
        pool_hi = sem("pool_hi")
        pooled_ready = sem("pooled_ready")
        pool_y_hi = sem("pool_y_hi")
        pool_y_ready = sem("pool_y_ready")
        scores_ready = sem("scores_ready")
        neg_max = sem("neg_max")
        exps = sem("exps")
        probs_ready = sem("probs_ready")
        probs_turned = sem("probs_turned")
        probs_t_ready = sem("probs_t_ready")
        heads_out = sem("heads_out")
        y_hi = sem("y_hi")
        y_ready = sem("y_ready")
        col_sum = sem("col_sum")
        stat_done = sem("stat_done")
        shift_ready = sem("shift_ready")
        shifted = sem("shifted")
        squared = sem("squared")
        sums_ready = sem("sums_ready")
        var_ready = sem("var_ready")
        std_ready = sem("std_ready")
        normed = sem("normed")
        affine = sem("affine")
        conv_gate = sem("conv_gate")
        silu_done = sem("silu_done")
        product = sem("product")
        act_hi = sem("act_hi")
        act_ready = sem("act_ready")
        pad_zero = sem("pad_zero")
        sq_used = sem("sq_used")
        lat_sq = sem("lat_sq")
        lat_sum = sem("lat_sum")
        lat_stat = sem("lat_stat")
        lat_var = sem("lat_var")
        lat_std = sem("lat_std")
        lat_normed = sem("lat_normed")
        lat_hi = sem("lat_hi")
        latent_ready = sem("latent_ready")
        swapped = sem("swapped")
        rope_ready = sem("rope_ready")
        final_turned = sem("final_turned")
        out_copied = sem("out_copied")
        out_saved = sem("out_saved")
        act_step = sem("act_step")
        dve_step = sem("dve_step")
        pool_step = sem("pool_step")

        block = ctx.enter_context(nc.Block())

        def bank_set(g):
            return (g % 2) * 4

        def first_cols(g, nb=4):
            return ps[:, bank_set(g):bank_set(g) + nb, 0:S]

        def second_cols(g, nb=4):
            return ps[:, bank_set(g):bank_set(g) + nb, S:2 * S]

        def wide(t, n):
            return t.to_broadcast([P, n, S])

        def n_loads(u):
            if U_QR <= u < U_QR + 3:
                return LC
            return 2 if U_GW <= u < U_GW + 6 or U_IN1 + 2 * UG <= u < U_IN1 + 2 * UG + 2 or U_UQ <= u < U_QR else 1

        def landed(u):
            return 16 * sum(n_loads(v) for v in range(u % RING, u + 1, RING))

        @block.sync
        def _(sp):
            def load(u, src, turn=0):
                s = u % RING
                if u >= RING:
                    sp.wait_ge(lo_ready, u - RING + 1 + turn)
                sp.dma_start(raw[:, s, :].rearrange("p (a b) -> p a b", a=2), src).then_inc(raw_landed[s], 16)

            def load_parts(u, parts):
                s = u % RING
                assert len(parts) == n_loads(u)
                sp.wait_ge(lo_ready, u - RING + 1)
                for cols, n, src in parts:
                    if cols is None:
                        dst = raw[:, s, :].rearrange("p (c w) -> p c w", c=8)[:, :, n * ROPE:(n + 1) * ROPE]
                    else:
                        dst = raw[:, s, cols].rearrange("p (a b) -> p a b", a=n)
                    sp.dma_start(dst, src).then_inc(raw_landed[s], 16)

            def rows(w):
                return w.rearrange("(c p) n -> p c n", p=P)

            def load_groups(u0, w, cols, n_units):
                for g, c in enumerate(cols):
                    for j in range(n_units):
                        load(u0 + g * n_units + j, rows(w)[:, 2 * j:2 * j + 2, c:c + 512])

            def load_group_loop(u0, w, n_groups, n_units, stride=512):
                with sp.Fori(0, n_groups // 2) as i:
                    for g in range(2):
                        for j in range(n_units):
                            load(u0 + g * n_units + j,
                                 rows(w)[:, 2 * j:2 * j + 2, bass.ds(i * (2 * stride) + g * stride, 512)],
                                 i * (2 * n_units))

            for q in range(4):
                sp.dma_start(mem_rows[:, :, q * 512:(q + 1) * 512],
                             mem[0].rearrange("(t p) d -> p t d", p=P)[:, :, q * 512:(q + 1) * 512]) \
                    .then_inc(mem_landed[q], 16)
            load_groups(0, mem_w_kv[0], (0,), UG // 2)
            sp.dma_start(pos_i[:], positions.to_broadcast([P, S])).then_inc(pos_landed, 16)
            sp.dma_start(freq[:], inv_freq).then_inc(pos_landed, 16)
            sp.dma_start(x_rows[:], x[0].rearrange("(t p) d -> p t d", p=P)).then_inc(x_landed, 16)
            for l in range(DEPTH):
                for t in range(3):
                    sp.dma_start(conv_rows[:, l, t, :], ffn_conv_w[l, t].rearrange("(c p) -> c p", p=P)) \
                        .then_inc(params_landed, 16)
                sp.dma_start(conv_rows[:, l, 3, :], ffn_conv_b[l].rearrange("(c p) -> c p", p=P)) \
                    .then_inc(params_landed, 16)
            for k, w in enumerate((ln1_g, ln1_b, ln2_g, ln2_b)):
                sp.dma_start(ln_rows[32 * k:32 * k + 32, :], w.rearrange("l (c p) -> (l c) p", p=P)) \
                    .then_inc(params_landed, 16)
            for r0, w in ((0, pool_scale), (POOL_CHUNKS, mla_q_norm_g), (POOL_CHUNKS + LC, mla_kv_norm_g)):
                sp.dma_start(misc_rows[r0:r0 + w.shape[1] // P, :], w[0].rearrange("(c p) -> c p", p=P)) \
                    .then_inc(params_landed, 16)

            for j in range(UG // 2, UG):
                load(j, rows(mem_w_kv[0])[:, 2 * j:2 * j + 2, 0:512])
            load_groups(UG, mem_w_kv[0], (512,), UG)
            load_groups(U_IN0, pool_w_in[0], (POOL_CH, 0, 512, 1024), UG)
            load_groups(U_MEM[1], mem_w_kv[1], (0, 512), UG)
            for r in range(6):
                blocks = [divmod(2 * r + h, GC) for h in range(2)]
                load_parts(U_GW + r, [(slice(h * GC * P, (h + 1) * GC * P), GC,
                                       rows(pool_group_w[0, w])[:, :, b * P:(b + 1) * P])
                                      for h, (w, b) in enumerate(blocks)])
            sp.wait_ge(evacuated, G_MEM[1] + 2)
            sp.dma_start(kv_scratch, kv_mem[1][:].rearrange("p a b -> p (a b)")).then_inc(kv_saved, 16)
            load_group_loop(U_OUT[0], pool_w_out[0], 4, UG)

            def load_ffn(l):
                with sp.Fori(0, FG) as i:
                    for h in range(2):
                        for j in range(UG):
                            load(U_UP[l] + h * UG + j,
                                 rows(ffn_w_up[l])[:, 2 * j:2 * j + 2, bass.ds(i * 512 + h * FF, 512)], i * (2 * UG))
                load_group_loop(U_DOWN[l], ffn_w_down[l], 4, DG)

            load_ffn(0)
            o_rope = 2 * QL
            load_groups(U_IN1, mla_w_in[0], (0,), UG)
            sp.wait_ge(units_done, U_IN1)
            sp.wait_ge(kv_saved, 16)
            sp.dma_start(kv_back[:].rearrange("p a b -> p (a b)"), kv_scratch).then_inc(kv_loaded, 16)
            load_groups(U_IN1 + UG, mla_w_in[0], (QL,), UG)
            for r in range(2):
                w_rope = rows(mla_w_in[0])[:, 8 * r:8 * r + 8, o_rope:o_rope + ROPE]
                load_parts(U_IN1 + 2 * UG + r, [(None, h, w_rope) for h in range(2)])
            load_groups(U_IN1 + 2 * UG + 2, mla_w_in[0], (o_rope + ROPE,), UG)
            per_head = mla_w_uq[0].rearrange("(c p) (h w) -> p c h w", p=P, w=HEAD + ROPE)
            for g in range(3):
                for j in range(2):
                    load_parts(U_UQ + 2 * g + j, [(slice(c * 512, (c + 1) * 512), 4,
                                                   per_head[:, 2 * j + c, 4 * g:4 * g + 4, 0:HEAD]) for c in range(2)])
            for r in range(3):
                load_parts(U_QR + r, [(slice(c * 256, (c + 1) * 256), 4,
                                       per_head[:, c, 4 * r:4 * r + 4, HEAD:HEAD + ROPE]) for c in range(LC)])
            load_groups(U_UK, mla_w_uk[0], (0, 512, 1024), 2)
            load_groups(U_UV, mla_w_uv[0], (0, 512, 1024), 2)
            load_group_loop(U_OUT[1], mla_w_out[0], 4, UG)
            load_ffn(1)
            for q in range(4):
                sp.wait_ge(out_copied, 2 * (q + 1))
                sp.dma_start(out[0].rearrange("(t p) d -> p t d", p=P)[:, :, q * 512:(q + 1) * 512],
                             out_rows[:, :, q * 512:(q + 1) * 512]).then_inc(out_saved, 16)
            sp.wait_ge(out_saved, 16 * 4)

        def walk(eng, split):
            state = [0]

            def to(n):
                n = min(n, U_END)
                while state[0] < n:
                    u = state[0]
                    turns = (n - u) // RING
                    calm = all(landed(v + RING * (turns - 1)) - landed(v) == 16 * (turns - 1) for v in range(u, u + RING)) \
                        if turns > 1 else False
                    if turns > 1 and calm and u >= RING:
                        with eng.Fori(0, turns) as i:
                            for j in range(RING):
                                split(u + j, i * RING, i * 16)
                        state[0] += RING * turns
                    else:
                        split(u, 0, 0)
                        state[0] += 1

            def skip(n):
                state[0] = n

            return to, skip

        LN_AT = [(0, 0, U_OUT[0], UG, G_OUT[0], H_OUT[0]), (0, 1, U_DOWN[0], DG, G_DOWN[0], H_DOWN[0]),
                 (1, 0, U_OUT[1], UG, G_OUT[1], H_OUT[1]), (1, 1, U_DOWN[1], DG, G_DOWN[1], H_DOWN[1])]
        PIECES = [(c, 1) for c in range(4)] + [(c, 2) for c in range(4, KC, 2)]
        NP = len(PIECES)
        U_NEXT = [U_UP[0], U_IN1, U_UP[1], U_END]

        def pieces_in(j):
            return sum(c <= 2 * j + 1 for c, _ in PIECES)

        def splits_after(k, c):
            return U_NEXT[k] + min(c // 2, RING + 2 if k != 1 else KC)

        HEADS = [[("mem", h) for h in range(MEM_HEADS)],
                 [("mla", h) for h in range(MLA_HEADS)] + [("mem", h) for h in range(MEM_HEADS)]]
        HEAD0 = [0, MEM_HEADS]

        def y_chunk(l, n):
            return POOL_CHUNKS + n if l == 0 else n

        @block.scalar
        def _(act):
            step = Steps(act, act_step)

            def split(u, turn, turn16):
                s = u % RING
                act.wait_ge(raw_landed[s], landed(u) + turn16)
                if u >= RING:
                    act.wait_ge(units_done, u - RING + 1 + turn)
                act.activation(w_hi[:, s, :], raw[:, s, :], ACT.Copy).then_inc(hi_ready, 1)

            split_to, skip_to = walk(act, split)

            def half_out(e, g, dst, nb=4):
                split_to(e + RING)
                act.wait_ge(units_done, e)
                act.activation(dst, first_cols(g, nb), ACT.Copy).then_inc(halves, 1)

            for j in range(KC // 2):
                act.wait_ge(mem_turned, j + 1)
                act.activation(mem_hl[:, 2 * j:2 * j + 2, 0:S], ps[:, j, :].rearrange("p (a b) -> p a b", a=2),
                               ACT.Copy).then_inc(mem_hi, 1)
            split_to(RING)
            act.wait_ge(trig, 1)
            act.activation(sin_t[:, 0, :], angle[:], ACT.Sin).then_inc(trig_done, 1)
            act.wait_ge(trig, 2)
            act.activation(cos_t[:, 0, :], turns[:], ACT.Sin).then_inc(trig_done, 1)
            def memory_keys(l):
                half_out(U_MEM[l] + UG, G_MEM[l], kv_mem[l][:, 0, :].rearrange("p (a b) -> p a b", a=4))

            memory_keys(0)
            split_to(U_IN0 + RING)
            for j in range(KC // 2):
                act.wait_ge(x_turned, j + 1)
                bank = ps[:, j % 4, :].rearrange("p (a b) -> p a b", a=2)
                act.activation(res[:, 2 * j:2 * j + 2, :], bank, ACT.Copy)
                act.activation(xy[:, 2 * j:2 * j + 2, 0:S], bank, ACT.Copy).then_inc(x_hi, 1)

            def attention(l):
                heads, h0 = HEADS[l], HEAD0[l]
                n = len(heads)
                for s in range(n + 3):
                    if s < n:
                        scale = MEM_SCALE if heads[s][0] == "mem" else MLA_SCALE
                        act.wait_ge(neg_max, h0 + s + 1)
                        if s >= 3:
                            act.wait_ge(probs_turned, h0 + s - 2)
                        for t in range(TB):
                            ins = act.activation(probs[s % 3][:, t, :], ps[:, s % 3, t * S:(t + 1) * S], ACT.Exp,
                                                 bias=soft[:, 1, 2 * s + t:2 * s + t + 1], scale=scale,
                                                 accum_out=soft[:, 2, 2 * s + t:2 * s + t + 1])
                        ins.then_inc(exps, 1)
                    if 2 <= s < n + 2:
                        h = s - 2
                        act.wait_ge(probs_turned, h0 + h + 1)
                        if h >= 2:
                            act.wait_ge(heads_out, h0 + h - 1)
                        act.activation(probs_t[h % 2][:].rearrange("p a b -> p (a b)"), ps[:, 3 + h % 3, :],
                                       ACT.Copy).then_inc(probs_t_ready, 1)
                    if s >= 3:
                        h = s - 3
                        act.wait_ge(heads_out, h0 + h + 1)
                        act.activation(xy[:, y_chunk(l, h), 0:S], ps[:, 6 + h % 2, 0:S], ACT.Copy).then_inc(y_hi, 1)

            def layer_norm(k):
                l, which, u0, n_units, g0, _ = LN_AT[k]
                for g in range(3):
                    if g:
                        act.wait_ge(evacuated, g0 + g)
                    half_out(u0 + (g + 1) * n_units, g0 + g, first_half[k][:])
                    if g == 1:
                        act.wait_ge(stat_done, 3 * k + 1)
                        act.activation(shift[:], ps[:, bank_set(g0), 0:S], ACT.Copy, scale=1.0 / 512) \
                            .then_inc(shift_ready, 1)
                        for gg, dst in ((0, sum_dd[k]), (1, squares[k])):
                            act.wait_ge(shifted, 4 * k + gg + 1)
                            act.activation(dst[:], res[:, 4 * gg:4 * gg + 4, :], ACT.Square).then_inc(squared, 1)
                    if g == 2:
                        act.wait_ge(sq_used, 2 * k + 1)
                        act.wait_ge(evacuated, g0 + 3)
                        act.activation(squares[k][:], res[:, 8:12, :], ACT.Square).then_inc(squared, 1)
                step.wait()
                step.done(act.activation(sqrt_warm[:], eps[:], ACT.Sqrt))
                split_to(u0 + 4 * n_units + RING)
                act.wait_ge(sq_used, 2 * k + 2)
                for h in range(2):
                    act.wait_ge(shifted, 4 * k + 3 + h)
                    act.activation(squares[k][:, 2 * h:2 * h + 2, :], res[:, 12 + 2 * h:14 + 2 * h, :],
                                   ACT.Square).then_inc(squared, 1)
                act.wait_ge(var_ready, k + 1)
                act.activation(std[:], var[:], ACT.Sqrt, bias=eps[:, 0:1]).then_inc(std_ready, 1)
                for p, (c0, n) in enumerate(PIECES):
                    act.wait_ge(normed, NP * k + p + 1)
                    for c in range(c0, c0 + n):
                        ins = act.activation(res[:, c, :], res[:, c, :], ACT.Identity,
                                             scale=ln_col[:, 2 * which, l, c:c + 1],
                                             bias=ln_col[:, 2 * which + 1, l, c:c + 1])
                        if k < 3:
                            step.done(ins)
                    if k < 3:
                        step.wait()
                        act.activation(xy[:, c0:c0 + n, 0:S], res[:, c0:c0 + n, :], ACT.Copy).then_inc(x_hi, 1)
                        split_to(splits_after(k, c0))
                    else:
                        ins.then_inc(affine, 1)

            def ffn(l):
                u0 = U_UP[l]
                A = RING + 2
                split_to(u0 + A)
                act.wait_ge(pad_zero, l + 1)
                with act.Fori(0, FG) as i:
                    def ahead(a, b):
                        for j in range(a, b):
                            split(u0 + j, i * (2 * UG), i * (2 * UG // RING * 16))

                    ahead(A, UG + RING)
                    act.wait_ge(units_done, i * (2 * UG) + (u0 + UG))
                    act.activation(h_pad[:, :, 1:S + 1], first_cols(G_UP[l]), ACT.Copy).then_inc(halves, 1)
                    ahead(UG + RING, UG + A + 2)
                    act.wait_ge(conv_gate, i + (FG * l + 1))
                    act.activation(gate[:], gate[:], ACT.Silu).then_inc(silu_done, 1)
                    ahead(UG + A + 2, 2 * UG + RING)
                    act.wait_ge(units_done, i * (2 * UG) + (u0 + 2 * UG))
                    act.activation(h_pad[:, :, 1:S + 1], first_cols(G_UP[l] + 1), ACT.Copy).then_inc(halves, 1)
                    ahead(2 * UG + RING, 2 * UG + A)
                    act.wait_ge(product, i + (FG * l + 1))
                    act.activation(act_hl[:, bass.ds(i * 4, 4), 0:S], val[:], ACT.Copy).then_inc(act_hi, 1)
                skip_to(u0 + A + 2 * FG * UG)

            half_out(U_IN0 + UG, G_IN0, q_mem[0][:])
            act.wait_ge(pads_ready, 1)
            for g in range(3):
                half_out(U_IN0 + (2 + g) * UG, G_IN0 + 1 + g, u_pad[:, 4 * g:4 * g + 4, PAD:PAD + S])
            for k in range(len(WINDOWS)):
                split_to(U_MEM[1] + 2 * k + 2)
                act.wait_ge(pool_diff, k + 1)
                act.activation(pooled[:, GC * k:GC * k + GC, 0:S], u_pad[:, GC * k:GC * k + GC, PAD:PAD + S],
                               ACT.Copy).then_inc(pool_hi, 1)
            memory_keys(1)
            split_to(U_GW + RING)
            attention(0)
            for g in range(3):
                if g:
                    act.wait_ge(pool_y_ready, g)
                half_out(U_GW + 2 * (g + 1), G_GW + g, y_pool[:])
                act.wait_ge(evacuated, G_GW + g + 1)
                for b in range(4):
                    step.done(act.activation(y_pool[:, b, :], y_pool[:, b, :], ACT.Copy,
                                             scale=misc_col[:, 4 * g + b:4 * g + b + 1]))
                step.wait()
                act.activation(xy[:, 4 * g:4 * g + 4, 0:S], y_pool[:], ACT.Copy).then_inc(pool_y_hi, 1)
            layer_norm(0)
            act.wait_ge(kv_saved, 16)
            ffn(0)
            layer_norm(1)

            def latent_norm(n, e, g, gains):
                if n:
                    act.wait_ge(latent_ready, n)
                half_out(e, g, latent[:])
                act.wait_ge(evacuated, g + 1)
                act.activation(latent_sq[:], latent[:], ACT.Square).then_inc(lat_sq, 1)
                act.wait_ge(lat_var, n + 1)
                act.activation(std[:], var[:], ACT.Sqrt).then_inc(lat_std, 1)
                act.wait_ge(lat_normed, n + 1)
                for c in range(LC):
                    step.done(act.activation(latent[:, c, :], latent[:, c, :], ACT.Copy,
                                             scale=misc_col[:, gains + c:gains + c + 1]))
                step.wait()
                act.activation((qn_hl, kvn_hl)[n][:, :, 0:S], latent[:], ACT.Copy).then_inc(lat_hi, 1)

            def swap_halves(g, src, dst):
                act.wait_ge(evacuated, g + 1)
                for q in range(4):
                    r, w = 32 * (q ^ 1), 32 * q
                    ins = act.activation(dst[w:w + 32, :, :], src[r:r + 32, :, :], ACT.Copy)
                ins.then_inc(swapped, 1)

            e = U_IN1
            latent_norm(0, e + UG, G_IN1, POOL_CHUNKS)
            latent_norm(1, e + 2 * UG, G_IN1 + 1, POOL_CHUNKS + LC)
            half_out(e + 2 * UG + 2, G_IN1 + 2, k_rope[:], 1)
            swap_halves(G_IN1 + 2, k_rope, k_swap)
            half_out(U_UQ, G_IN1 + 3, q_mem[1][:])
            for g in range(3):
                half_out(U_UQ + 2 * (g + 1), G_UQ + g, q_nope[:, 4 * g:4 * g + 4, :])
            half_out(U_QR + 2, G_QR, q_rope[:, 0:4, :])
            half_out(U_QR + 3, G_QR + 1, q_rope[:, 4:6, :], 2)
            swap_halves(G_QR + 1, q_rope, q_swap)
            for g in range(3):
                half_out(U_UK + 2 * (g + 1), G_UK + g, k_nope[:, 4 * g:4 * g + 4, :])
            split_to(U_OUT[1] + RING)
            attention(1)
            layer_norm(2)
            ffn(1)
            layer_norm(3)
            for j in range(KC // 2):
                act.wait_ge(final_turned, j + 1)
                act.activation(out_rows[:, :, 2 * j * P:(2 * j + 2) * P],
                               ps[:, j, :].rearrange("p (t b) -> p t b", t=2), ACT.Copy).then_inc(out_copied, 1)

        @block.vector
        def _(dve):
            step = Steps(dve, dve_step)

            def split(u, turn, turn16):
                s = u % RING
                dve.wait_ge(hi_ready, u + 1 + turn)
                dve.tensor_tensor(w_lo[:, s, :], raw[:, s, :], w_hi[:, s, :], ALU.subtract).then_inc(lo_ready, 1)

            split_to, skip_to = walk(dve, split)

            def add_half(e, g, h, dst, nb=4):
                split_to(e + RING)
                dve.wait_ge(halves, h + 1)
                dve.tensor_tensor(dst, dst, second_cols(g, nb), ALU.add).then_inc(evacuated, 1)

            def rows_out(e, g, dst):
                split_to(e + RING)
                dve.wait_ge(units_done, e)
                b = bank_set(g)
                dve.tensor_copy(dst, ps[:, b:b + TB, :]).then_inc(evacuated, 1)

            for j in range(KC // 2):
                dve.wait_ge(mem_hi, j + 1)
                dve.tensor_tensor(mem_hl[:, 2 * j:2 * j + 2, S:2 * S], ps[:, j, :].rearrange("p (a b) -> p a b", a=2),
                                  mem_hl[:, 2 * j:2 * j + 2, 0:S], ALU.subtract).then_inc(mem_ready, 1)
            split_to(RING)

            dve.wait_ge(pos_landed, 32)
            for q in range(4):
                step.done(dve.memset(sign[32 * q:32 * q + 32, :], -1.0 if q % 2 == 0 else 1.0))
            step.done(dve.tensor_copy(turns[:], pos_i[:]))
            step.wait()
            step.done(dve.tensor_scalar(angle[:], turns[:], freq[:, 0:1], None, ALU.mult))
            step.wait()
            step.done(dve.tensor_scalar(turns[:], angle[:], 1.0 / 6.283185307179586, MAGIC, ALU.mult, ALU.add))
            step.wait()
            step.done(dve.tensor_scalar(turns[:], turns[:], MAGIC, None, ALU.subtract))
            for part in TWO_PI_PARTS:
                step.wait()
                step.done(dve.scalar_tensor_tensor(out=angle[:], in0=turns[:], scalar=-part, in1=angle[:],
                                                   op0=ALU.mult, op1=ALU.add))
            step.wait()
            step.done(dve.tensor_scalar(angle[:], angle[:], 3.1415925, -3.1415925, ALU.min, ALU.max))
            step.wait()
            step.done(dve.scalar_tensor_tensor(out=turns[:], in0=angle[:], scalar=-1.0, in1=angle[:],
                                               op0=ALU.mult, op1=ALU.max))
            step.wait()
            dve.tensor_scalar(angle[:], angle[:], sign[:, 0:1], None, ALU.mult).then_inc(trig, 1)
            dve.tensor_scalar(turns[:], turns[:], -1.0, 1.5707964, ALU.mult, ALU.add).then_inc(trig, 1)

            def heads_of(t):
                return t.rearrange("p (a b) -> p a b", a=4)

            def memory_kv(l):
                add_half(U_MEM[l] + UG, G_MEM[l], H_MEM[l], heads_of(kv_mem[l][:, 0, :]))
                rows_out(U_MEM[l] + 2 * UG, G_MEM[l] + 1, kv_mem[l][:, 1, :].rearrange("p (a b) -> p a b", a=TB))

            memory_kv(0)

            def x_lo(c, n, src):
                dve.tensor_tensor(xy[:, c:c + n, S:2 * S], src, xy[:, c:c + n, 0:S], ALU.subtract).then_inc(x_ready, 1)

            for j in range(KC // 2):
                dve.wait_ge(x_hi, j + 1)
                x_lo(2 * j, 2, ps[:, j % 4, :].rearrange("p (a b) -> p a b", a=2))
            for l in range(DEPTH):
                dve.wait_ge(params_turned, l + 1)
                dve.tensor_copy(conv_col[:, l, :, :].rearrange("p a b -> p (a b)"), ps[:, l, 0:8 * FC]) \
                    .then_inc(params_ready, 1)
            dve.wait_ge(params_turned, 3)
            dve.tensor_copy(ln_col[:].rearrange("p a b c -> p (a b c)"), ps[:, 2, 0:P]).then_inc(params_ready, 1)
            dve.tensor_copy(misc_col[:], ps[:, 2, P:P + POOL_CHUNKS + 2 * LC]).then_inc(params_ready, 1)

            def attention(l):
                heads, h0 = HEADS[l], HEAD0[l]
                n = len(heads)
                for s in range(n + 3):
                    if s < n:
                        scale = MEM_SCALE if heads[s][0] == "mem" else MLA_SCALE
                        c = slice(2 * s, 2 * s + TB)
                        dve.wait_ge(scores_ready, h0 + s + 1)
                        step.done(dve.tensor_reduce(soft[:, 0, c], ps[:, s % 3, :].rearrange("p (a b) -> p a b", a=TB),
                                                    AX_X, ALU.max))
                        step.wait()
                        dve.tensor_scalar(soft[:, 1, c], soft[:, 0, c], -scale, None, ALU.mult).then_inc(neg_max, 1)
                    if 1 <= s <= n:
                        c = slice(2 * (s - 1), 2 * (s - 1) + TB)
                        dve.wait_ge(exps, h0 + s)
                        step.done(dve.reciprocal(soft[:, 3, c], soft[:, 2, c]))
                        step.wait()
                        for t in range(TB):
                            i = 2 * (s - 1) + t
                            ins = dve.tensor_scalar(probs[(s - 1) % 3][:, t, :], probs[(s - 1) % 3][:, t, :],
                                                    soft[:, 3, i:i + 1], None, ALU.mult)
                        ins.then_inc(probs_ready, 1)
                    if s >= 3:
                        h = s - 3
                        dve.wait_ge(y_hi, h0 + h + 1)
                        y = xy[:, y_chunk(l, h), :]
                        dve.tensor_tensor(y[:, S:2 * S], ps[:, 6 + h % 2, 0:S], y[:, 0:S], ALU.subtract) \
                            .then_inc(y_ready, 1)

            def layer_norm(k):
                l, which, u0, n_units, g0, h0 = LN_AT[k]

                def chunks(g):
                    return res[:, 4 * g:4 * g + 4, :]

                alpha = dict(scalar=ALPHA, op0=ALU.mult)
                shift4 = wide(shift[:].unsqueeze(1), 4)
                for g in range(3):
                    split_to(u0 + (g + 1) * n_units + RING)
                    dve.wait_ge(halves, h0 + g + 1)
                    if g < 2:
                        step.done(dve.scalar_tensor_tensor(out=chunks(g), in0=chunks(g), in1=second_cols(g0 + g),
                                                           op1=ALU.add, **alpha))
                    else:
                        step.done(dve.tensor_tensor(chunks(g), chunks(g), second_cols(g0 + g), ALU.add))
                    step.wait()
                    dve.tensor_tensor(chunks(g), chunks(g), first_half[k][:], ALU.add).then_inc(evacuated, 1)
                    dve.wait_ge(evacuated, g0 + g + 1)
                    if g == 0:
                        step.done(dve.tensor_tensor(fold_b[:], res[:, 0:2, :], res[:, 2:4, :], ALU.add))
                        step.wait()
                        dve.tensor_tensor(fold_a[:], fold_b[:, 0, :], fold_b[:, 1, :], ALU.add).then_inc(col_sum, 1)
                    if g == 1:
                        dve.wait_ge(shift_ready, k + 1)
                        for gg in range(2):
                            dve.tensor_tensor(chunks(gg), chunks(gg), shift4, ALU.subtract).then_inc(shifted, 1)
                        for gg in (2, 3):
                            step.done(dve.scalar_tensor_tensor(out=chunks(gg), in0=chunks(gg), in1=shift4,
                                                               op1=ALU.subtract, **alpha))
                        dve.wait_ge(shifted, 4 * k + 2)
                        step.done(dve.tensor_tensor(sum_d[k][:], chunks(0), chunks(1), ALU.add))
                        step.wait()
                step.done(dve.tensor_tensor(sum_d[k][:], sum_d[k][:], chunks(2), ALU.add))
                step.wait()
                step.done(dve.tensor_tensor(fold_b[:], sum_d[k][:, 0:2, :], sum_d[k][:, 2:4, :], ALU.add))
                step.wait()
                dve.tensor_tensor(fold_a[:], fold_b[:, 0, :], fold_b[:, 1, :], ALU.add).then_inc(sums_ready, 1)
                dve.wait_ge(sums_ready, 2 * k + 1)
                dve.wait_ge(sq_used, 2 * k + 2)
                step.done(dve.tensor_tensor(fold_b[:], sum_dd[k][:, 0:2, :], sum_dd[k][:, 2:4, :], ALU.add))
                step.wait()
                dve.tensor_tensor(sum_dd[k][:, 0, :], fold_b[:, 0, :], fold_b[:, 1, :], ALU.add) \
                    .then_inc(sums_ready, 1)
                split_to(u0 + 4 * n_units + RING)
                dve.wait_ge(units_done, u0 + 4 * n_units)
                b3 = bank_set(g0 + 3)
                for h in range(2):
                    two = res[:, 12 + 2 * h:14 + 2 * h, :]
                    dve.tensor_tensor(two, two, ps[:, b3 + 2 * h:b3 + 2 * h + 2, 0:S], ALU.add).then_inc(shifted, 1)
                dve.wait_ge(shifted, 4 * k + 4)
                dve.sem_inc(evacuated, 1)
                dve.wait_ge(stat_done, 3 * k + 2)
                step.done(dve.tensor_scalar(mean[:], ps[:, bank_set(g0), 0:S], 1.0 / D, None, ALU.mult))
                step.wait()
                step.done(dve.tensor_tensor(mean_rstd[:], mean[:], mean[:], ALU.mult))
                step.wait()
                dve.wait_ge(stat_done, 3 * k + 3)
                dve.scalar_tensor_tensor(out=var[:], in0=ps[:, bank_set(g0) + 1, 0:S], scalar=1.0 / D,
                                         in1=mean_rstd[:], op0=ALU.mult, op1=ALU.subtract).then_inc(var_ready, 1)
                dve.wait_ge(std_ready, k + 1)
                step.done(dve.reciprocal(rstd[:], std[:]))
                step.wait()
                step.done(dve.tensor_tensor(mean_rstd[:], mean[:], rstd[:], ALU.mult))
                for p in range(NP + 1):
                    if p < NP:
                        c0, n = PIECES[p]
                        piece = res[:, c0:c0 + n, :]
                        step.done(dve.tensor_tensor(piece, piece, wide(rstd[:].unsqueeze(1), n), ALU.mult))
                        step.wait()
                        dve.tensor_tensor(piece, piece, wide(mean_rstd[:].unsqueeze(1), n), ALU.subtract) \
                            .then_inc(normed, 1)
                    if p >= 1 and k < 3:
                        c0, n = PIECES[p - 1]
                        dve.wait_ge(x_hi, KC // 2 + NP * k + p)
                        x_lo(c0, n, res[:, c0:c0 + n, :])
                        split_to(splits_after(k, c0))

            def ffn(l):
                u0 = U_UP[l]
                A = RING + 2
                split_to(u0 + A)
                dve.memset(h_pad[:, :, 0:1], 0.0)
                dve.memset(h_pad[:, :, S + 1:S + 2], 0.0).then_inc(pad_zero, 1)

                def convolve(dst, chunk, between=lambda: None):
                    def col(t, b):
                        return conv_col[:, l, t, bass.ds(chunk + b, 1)]

                    done = [step.done(dve.tensor_scalar(dst[:, b, :], h_pad[:, b, 1:S + 1], col(1, b), col(3, b),
                                                        ALU.mult, ALU.add)) for b in range(4)]
                    for t in (0, 2):
                        between()
                        for b in range(4):
                            step.wait(done[b])
                            done[b] = step.done(dve.scalar_tensor_tensor(
                                out=dst[:, b, :], in0=h_pad[:, b, t:t + S], scalar=col(t, b), in1=dst[:, b, :],
                                op0=ALU.mult, op1=ALU.add))

                with dve.Fori(0, FG) as i:
                    step.loop(i, 24)
                    at_ = [A]

                    def ahead(n):
                        for j in range(at_[0], n):
                            split(u0 + j, i * (2 * UG), 0)
                        at_[0] = n

                    def hidden(half):
                        g = G_UP[l] + half
                        dve.wait_ge(halves, i * 2 + (H_UP[l] + half + 1))
                        dve.tensor_tensor(h_pad[:, :, 1:S + 1], h_pad[:, :, 1:S + 1], second_cols(g), ALU.add) \
                            .then_inc(evacuated, 1)
                        dve.wait_ge(evacuated, i * 2 + (g + 1))

                    ahead(UG + RING)
                    hidden(0)
                    convolve(gate, i * 4, lambda: ahead(at_[0] + 1))
                    step.wait()
                    dve.sem_inc(conv_gate, 1)
                    ahead(2 * UG + RING)
                    hidden(1)
                    convolve(val, i * 4 + FC, lambda: ahead(at_[0] + 1))
                    assert at_[0] == 2 * UG + A
                    dve.wait_ge(silu_done, i + (FG * l + 1))
                    step.wait()
                    dve.tensor_tensor(val[:], val[:], gate[:], ALU.mult).then_inc(product, 1)
                    dve.wait_ge(act_hi, i + (FG * l + 1))
                    a = act_hl[:, bass.ds(i * 4, 4), :]
                    dve.tensor_tensor(a[:, :, S:2 * S], val[:], a[:, :, 0:S], ALU.subtract).then_inc(act_ready, 1)
                step.end_loop(FG)
                skip_to(u0 + A + 2 * FG * UG)

            add_half(U_IN0 + UG, G_IN0, H_IN0, q_mem[0][:])
            for g in range(3):
                add_half(U_IN0 + (2 + g) * UG, G_IN0 + 1 + g, H_IN0 + 1 + g, u_pad[:, 4 * g:4 * g + 4, PAD:PAD + S])
            for k in range(len(WINDOWS)):
                split_to(U_MEM[1] + 2 * k + 2)
                u = u_pad[:, GC * k:GC * k + GC, PAD:PAD + S]
                dve.wait_ge(windowed, k + 1)
                dve.tensor_tensor(u, win[(k + 1) % 2][:, :, PAD:PAD + S], u, ALU.subtract).then_inc(pool_diff, 1)
                dve.wait_ge(pool_hi, k + 1)
                p = pooled[:, GC * k:GC * k + GC, :]
                dve.tensor_tensor(p[:, :, S:2 * S], u, p[:, :, 0:S], ALU.subtract).then_inc(pooled_ready, 1)
            memory_kv(1)
            split_to(U_GW + RING)
            attention(0)
            for g in range(3):
                add_half(U_GW + 2 * (g + 1), G_GW + g, H_GW + g, y_pool[:])
                dve.wait_ge(pool_y_hi, g + 1)
                y = xy[:, 4 * g:4 * g + 4, :]
                dve.tensor_tensor(y[:, :, S:2 * S], y_pool[:], y[:, :, 0:S], ALU.subtract).then_inc(pool_y_ready, 1)
            layer_norm(0)
            ffn(0)
            layer_norm(1)

            def latent_norm(n, e, g, h):
                add_half(e, g, h, latent[:])
                dve.wait_ge(lat_sq, n + 1)
                sq = latent_sq
                step.done(dve.tensor_tensor(sq[:, 0:2, :], sq[:, 0:2, :], sq[:, 2:4, :], ALU.add))
                step.wait()
                dve.tensor_tensor(sq[:, 0, :], sq[:, 0, :], sq[:, 1, :], ALU.add).then_inc(lat_sum, 1)
                dve.wait_ge(lat_stat, n + 1)
                dve.tensor_scalar(var[:], ps[:, bank_set(g), 0:S], 1.0 / QL, RMS_EPS, ALU.mult, ALU.add) \
                    .then_inc(lat_var, 1)
                dve.wait_ge(lat_std, n + 1)
                step.done(dve.reciprocal(rstd[:], std[:]))
                step.wait()
                dve.tensor_tensor(latent[:], latent[:], wide(rstd[:].unsqueeze(1), LC), ALU.mult) \
                    .then_inc(lat_normed, 1)
                dve.wait_ge(lat_hi, n + 1)
                hl = (qn_hl, kvn_hl)[n]
                dve.tensor_tensor(hl[:, :, S:2 * S], latent[:], hl[:, :, 0:S], ALU.subtract).then_inc(latent_ready, 1)

            def rotate(n, t, swap, width):
                dve.wait_ge(swapped, n)
                step.done(dve.tensor_tensor(t[:], t[:], cos_t[:].to_broadcast([P, width, S]), ALU.mult))
                step.done(dve.tensor_tensor(swap[:], swap[:], sin_t[:].to_broadcast([P, width, S]), ALU.mult))
                step.wait()
                dve.tensor_tensor(t[:], t[:], swap[:], ALU.add).then_inc(rope_ready, 1)

            latent_norm(0, U_IN1 + UG, G_IN1, H_IN1)
            latent_norm(1, U_IN1 + 2 * UG, G_IN1 + 1, H_IN1 + 1)
            add_half(U_IN1 + 2 * UG + 2, G_IN1 + 2, H_IN1 + 2, k_rope[:], 1)
            dve.wait_ge(trig_done, 2)
            rotate(1, k_rope, k_swap, 1)
            add_half(U_UQ, G_IN1 + 3, H_IN1 + 3, q_mem[1][:])
            for g in range(3):
                add_half(U_UQ + 2 * (g + 1), G_UQ + g, H_UQ + g, q_nope[:, 4 * g:4 * g + 4, :])
            add_half(U_QR + 2, G_QR, H_QR, q_rope[:, 0:4, :])
            add_half(U_QR + 3, G_QR + 1, H_QR + 1, q_rope[:, 4:6, :], 2)
            rotate(2, q_rope, q_swap, MLA_HEADS // 2)
            for g in range(3):
                add_half(U_UK + 2 * (g + 1), G_UK + g, H_UK + g, k_nope[:, 4 * g:4 * g + 4, :])
            for g in range(3):
                rows_out(U_UV + 2 * (g + 1), G_UV + g, v_mla[:, :, 512 * g:512 * g + 512])
            attention(1)
            layer_norm(2)
            ffn(1)
            layer_norm(3)

        @block.gpsimd
        def _(pool):
            step = Steps(pool, pool_step)
            step.done(pool.memset(ident[:], 0.0))
            step.wait()
            step.done(pool.affine_select(out=ident[:], in_=ident[:], compare_op=ALU.not_equal, fill=1.0, base=0,
                                         pattern=[[-1, P]], channel_multiplier=1))
            step.wait()
            pool.memset(ones[:], 1.0).then_inc(consts_ready, 1)
            pool.memset(eps[:], LN_EPS)
            for k, w in enumerate(WINDOWS):
                h = w // 2
                pool.memset(inv_count[:, k, h:S - h + 1], 1.0 / w)
                for t in range(h):
                    pool.memset(inv_count[:, k, t:t + 1], 1.0 / (t + h))
                for t in range(S - h + 1, S):
                    pool.memset(inv_count[:, k, t:t + 1], 1.0 / (S - t + h))

            pool.wait_ge(mem_turned, KC // 2)
            pool.memset(u_pad[:, :, 0:PAD], 0.0)
            pool.memset(u_pad[:, :, PAD + S:], 0.0).then_inc(pads_ready, 1)
            pool.wait_ge(pads_ready, 1)
            for k, w in enumerate(WINDOWS):
                pool.wait_ge(evacuated, G_IN0 + 1 + (1, 2, 3, 3)[k])
                src = u_pad[:, GC * k:GC * k + GC, :]
                n = 0
                for m in range(k + 1):
                    back, ahead_ = (1, 0) if m == 0 else (2 ** (m - 1), 2 ** (m - 1))
                    reach = w // 2 - 2 ** m
                    a, b = PAD - reach, PAD + S + reach
                    dst = win[(k - m) % 2][:, :, a:b]
                    if k >= 1 and m < 2:
                        pool.wait_ge(pool_diff, k)
                    step.done(pool.tensor_tensor(dst, src[:, :, a - back:b - back],
                                                 src[:, :, a + ahead_:b + ahead_], ALU.add))
                    step.wait()
                    src = win[(k - m) % 2]
                assert src is win[0]
                pool.tensor_tensor(win[(k + 1) % 2][:, :, PAD:PAD + S], src[:, :, PAD:PAD + S],
                                   wide(inv_count[:, k:k + 1, :], GC), ALU.mult).then_inc(windowed, 1)

            for k in range(4):
                for g in range(1, 3):
                    pool.wait_ge(squared, 5 * k + g + 1)
                    if g > 1:
                        pool.wait_ge(sq_used, 2 * k + g - 1)
                    pool.tensor_tensor(sum_dd[k][:], sum_dd[k][:], squares[k][:], ALU.add).then_inc(sq_used, 1)

        @block.tensor
        def _(pe):
            def multiply(u, g, rhs, chunks, nb=4, width=512, first=False, last=False, turn=0, narrow=False):
                s, b0 = u % RING, bank_set(g)
                pe.wait_ge(lo_ready, u + 1 + turn)
                for c in range(chunks):
                    x_hl = rhs(c)
                    end = last and c == chunks - 1
                    for b in range(nb):
                        at_ = c * width + b * P
                        hi, lo = w_hi[:, s, at_:at_ + P], w_lo[:, s, at_:at_ + P]
                        bank = ps[:, b0 + b, :]
                        if narrow:
                            pe.matmul(bank[:, 0:S], hi, x_hl[:, 0:S], start=first and c == 0, stop=False)
                            pe.matmul(bank[:, 0:S], hi, x_hl[:, S:2 * S], start=False, stop=False)
                            ins = pe.matmul(bank[:, 0:S], lo, x_hl[:, 0:S], start=False, stop=end)
                        elif end:
                            pe.matmul(bank[:, S:2 * S], lo, x_hl[:, 0:S], start=False, stop=False)
                            ins = pe.matmul(bank, hi, x_hl, start=False, stop=True)
                        else:
                            pe.matmul(bank, hi, x_hl, start=first and c == 0, stop=False)
                            ins = pe.matmul(bank[:, S:2 * S], lo, x_hl[:, 0:S], start=False, stop=False)
                ins.then_inc(units_done, 1)

            def multiply_rows(u, g, lhs, chunks, first=False, last=False):
                s, b0 = u % RING, bank_set(g)
                pe.wait_ge(lo_ready, u + 1)
                for c in range(chunks):
                    x_hl = lhs(c)
                    hi, lo = w_hi[:, s, c * 512:(c + 1) * 512], w_lo[:, s, c * 512:(c + 1) * 512]
                    for t in range(TB):
                        x_hi_, x_lo_ = x_hl[:, t * P:(t + 1) * P], x_hl[:, S + t * P:S + (t + 1) * P]
                        end = last and c == chunks - 1
                        pe.matmul(ps[:, b0 + t, :], x_hi_, hi, start=first and c == 0, stop=False)
                        pe.matmul(ps[:, b0 + t, :], x_lo_, hi, start=False, stop=False)
                        ins = pe.matmul(ps[:, b0 + t, :], x_hi_, lo, start=False, stop=end)
                ins.then_inc(units_done, 1)

            def banks_free(g, turn=0):
                pe.wait_ge(evacuated, g - 1 + turn)

            def xy_chunk(j):
                return lambda c: xy[:, 2 * j + c, :]

            def column_sums(bank, src):
                return pe.matmul(ps[:, bank, 0:S], ones[:], src, start=True, stop=True)

            pe.wait_ge(consts_ready, 1)
            for j in range(KC // 2):
                pe.wait_ge(mem_landed[j // 2], 16)
                for c in range(2):
                    for t in range(TB):
                        ins = pe.transpose(ps[:, j, c * S + t * P:c * S + (t + 1) * P],
                                           mem_rows[:, t, (2 * j + c) * P:(2 * j + c + 1) * P], ident[:])
                ins.then_inc(mem_turned, 1)
            def memory_kv(l):
                for kind in range(2):
                    g = G_MEM[l] + kind
                    if l == 0:
                        pe.wait_ge(mem_ready, 4 * (kind + 1))
                    else:
                        banks_free(g)
                    for j in range(UG):
                        pe.wait_ge(mem_ready, j + 1)
                        (multiply, multiply_rows)[kind](U_MEM[l] + kind * UG + j, g, lambda c: mem_hl[:, 2 * j + c, :],
                                                        2, first=j == 0, last=j == UG - 1)

            memory_kv(0)

            pe.wait_ge(evacuated, 1)
            pe.wait_ge(x_landed, 16)
            for j in range(KC // 2):
                if j >= 4:
                    pe.wait_ge(x_ready, j - 3)
                for c in range(2):
                    for t in range(TB):
                        ins = pe.transpose(ps[:, j % 4, c * S + t * P:c * S + (t + 1) * P],
                                           x_rows[:, t, (2 * j + c) * P:(2 * j + c + 1) * P], ident[:])
                ins.then_inc(x_turned, 1)
            pe.wait_ge(params_landed, 16 * (4 * DEPTH + 7))
            for l in range(DEPTH):
                pe.wait_ge(x_ready, 5 + l)
                for t in range(4):
                    ins = pe.transpose(ps[:, l, t * 2 * FC:(t + 1) * 2 * FC], conv_rows[:, l, t, :],
                                       ident[0:2 * FC, 0:2 * FC])
                ins.then_inc(params_turned, 1)
            pe.wait_ge(x_ready, 7)
            n_misc = POOL_CHUNKS + 2 * LC
            pe.transpose(ps[:, 2, 0:P], ln_rows[:], ident[:])
            pe.transpose(ps[:, 2, P:P + n_misc], misc_rows[:], ident[0:n_misc, 0:n_misc]).then_inc(params_turned, 1)

            def attention(l):
                heads, h0 = HEADS[l], HEAD0[l]
                n = len(heads)
                kv = (kv_mem[0], kv_back)[l]
                for s in range(n + 3):
                    if s < n:
                        kind, h = heads[s]
                        if s >= 3:
                            pe.wait_ge(exps, h0 + s - 2)
                        q = q_mem[l][:, h, :] if kind == "mem" else q_nope[:, h, :]
                        k = kv[:, 0, h * S:(h + 1) * S] if kind == "mem" else k_nope[:, h, :]
                        for t in range(TB):
                            bank = ps[:, s % 3, t * S:(t + 1) * S]
                            rot = kind == "mla"
                            ins = pe.matmul(bank, q[:, t * P:(t + 1) * P], k, start=True, stop=not rot)
                            if rot:
                                r = ROPE * (h % 2)
                                ins = pe.matmul(bank, q_rope[r:r + ROPE, h // 2, t * P:(t + 1) * P],
                                                k_rope[r:r + ROPE, 0, :], start=False, stop=True)
                        ins.then_inc(scores_ready, 1)
                    if 2 <= s < n + 2:
                        h = s - 2
                        pe.wait_ge(probs_ready, h0 + h + 1)
                        if h >= 3:
                            pe.wait_ge(probs_t_ready, h0 + h - 2)
                        for m in range(TB):
                            for t in range(TB):
                                ins = pe.transpose(ps[:, 3 + h % 3, m * S + t * P:m * S + (t + 1) * P],
                                                   probs[h % 3][:, t, m * P:(m + 1) * P], ident[:])
                        ins.then_inc(probs_turned, 1)
                    if s >= 3:
                        n_, (kind, h) = s - 3, heads[s - 3]
                        pe.wait_ge(probs_t_ready, h0 + n_ + 1)
                        if n_ >= 2:
                            pe.wait_ge(y_ready, h0 + n_ - 1)
                        for m in range(TB):
                            v = kv[:, 1, m * 512 + h * HEAD:m * 512 + (h + 1) * HEAD] if kind == "mem" \
                                else v_mla[:, m, h * HEAD:(h + 1) * HEAD]
                            ins = pe.matmul(ps[:, 6 + n_ % 2, 0:S], v, probs_t[n_ % 2][:, m, :],
                                            start=m == 0, stop=m == TB - 1)
                        ins.then_inc(heads_out, 1)

            def early_sums(k):
                b = bank_set(LN_AT[k][4])
                pe.wait_ge(sums_ready, 2 * k + 2)
                pe.matmul(ps[:, b, 0:S], ones[:], fold_a[:], start=True, stop=False)
                pe.matmul(ps[:, b + 1, 0:S], ones[:], sum_dd[k][:, 0, :], start=True, stop=False)

            def last_sums(k):
                b = bank_set(LN_AT[k][4])
                for c in range(4):
                    pe.wait_ge(shifted, 4 * k + 3 + c // 2)
                    ins = pe.matmul(ps[:, b, 0:S], ones[:], res[:, 12 + c, :], start=False, stop=c == 3)
                ins.then_inc(stat_done, 1)
                for c in range(4):
                    pe.wait_ge(squared, 5 * k + 4 + c // 2)
                    ins = pe.matmul(ps[:, b + 1, 0:S], ones[:], squares[k][:, c, :], start=False, stop=c == 3)
                ins.then_inc(stat_done, 1)

            def mix_out(l):
                k = 2 * l
                for g in range(4):
                    gg = G_OUT[l] + g
                    if g >= 2 or l == 1:
                        banks_free(gg)
                    for j in range(UG):
                        if g == 0 and l == 0 and j < POOL_CHUNKS // 2:
                            pe.wait_ge(pool_y_ready, j // 2 + 1)
                        if g == 1 and j == 4:
                            pe.wait_ge(col_sum, k + 1)
                            column_sums(bank_set(G_OUT[l]), fold_a[:]).then_inc(stat_done, 1)
                        if g == 2 and j == 0:
                            pe.wait_ge(shift_ready, k + 1)
                        if g == 3 and j == 4:
                            early_sums(k)
                        multiply(U_OUT[l] + g * UG + j, gg, xy_chunk(j), 2, first=j == 0, last=j == UG - 1,
                                 narrow=g == 3)
                last_sums(k)

            def ffn(l):
                k = 2 * l + 1
                with pe.Fori(0, FG) as i:
                    for h in range(2):
                        g = G_UP[l] + h
                        banks_free(g, i * 2)
                        if h == 0:
                            pe.wait_ge(var_ready, 2 * l + 1)
                        for j in range(UG):
                            if h == 0:
                                pe.wait_ge(x_ready, KC // 2 + NP * 2 * l + pieces_in(j))
                            multiply(U_UP[l] + h * UG + j, g, xy_chunk(j), 2, first=j == 0, last=j == UG - 1,
                                     turn=i * (2 * UG))
                flat = act_hl[:].rearrange("p a b -> p (a b)")
                loops = (DG - 6) // RING
                for g in range(4):
                    gg, u = G_DOWN[l] + g, U_DOWN[l] + g * DG
                    banks_free(gg)
                    if g == 2:
                        pe.wait_ge(shift_ready, k + 1)
                    for j in range(2):
                        pe.wait_ge(act_ready, FG * l + 1)
                        multiply(u + j, gg, lambda c: act_hl[:, 2 * j + c, :], 2, first=j == 0, narrow=g == 3)
                    pe.wait_ge(act_ready, FG * l + FG - 2)
                    with pe.Fori(0, loops) as i:
                        for j in range(RING):
                            multiply(u + 2 + j, gg,
                                     lambda c: flat[:, bass.ds(i * (2 * RING * 2 * S) + (4 + 2 * j + c) * 2 * S, 2 * S)],
                                     2, turn=i * RING, narrow=g == 3)
                    if g == 1:
                        pe.wait_ge(col_sum, k + 1)
                        column_sums(bank_set(G_DOWN[l]), fold_a[:]).then_inc(stat_done, 1)
                    if g == 3:
                        early_sums(k)
                    pe.wait_ge(act_ready, FG * l + FG)
                    for j in range(DG - RING, DG):
                        multiply(u + j, gg, lambda c: act_hl[:, 2 * j + c, :], 2, last=j == DG - 1,
                                 narrow=g == 3)
                last_sums(k)

            pe.wait_ge(params_ready, 4)
            for g in range(4):
                banks_free(G_IN0 + g)
                for j in range(UG):
                    if g == 0:
                        pe.wait_ge(x_ready, j + 1)
                        if j == 0:
                            pe.wait_ge(x_ready, 8)
                    multiply(U_IN0 + g * UG + j, G_IN0 + g, xy_chunk(j), 2, first=j == 0, last=j == UG - 1)
            memory_kv(1)
            pe.wait_ge(evacuated, G_GW)
            attention(0)
            pe.wait_ge(y_ready, HEAD0[1])
            for r in range(6):
                u, g = U_GW + r, G_GW + r // 2
                s = u % RING
                if r % 2 == 0 and r >= 4:
                    banks_free(g)
                pe.wait_ge(lo_ready, u + 1)
                for h in range(2):
                    w, b = divmod(2 * r + h, GC)
                    pe.wait_ge(pooled_ready, w + 1)
                    bank = ps[:, bank_set(g) + 2 * (r % 2) + h, :]
                    for c in range(GC):
                        at_ = (h * GC + c) * P
                        pc = pooled[:, GC * w + c, :]
                        hi, lo = w_hi[:, s, at_:at_ + P], w_lo[:, s, at_:at_ + P]
                        if c == GC - 1:
                            pe.matmul(bank[:, S:2 * S], lo, pc[:, 0:S], start=False, stop=False)
                            ins = pe.matmul(bank, hi, pc, start=False, stop=True)
                        else:
                            pe.matmul(bank, hi, pc, start=c == 0, stop=False)
                            pe.matmul(bank[:, S:2 * S], lo, pc[:, 0:S], start=False, stop=False)
                ins.then_inc(units_done, 1)
            banks_free(G_OUT[0])
            banks_free(G_OUT[0] + 1)
            mix_out(0)
            ffn(0)

            g = G_IN1
            pe.wait_ge(var_ready, 2)
            for n in range(2):
                banks_free(g + n)
                for j in range(UG):
                    if n == 1 and j == 4:
                        pe.wait_ge(lat_sum, 1)
                        column_sums(bank_set(g), latent_sq[:, 0, :]).then_inc(lat_stat, 1)
                    pe.wait_ge(x_ready, KC // 2 + NP + pieces_in(j))
                    multiply(U_IN1 + n * UG + j, g + n, xy_chunk(j), 2, first=j == 0, last=j == UG - 1)
            pe.wait_ge(lat_var, 1)
            banks_free(g + 2)
            for r in range(2):
                multiply(U_IN1 + 2 * UG + r, g + 2, lambda c: xy[:, 8 * r + c, :], 8, nb=1, width=P,
                         first=r == 0, last=r == 1)
            pe.wait_ge(lat_sum, 2)
            column_sums(bank_set(g + 1), latent_sq[:, 0, :]).then_inc(lat_stat, 1)
            pe.wait_ge(lat_var, 2)
            banks_free(g + 3)
            for j in range(UG):
                multiply(U_IN1 + 2 * UG + 2 + j, g + 3, xy_chunk(j), 2, first=j == 0, last=j == UG - 1)
            pe.wait_ge(latent_ready, 1)
            for n in range(3):
                banks_free(G_UQ + n)
                for j in range(2):
                    multiply(U_UQ + 2 * n + j, G_UQ + n, lambda c: qn_hl[:, 2 * j + c, :], 2, first=j == 0, last=j == 1)
            for r in range(3):
                gg = G_QR + r // 2
                if r != 1:
                    banks_free(gg)
                s, b0 = (U_QR + r) % RING, bank_set(gg) + 2 * (r % 2)
                pe.wait_ge(lo_ready, U_QR + r + 1)
                for b in range(2):
                    for c in range(LC):
                        at_ = c * 256 + b * P
                        hi, lo = w_hi[:, s, at_:at_ + P], w_lo[:, s, at_:at_ + P]
                        bank, xc = ps[:, b0 + b, :], qn_hl[:, c, :]
                        if c == LC - 1:
                            pe.matmul(bank[:, S:2 * S], lo, xc[:, 0:S], start=False, stop=False)
                            ins = pe.matmul(bank, hi, xc, start=False, stop=True)
                        else:
                            pe.matmul(bank, hi, xc, start=c == 0, stop=False)
                            pe.matmul(bank[:, S:2 * S], lo, xc[:, 0:S], start=False, stop=False)
                ins.then_inc(units_done, 1)
            pe.wait_ge(latent_ready, 2)
            for n in range(3):
                banks_free(G_UK + n)
                for j in range(2):
                    multiply(U_UK + 2 * n + j, G_UK + n, lambda c: kvn_hl[:, 2 * j + c, :], 2, first=j == 0, last=j == 1)
            for n in range(3):
                banks_free(G_UV + n)
                for j in range(2):
                    multiply_rows(U_UV + 2 * n + j, G_UV + n, lambda c: kvn_hl[:, 2 * j + c, :], 2,
                                  first=j == 0, last=j == 1)
            pe.wait_ge(evacuated, G_OUT[1])
            pe.wait_ge(rope_ready, 2)
            pe.wait_ge(kv_loaded, 16)
            attention(1)
            pe.wait_ge(y_ready, HEAD0[1] + len(HEADS[1]))
            mix_out(1)
            ffn(1)
            pe.wait_ge(var_ready, 4)
            pe.wait_ge(evacuated, G_DOWN[1] + 4)
            for j in range(KC // 2):
                pe.wait_ge(affine, pieces_in(j))
                for t in range(TB):
                    for c in range(2):
                        ins = pe.transpose(ps[:, j, t * 2 * P + c * P:t * 2 * P + (c + 1) * P],
                                           res[:, 2 * j + c, t * P:(t + 1) * P], ident[:])
                ins.then_inc(final_turned, 1)


LN_EPS = 1e-5
RMS_EPS = 1e-6
_INS = ["x", "mem", "positions", "pool_w_in", "pool_group_w", "pool_scale", "pool_w_out", "mla_w_in", "mla_q_norm_g",
        "mla_kv_norm_g", "mla_w_uq", "mla_w_uk", "mla_w_uv", "mla_w_out", "mem_w_kv", "ln1_g", "ln1_b", "ln2_g",
        "ln2_b", "ffn_w_up", "ffn_conv_w", "ffn_conv_b", "ffn_w_down"]


def kernel(**inputs):
    import numpy as _np
    import concourse.bacc as _bacc
    from concourse import mybir as _mybir
    from concourse.bass_utils import run_bass_kernel_spmd as _run

    nc = _bacc.Bacc("TRN2", target_bir_lowering=False, num_devices=1)
    arrays, args = {}, []
    for name in _INS:
        a = _np.ascontiguousarray(inputs[name])
        arrays[f"in_{name}_dram"] = a
        args.append(nc.dram_tensor(f"in_{name}_dram", a.shape, _mybir.dt.from_np(a.dtype), kind="ExternalInput").ap())
    half = ROPE // 2
    freqs = _np.float32(10000.0) ** (-_np.arange(0, ROPE, 2, dtype=_np.float32) / _np.float32(ROPE))
    arrays["rotary_freq"] = _np.ascontiguousarray(_np.tile(freqs, P // half).reshape(P, 1).astype(_np.float32))
    args.append(nc.dram_tensor("rotary_freq", (P, 1), _mybir.dt.float32, kind="ExternalInput").ap())
    shape = inputs["x"].shape
    args.append(nc.dram_tensor("out_0_dram", shape, _mybir.dt.float32, kind="ExternalOutput").ap())
    encoder_trunk(nc, *args)
    r = _run(nc, [arrays], core_ids=[0])
    return r.results[0]["out_0_dram"]
```

```python
from contextlib import ExitStack

import concourse.bass as bass
from concourse import mybir

P = 128
F32 = mybir.dt.float32
F32R = mybir.dt.float32r
I32 = mybir.dt.int32
ALU = mybir.AluOpType
ACT = mybir.ActivationFunctionType
AX_X = mybir.AxisListType.X

RING = 4
UNIT = 1024
BANK = 512
HEAD = 128
ROPE = 64
WINDOWS = (2, 4, 8, 16)
PAD = 8
MAGIC = 1.5 * 2.0 ** 23
TWO_PI_PARTS = (6.28125, 1.9350051879882812e-03, 3.0199159819e-07)


class Steps:

    def __init__(self, engine, sem):
        self.engine, self.sem, self.n, self.turn = engine, sem, 0, 0

    def done(self, instruction):
        instruction.then_inc(self.sem, 1)
        self.n += 1
        return self.n

    def wait(self, n=None):
        self.engine.wait_ge(self.sem, (self.n if n is None else n) + self.turn)

    def loop(self, i, per_turn):
        self.first, self.per_turn = self.n, per_turn
        self.turn = i * per_turn

    def end_loop(self, turns):
        assert self.n - self.first == self.per_turn, (self.n - self.first, self.per_turn)
        self.turn = 0
        self.n = self.first + self.per_turn * turns


def encoder_trunk(nc, x, mem, positions, pool_w_in, pool_group_w, pool_scale, pool_w_out, mla_w_in,
                  mla_q_norm_g, mla_kv_norm_g, mla_w_uq, mla_w_uk, mla_w_uv, mla_w_out, mem_w_kv,
                  ln1_g, ln1_b, ln2_g, ln2_b, ffn_w_up, ffn_conv_w, ffn_conv_b, ffn_w_down, inv_freq, out):
    _, S, D = x.shape
    DEPTH = ffn_w_up.shape[0]
    FF = ffn_w_down.shape[1]
    KC = D // P
    FC = FF // P
    TB = S // P
    MEM_HEADS = mem_w_kv.shape[2] // (2 * HEAD)
    MLA_HEADS = mla_w_uk.shape[2] // HEAD
    QL = mla_w_uq.shape[1]
    LC = QL // P
    POOL_CH = D - MEM_HEADS * HEAD
    POOL_CHUNKS = POOL_CH // P
    GC = POOL_CHUNKS // len(WINDOWS)
    ALPHA = (2 * DEPTH) ** 0.25
    MEM_SCALE = HEAD ** -0.5
    MLA_SCALE = (HEAD + ROPE) ** -0.5
    assert (S, D, DEPTH, FC, MEM_HEADS, MLA_HEADS, LC) == (256, 2048, 2, 44, 4, 12, 4)

    UG = KC // 2
    DG = FC // 2
    FG = FC // 4
    U_IN0 = 2 * UG
    U_K = [0, U_IN0 + 4 * UG]
    U_GW = U_K[1] + UG
    U_OUT = [U_GW + 6, 0]
    U_V = [UG, U_OUT[0] + 4 * UG]
    U_UP = [U_V[1] + UG, 0]
    U_DOWN = [U_UP[0] + 2 * FG * UG, 0]
    U_IN1 = U_DOWN[0] + 4 * DG
    U_UQ = U_IN1 + 3 * UG + 2
    U_QR = U_UQ + 6
    U_UK = U_QR + 3
    U_UV = U_UK + 6
    U_OUT[1] = U_UV + 6
    U_UP[1] = U_OUT[1] + 4 * UG
    U_DOWN[1] = U_UP[1] + 2 * FG * UG
    U_END = U_DOWN[1] + 4 * DG
    G_IN0, G_GW, G_OUT0 = 2, 7, 10
    G_K, G_V = [0, 6], [1, G_OUT0 + 4]
    G_UP0 = G_V[1] + 1
    G_DOWN0 = G_UP0 + 2 * FG
    G_IN1 = G_DOWN0 + 4
    G_UQ = G_IN1 + 4
    G_QR = G_UQ + 3
    G_UK = G_QR + 2
    G_UV = G_UK + 3
    G_OUT1 = G_UV + 3
    G_OUT = [G_OUT0, G_OUT1]
    G_UP = [G_UP0, G_OUT1 + 4]
    G_DOWN = [G_DOWN0, G_OUT1 + 4 + 2 * FG]
    H_K, H_IN0 = [0, 5], 1
    H_GW = H_K[1] + 1
    H_OUT = [H_GW + 3, 0]
    H_UP = [H_OUT[0] + 3, 0]
    H_DOWN = [H_UP[0] + 2 * FG, 0]
    H_IN1 = H_DOWN[0] + 3
    H_UQ = H_IN1 + 4
    H_QR = H_UQ + 3
    H_UK = H_QR + 2
    H_OUT[1] = H_UK + 3
    H_UP[1] = H_OUT[1] + 3
    H_DOWN[1] = H_UP[1] + 2 * FG

    kv_scratch = nc.dram_tensor("kv_scratch", (P, 8 * S), F32, kind="Internal").ap()

    with ExitStack() as ctx:
        def sb(name, shape, dt=F32):
            return ctx.enter_context(nc.sbuf_tensor(name, shape, dt))

        def sem(name):
            return ctx.enter_context(nc.semaphore(name))

        raw = sb("raw", [P, RING, UNIT])
        w_hi = sb("w_hi", [P, RING, UNIT], F32R)
        w_lo = sb("w_lo", [P, RING, UNIT], F32R)
        res = sb("res", [P, KC, S])
        KB = 1024

        base0 = nc.sbuf_base
        sb("xy_region", [P, KC * 2 * S])
        sb("act_region", [P, FC * 2 * S])
        sb("tmp_region", [P, 3088])
        XY = base0
        AR = XY + KC * 2 * S * 4
        TR = AR + FC * 2 * S * 4
        assert nc.sbuf_base == TR + 3088 * 4, (nc.sbuf_base, TR)

        def at(name, shape, offset, dt=F32):
            return nc.alloc_sbuf_tensor_at(name, shape, dt, offset=offset)

        xy = at("xy", [P, KC, 2 * S], XY, F32R)
        act_hl = at("act_hl", [P, FC, 2 * S], AR, F32R)
        first_half = [at(f"first_half{k}", [P, 4, S], o) for k, o in ((0, AR + 32 * KB), (1, XY), (2, AR), (3, XY))]
        squares = [at(f"squares{k}", [P, 4, S], o + 4 * KB) for k, o in ((0, AR + 32 * KB), (1, XY), (2, AR), (3, XY))]
        sum_d = [at(f"sum_d{k}", [P, 4, S], o + 8 * KB) for k, o in ((0, AR + 32 * KB), (1, XY), (2, AR), (3, XY))]
        sum_dd = [at(f"sum_dd{k}", [P, 4, S], o + 12 * KB) for k, o in ((0, AR + 32 * KB), (1, XY), (2, AR), (3, XY))]
        mem_hl = at("mem_hl", [P, KC, 2 * S], AR, F32R)
        mem_rows = at("mem_rows", [P, TB, D], AR + 32 * KB)
        kv_mem = [at(f"kv_mem{l}", [P, 2, 4 * S], o) for l, o in ((0, AR + 49 * KB), (1, AR + 57 * KB))]
        x_rows = at("x_rows", [P, TB, D], AR + 65 * KB)
        conv_rows = at("conv_rows", [FC * 2, DEPTH, 4, P], AR + 81 * KB)
        ln_rows = at("ln_rows", [P, P], AR + 85 * KB)
        misc_rows = at("misc_rows", [POOL_CHUNKS + 2 * LC, P], AR + 85 * KB + 512)
        pos_i = at("pos_i", [P, S], AR + 86 * KB, I32)
        angle = at("angle", [P, S], AR + 87 * KB)
        turns = at("turns", [P, S], TR + 8 * KB)
        q_mem = [at("q_mem0", [P, 4, S], AR + 32 * KB + 13056), at("q_mem1", [P, 4, S], AR + 74 * KB)]
        u_pad = at("u_pad", [P, POOL_CHUNKS, S + 2 * PAD], AR + 32 * KB)
        win = [at(f"win{k}", [P, GC, S + 2 * PAD], TR + KB + 3264 * k) for k in range(2)]
        y_pool = [at(f"y_pool{k}", [P, 4, S], AR + (32 + 4 * k) * KB) for k in range(2)]
        pooled = at("pooled", [P, POOL_CHUNKS, 2 * S], AR + 65 * KB, F32R)
        qn_hl = at("qn_hl", [P, LC, 2 * S], AR, F32R)
        kvn_hl = at("kvn_hl", [P, LC, 2 * S], AR + 8 * KB, F32R)
        latent = at("latent", [P, LC, S], AR + 16 * KB)
        latent_sq = at("latent_sq", [P, LC, S], AR + 20 * KB)
        k_rope = at("k_rope", [P, 1, S], AR + 24 * KB)
        k_swap = at("k_swap", [P, 1, S], AR + 25 * KB)
        q_rope = at("q_rope", [P, MLA_HEADS // 2, S], AR + 26 * KB)
        q_swap = at("q_swap", [P, MLA_HEADS // 2, S], AR + 32 * KB)
        q_nope = at("q_nope", [P, MLA_HEADS, S], AR + 38 * KB)
        k_nope = at("k_nope", [P, MLA_HEADS, S], AR + 50 * KB)
        v_mla = at("v_mla", [P, TB, MLA_HEADS * HEAD], AR + 62 * KB)
        kv_back = at("kv_back", [P, 2, 4 * S], AR + 78 * KB)
        out_rows = at("out_rows", [P, TB, D], AR)
        h_pad = at("h_pad", [P, 4, S + 2], TR)
        gate = at("gate", [P, 4, S], TR + 4128)
        val = at("val", [P, 4, S], TR + 4128 + 4 * KB)
        probs, probs_t = [[[at(f"{name}{l}{k}", [P, TB, S], o + 2 * KB * (first + k)) for k in range(n)]
                           for l, o in ((0, XY), (1, TR + KB))] for name, first, n in (("probs", 0, 3), ("probs_t", 3, 2))]
        soft = at("soft", [P, 4, 2 * 16], TR + 11 * KB)
        shift, mean, var, std, rstd, mean_sq, fold_a = [at(n, [P, S], TR + KB * k) for k, n in enumerate(
            ["shift", "mean", "var", "std", "rstd", "mean_sq", "fold_a"])]
        fold_b = at("fold_b", [P, 2, S], TR + 7 * KB)
        conv_col = sb("conv_col", [P, DEPTH, 4, 2 * FC])
        ln_col = sb("ln_col", [P, 4, DEPTH, KC])
        misc_col = sb("misc_col", [P, POOL_CHUNKS + 2 * LC])
        ident = sb("ident", [P, P])
        ones = sb("ones", [P, P])
        cos_t = sb("cos_t", [P, 1, S])
        sin_t = sb("sin_t", [P, 1, S])
        sign = sb("sign", [P, 1])
        freq = sb("freq", [P, 1])
        eps = sb("eps", [P, 1])
        inv_count = sb("inv_count", [P, len(WINDOWS), S])
        sqrt_warm = sb("sqrt_warm", [P, 1])
        silu_warm = sb("silu_warm", [P, 1])

        ps = ctx.enter_context(nc.psum_tensor("ps", [P, 8, BANK], F32))

        raw_landed = [sem(f"raw_landed{s}") for s in range(RING)]
        hi_ready = sem("hi_ready")
        lo_ready = sem("lo_ready")
        units_done = sem("units_done")
        halves = sem("halves")
        evacuated = sem("evacuated")
        mem_landed = [sem(f"mem_landed{q}") for q in range(4)]
        x_landed = sem("x_landed")
        params_landed = sem("params_landed")
        pos_landed = sem("pos_landed")
        consts_ready = sem("consts_ready")
        mem_turned = sem("mem_turned")
        mem_hi = sem("mem_hi")
        mem_ready = sem("mem_ready")
        x_turned = sem("x_turned")
        x_hi = sem("x_hi")
        x_ready = sem("x_ready")
        params_turned = sem("params_turned")
        params_ready = sem("params_ready")
        trig = sem("trig")
        trig_done = sem("trig_done")
        kv_saved = sem("kv_saved")
        kv_loaded = sem("kv_loaded")
        pads_ready = sem("pads_ready")
        windowed = sem("windowed")
        pool_diff = sem("pool_diff")
        pool_hi = sem("pool_hi")
        pooled_ready = sem("pooled_ready")
        pool_y_hi = sem("pool_y_hi")
        pool_y_ready = sem("pool_y_ready")
        scores_ready = sem("scores_ready")
        neg_max = sem("neg_max")
        exps = sem("exps")
        probs_ready = sem("probs_ready")
        probs_turned = sem("probs_turned")
        probs_t_ready = sem("probs_t_ready")
        heads_out = sem("heads_out")
        y_hi = sem("y_hi")
        y_ready = sem("y_ready")
        col_sum = sem("col_sum")
        stat_done = sem("stat_done")
        shift_ready = sem("shift_ready")
        shifted = sem("shifted")
        tail_sum = sem("tail_sum")
        squared = sem("squared")
        sums_ready = sem("sums_ready")
        var_ready = sem("var_ready")
        std_ready = sem("std_ready")
        normed = sem("normed")
        mean_ready = sem("mean_ready")
        centred = sem("centred")
        affine = sem("affine")
        conv_gate = sem("conv_gate")
        silu_done = sem("silu_done")
        product = sem("product")
        act_hi = sem("act_hi")
        act_ready = sem("act_ready")
        pad_zero = sem("pad_zero")
        sq_used = sem("sq_used")
        lat_sq = sem("lat_sq")
        lat_sum = sem("lat_sum")
        lat_stat = sem("lat_stat")
        lat_var = sem("lat_var")
        lat_std = sem("lat_std")
        lat_normed = sem("lat_normed")
        lat_hi = sem("lat_hi")
        latent_ready = sem("latent_ready")
        swapped = sem("swapped")
        rope_ready = sem("rope_ready")
        final_turned = sem("final_turned")
        out_copied = sem("out_copied")
        out_saved = sem("out_saved")
        act_step = sem("act_step")
        dve_step = sem("dve_step")
        pool_step = sem("pool_step")

        block = ctx.enter_context(nc.Block())

        def bank_set(g):
            return (g % 2) * 4

        def first_cols(g, nb=4):
            return ps[:, bank_set(g):bank_set(g) + nb, 0:S]

        def second_cols(g, nb=4):
            return ps[:, bank_set(g):bank_set(g) + nb, S:2 * S]

        def stat_banks(k):
            b = bank_set(LN_AT[k][4]) + 2
            return b, b + 1

        def head_bank(l, kind, n):
            banks = ((4, 5, 6, 7, 0, 1, 2, 3), (2, 3, 0, 1, 4, 5, 6, 7))[l]
            return banks[{"scores": n % 3, "turned": 3 + n % 3, "out": 6 + n % 2}[kind]]

        def wide(t, n):
            return t.to_broadcast([P, n, S])

        LN_AT = [(0, 0, U_OUT[0], UG, G_OUT[0], H_OUT[0]), (0, 1, U_DOWN[0], DG, G_DOWN[0], H_DOWN[0]),
                 (1, 0, U_OUT[1], UG, G_OUT[1], H_OUT[1]), (1, 1, U_DOWN[1], DG, G_DOWN[1], H_DOWN[1])]
        OUT_TURN = POOL_CHUNKS // 2
        SINGLES = 4
        PIECES = [(c, 1) for c in range(SINGLES)] + [(c, 2) for c in range(SINGLES, KC, 2)]
        NP = len(PIECES)
        EARLY = 2
        U_NEXT = [U_V[1], U_IN1, U_UP[1], U_END]

        def pieces_in(j):
            return sum(c <= 2 * j + 1 for c, _ in PIECES)

        def splits_after(k, p):
            if k == 0:
                return min(U_NEXT[0] + RING + 2 + p, U_UP[0] + RING + 2)
            first_left = RING if p > 1 else RING - 1
            return U_NEXT[k] + max(first_left, min(PIECES[p][0] // 2, RING + 2 if k != 1 else KC))

        HEADS = [[("mem", h) for h in range(MEM_HEADS)],
                 [("mem", h) for h in range(MEM_HEADS)] + [("mla", h) for h in range(MLA_HEADS)]]
        HEAD0 = [0, MEM_HEADS]
        FIRST_STEPS, LAST_STEPS = range(2), [range(2, len(heads) + 3) for heads in HEADS]

        def y_chunk(l, n):
            kind, h = HEADS[l][n]
            return POOL_CHUNKS + h if kind == "mem" else h

        def n_loads(u):
            if U_QR <= u < U_QR + 3:
                return LC
            return 2 if U_GW <= u < U_GW + 6 or U_IN1 + 2 * UG <= u < U_IN1 + 2 * UG + 2 or U_UQ <= u < U_QR else 1

        def landed(u):
            return 16 * sum(n_loads(v) for v in range(u % RING, u + 1, RING))

        def rotate(eng, step, n_swaps, t, swap, width):
            eng.wait_ge(swapped, n_swaps)
            step.done(eng.tensor_tensor(t[:], t[:], cos_t[:].to_broadcast([P, width, S]), ALU.mult))
            step.done(eng.tensor_tensor(swap[:], swap[:], sin_t[:].to_broadcast([P, width, S]), ALU.mult))
            step.wait()
            eng.tensor_tensor(t[:], t[:], swap[:], ALU.add).then_inc(rope_ready, 1)

        @block.sync
        def _(sp):
            def load(u, src, turn=0):
                s = u % RING
                if u >= RING:
                    sp.wait_ge(lo_ready, u - RING + 1 + turn)
                sp.dma_start(raw[:, s, :].rearrange("p (a b) -> p a b", a=2), src).then_inc(raw_landed[s], 16)

            def load_parts(u, parts):
                s = u % RING
                assert len(parts) == n_loads(u)
                sp.wait_ge(lo_ready, u - RING + 1)
                for cols, n, src in parts:
                    if cols is None:
                        dst = raw[:, s, :].rearrange("p (c w) -> p c w", c=8)[:, :, n * ROPE:(n + 1) * ROPE]
                    else:
                        dst = raw[:, s, cols].rearrange("p (a b) -> p a b", a=n)
                    sp.dma_start(dst, src).then_inc(raw_landed[s], 16)

            def rows(w):
                return w.rearrange("(c p) n -> p c n", p=P)

            def load_groups(u0, w, cols, n_units, first=0):
                for g, c in enumerate(cols):
                    for j in range(n_units):
                        r = 2 * ((j + first) % n_units)
                        load(u0 + g * n_units + j, rows(w)[:, r:r + 2, c:c + 512])

            def load_group_loop(u0, w, n_groups, n_units):
                with sp.Fori(0, n_groups // 2) as i:
                    for g in range(2):
                        for j in range(n_units):
                            load(u0 + g * n_units + j,
                                 rows(w)[:, 2 * j:2 * j + 2,
                                         bass.ds(i * 1024 + g * 512, 512)],
                                 i * (2 * n_units))

            for q in range(4):
                sp.dma_start(mem_rows[:, :, q * 512:(q + 1) * 512],
                             mem[0].rearrange("(t p) d -> p t d", p=P)[:, :, q * 512:(q + 1) * 512]) \
                    .then_inc(mem_landed[q], 16)
            load_groups(0, mem_w_kv[0], (0,), UG // 2)
            sp.dma_start(pos_i[:], positions.to_broadcast([P, S])).then_inc(pos_landed, 16)
            sp.dma_start(freq[:], inv_freq).then_inc(pos_landed, 16)
            for j in range(UG // 2, UG):
                load(j, rows(mem_w_kv[0])[:, 2 * j:2 * j + 2, 0:512])
            sp.dma_start(x_rows[:], x[0].rearrange("(t p) d -> p t d", p=P)).then_inc(x_landed, 16)
            for l in range(DEPTH):
                for t in range(3):
                    sp.dma_start(conv_rows[:, l, t, :], ffn_conv_w[l, t].rearrange("(c p) -> c p", p=P)) \
                        .then_inc(params_landed, 16)
                sp.dma_start(conv_rows[:, l, 3, :], ffn_conv_b[l].rearrange("(c p) -> c p", p=P)) \
                    .then_inc(params_landed, 16)
            for k, w in enumerate((ln1_g, ln1_b, ln2_g, ln2_b)):
                sp.dma_start(ln_rows[32 * k:32 * k + 32, :], w.rearrange("l (c p) -> (l c) p", p=P)) \
                    .then_inc(params_landed, 16)
            for r0, w in ((0, pool_scale), (POOL_CHUNKS, mla_q_norm_g), (POOL_CHUNKS + LC, mla_kv_norm_g)):
                sp.dma_start(misc_rows[r0:r0 + w.shape[1] // P, :], w[0].rearrange("(c p) -> c p", p=P)) \
                    .then_inc(params_landed, 16)
            load_groups(UG, mem_w_kv[0], (512,), UG)
            load_groups(U_IN0, pool_w_in[0], (POOL_CH, 0, 512, 1024), UG)
            load_groups(U_K[1], mem_w_kv[1], (0,), UG)
            for r in range(6):
                blocks = [divmod(2 * r + h, GC) for h in range(2)]
                load_parts(U_GW + r, [(slice(h * GC * P, (h + 1) * GC * P), GC,
                                       rows(pool_group_w[0, w])[:, :, b * P:(b + 1) * P])
                                      for h, (w, b) in enumerate(blocks)])
            load_groups(U_OUT[0], pool_w_out[0], (0, 512, 1024, 1536), UG, OUT_TURN)
            load_groups(U_V[1], mem_w_kv[1], (512,), UG)

            def load_ffn(l):
                with sp.Fori(0, FG) as i:
                    for h in range(2):
                        for j in range(UG):
                            load(U_UP[l] + h * UG + j,
                                 rows(ffn_w_up[l])[:, 2 * j:2 * j + 2, bass.ds(i * 512 + h * FF, 512)], i * (2 * UG))
                load_group_loop(U_DOWN[l], ffn_w_down[l], 4, DG)

            load_ffn(0)
            o_rope = 2 * QL
            load_groups(U_IN1, mla_w_in[0], (0,), UG)
            sp.wait_ge(units_done, U_IN1)
            sp.wait_ge(kv_saved, 16)
            sp.dma_start(kv_back[:].rearrange("p a b -> p (a b)"), kv_scratch).then_inc(kv_loaded, 16)
            load_groups(U_IN1 + UG, mla_w_in[0], (QL,), UG)
            for r in range(2):
                w_rope = rows(mla_w_in[0])[:, 8 * r:8 * r + 8, o_rope:o_rope + ROPE]
                load_parts(U_IN1 + 2 * UG + r, [(None, h, w_rope) for h in range(2)])
            load_groups(U_IN1 + 2 * UG + 2, mla_w_in[0], (o_rope + ROPE,), UG)
            per_head = mla_w_uq[0].rearrange("(c p) (h w) -> p c h w", p=P, w=HEAD + ROPE)
            for g in range(3):
                for j in range(2):
                    load_parts(U_UQ + 2 * g + j, [(slice(c * 512, (c + 1) * 512), 4,
                                                   per_head[:, 2 * j + c, 4 * g:4 * g + 4, 0:HEAD]) for c in range(2)])
            for r in range(3):
                load_parts(U_QR + r, [(slice(c * 256, (c + 1) * 256), 4,
                                       per_head[:, c, 4 * r:4 * r + 4, HEAD:HEAD + ROPE]) for c in range(LC)])
            load_groups(U_UK, mla_w_uk[0], (0, 512, 1024), 2)
            load_groups(U_UV, mla_w_uv[0], (0, 512, 1024), 2)
            load_groups(U_OUT[1], mla_w_out[0], (0, 512, 1024, 1536), UG, OUT_TURN)
            load_ffn(1)
            for q in range(4):
                sp.wait_ge(out_copied, 2 * (q + 1))
                sp.dma_start(out[0].rearrange("(t p) d -> p t d", p=P)[:, :, q * 512:(q + 1) * 512],
                             out_rows[:, :, q * 512:(q + 1) * 512]).then_inc(out_saved, 16)
            sp.wait_ge(out_saved, 16 * 4)

        def walk(eng, split):
            state = [0]

            def to(n):
                n = min(n, U_END)
                while state[0] < n:
                    u = state[0]
                    turns = (n - u) // RING
                    calm = all(landed(v + RING * (turns - 1)) - landed(v) == 16 * (turns - 1) for v in range(u, u + RING)) \
                        if turns > 1 else False
                    if turns > 1 and calm and u >= RING:
                        with eng.Fori(0, turns) as i:
                            for j in range(RING):
                                split(u + j, i * RING, i * 16)
                        state[0] += RING * turns
                    else:
                        split(u, 0, 0)
                        state[0] += 1

            def skip(n):
                state[0] = n

            return to, skip

        @block.scalar
        def _(act):
            step = Steps(act, act_step)

            def split(u, turn, turn16):
                s = u % RING
                act.wait_ge(raw_landed[s], landed(u) + turn16)
                if u >= RING:
                    act.wait_ge(units_done, u - RING + 1 + turn)
                act.activation(w_hi[:, s, :], raw[:, s, :], ACT.Copy).then_inc(hi_ready, 1)

            split_to, skip_to = walk(act, split)

            def half_out(e, g, dst, nb=4, ahead=RING):
                split_to(e + ahead)
                act.wait_ge(units_done, e)
                act.activation(dst, first_cols(g, nb), ACT.Copy).then_inc(halves, 1)

            for j in range(KC // 2):
                act.wait_ge(mem_turned, j + 1)
                act.activation(mem_hl[:, 2 * j:2 * j + 2, 0:S], ps[:, j, :].rearrange("p (a b) -> p a b", a=2),
                               ACT.Copy).then_inc(mem_hi, 1)
                if j == 5:
                    split_to(1)
            split_to(RING)
            act.wait_ge(trig, 1)
            act.activation(sin_t[:, 0, :], angle[:], ACT.Sin).then_inc(trig_done, 1)
            act.wait_ge(trig, 2)
            act.activation(cos_t[:, 0, :], turns[:], ACT.Sin).then_inc(trig_done, 1)
            def memory_keys(l):
                half_out(U_K[l] + UG, G_K[l], kv_mem[l][:, 0, :].rearrange("p (a b) -> p a b", a=4), ahead=RING - 1)

            memory_keys(0)
            split_to(U_IN0 + RING)
            for j in range(KC // 2):
                act.wait_ge(x_turned, j + 1)
                bank = ps[:, j % 4, :].rearrange("p (a b) -> p a b", a=2)
                act.activation(res[:, 2 * j:2 * j + 2, :], bank, ACT.Copy)
                act.activation(xy[:, 2 * j:2 * j + 2, 0:S], bank, ACT.Copy).then_inc(x_hi, 1)

            def attention(l, steps):
                heads, h0 = HEADS[l], HEAD0[l]
                n = len(heads)
                for s in steps:
                    if s < n:
                        scale = MEM_SCALE if heads[s][0] == "mem" else MLA_SCALE
                        act.wait_ge(neg_max, h0 + s + 1)
                        if s >= 3:
                            act.wait_ge(probs_turned, h0 + s - 2)
                        for t in range(TB):
                            ins = act.activation(probs[l][s % 3][:, t, :],
                                                 ps[:, head_bank(l, "scores", s), t * S:(t + 1) * S], ACT.Exp,
                                                 bias=soft[:, 1, 2 * s + t:2 * s + t + 1], scale=scale,
                                                 accum_out=soft[:, 2, 2 * s + t:2 * s + t + 1])
                        ins.then_inc(exps, 1)
                    if 2 <= s < n + 2:
                        h = s - 2
                        act.wait_ge(probs_turned, h0 + h + 1)
                        if h >= 2:
                            act.wait_ge(heads_out, h0 + h - 1)
                        act.activation(probs_t[l][h % 2][:].rearrange("p a b -> p (a b)"),
                                       ps[:, head_bank(l, "turned", h), :], ACT.Copy).then_inc(probs_t_ready, 1)
                    if s >= 3:
                        h = s - 3
                        act.wait_ge(heads_out, h0 + h + 1)
                        act.activation(xy[:, y_chunk(l, h), 0:S], ps[:, head_bank(l, "out", h), 0:S],
                                       ACT.Copy).then_inc(y_hi, 1)

            def layer_norm(k):
                l, which, u0, n_units, g0, _ = LN_AT[k]
                for g in range(3):
                    if g:
                        act.wait_ge(evacuated, g0 + g)
                    if g == 1:
                        split_to(u0 + 2 * n_units + 1)
                        act.wait_ge(stat_done, 3 * k + 1)
                        act.activation(shift[:], ps[:, stat_banks(k)[0], 0:S], ACT.Copy, scale=1.0 / 512) \
                            .then_inc(shift_ready, 1)
                    half_out(u0 + (g + 1) * n_units, g0 + g, first_half[k][:])
                    if g == 1:
                        for gg, dst in ((0, sum_dd[k]), (1, squares[k])):
                            split_to(u0 + 2 * n_units + RING + gg + 1)
                            act.wait_ge(shifted, 4 * k + gg + 1)
                            act.activation(dst[:], res[:, 4 * gg:4 * gg + 4, :], ACT.Square).then_inc(squared, 1)
                    if g == 2:
                        act.wait_ge(sq_used, 2 * k + 1)
                        act.wait_ge(evacuated, g0 + 3)
                        act.activation(squares[k][:], res[:, 8:12, :], ACT.Square).then_inc(squared, 1)
                step.wait()
                step.done(act.activation(sqrt_warm[:], eps[:], ACT.Sqrt))
                split_to(u0 + 4 * n_units + RING - 1)
                act.wait_ge(sq_used, 2 * k + 2)
                for h in range(2):
                    act.wait_ge(shifted, 4 * k + 3 + h)
                    act.activation(squares[k][:, 2 * h:2 * h + 2, :], res[:, 12 + 2 * h:14 + 2 * h, :],
                                   ACT.Square).then_inc(squared, 1)
                if k == 0:
                    split_to(U_NEXT[0] + RING + 1)
                act.wait_ge(var_ready, k + 1)
                act.activation(std[:], var[:], ACT.Sqrt, bias=eps[:, 0:1]).then_inc(std_ready, 1)
                if k == 0:
                    split_to(U_NEXT[0] + RING + 2)
                gain, bias = ln_col[:, 2 * which, l, :], ln_col[:, 2 * which + 1, l, :]

                def add_bias(p):
                    c = PIECES[p][0]
                    if k < 3:
                        act.wait_ge(x_ready, KC // 2 + NP * k + p + 1)
                    act.activation(res[:, c, :], res[:, c, :], ACT.Identity, bias=bias[:, c:c + 1]).then_inc(affine, 1)

                for p, (c0, n) in enumerate(PIECES):
                    if p == SINGLES and k < 3:
                        add_bias(p - 1)
                    act.wait_ge(normed, NP * k + p + 1)
                    if n == 2:
                        for c in range(c0, c0 + n):
                            ins = act.activation(res[:, c, :], res[:, c, :], ACT.Identity, scale=gain[:, c:c + 1],
                                                 bias=bias[:, c:c + 1])
                        ins.then_inc(affine, 1)
                        if k < 3:
                            act.wait_ge(affine, NP * k + p + 1)
                            act.activation(xy[:, c0:c0 + n, 0:S], res[:, c0:c0 + n, :], ACT.Copy).then_inc(x_hi, 1)
                    elif k == 3:
                        add_bias(p)
                    else:
                        act.activation(xy[:, c0, 0:S], res[:, c0, :], ACT.Identity, bias=bias[:, c0:c0 + 1]) \
                            .then_inc(x_hi, 1)
                        if p:
                            add_bias(p - 1)
                    split_to(splits_after(k, p))

            def ffn(l):
                u0 = U_UP[l]
                A = RING + 2
                split_to(u0 + A)
                act.wait_ge(pad_zero, l + 1)
                act.activation(silu_warm[:], eps[:], ACT.Silu)
                with act.Fori(0, FG) as i:
                    def ahead(a, b):
                        for j in range(a, b):
                            split(u0 + j, i * (2 * UG), i * (2 * UG // RING * 16))

                    ahead(A, UG + RING)
                    act.wait_ge(units_done, i * (2 * UG) + (u0 + UG))
                    act.activation(h_pad[:, :, 1:S + 1], first_cols(G_UP[l]), ACT.Copy).then_inc(halves, 1)
                    ahead(UG + RING, UG + A + 4)
                    act.wait_ge(conv_gate, i + (FG * l + 1))
                    act.activation(gate[:], gate[:], ACT.Silu).then_inc(silu_done, 1)
                    ahead(UG + A + 4, 2 * UG + RING)
                    act.wait_ge(units_done, i * (2 * UG) + (u0 + 2 * UG))
                    act.activation(h_pad[:, :, 1:S + 1], first_cols(G_UP[l] + 1), ACT.Copy).then_inc(halves, 1)
                    ahead(2 * UG + RING, 2 * UG + A)
                    act.wait_ge(product, i + (FG * l + 1))
                    act.wait_ge(kv_saved, 16)
                    act.activation(act_hl[:, bass.ds(i * 4, 4), 0:S], val[:], ACT.Copy).then_inc(act_hi, 1)
                skip_to(u0 + A + 2 * FG * UG)

            half_out(U_IN0 + UG, G_IN0, q_mem[0][:])
            act.wait_ge(pads_ready, 1)
            for g in range(3):
                half_out(U_IN0 + (2 + g) * UG, G_IN0 + 1 + g, u_pad[:, 4 * g:4 * g + 4, PAD:PAD + S])
            for k in range(len(WINDOWS)):
                if k == 2:
                    attention(0, FIRST_STEPS)
                if k == 3:
                    memory_keys(1)
                    attention(0, LAST_STEPS[0])
                split_to(min(U_K[1] + RING + 3 * k, U_GW + RING))
                act.wait_ge(pool_diff, k + 1)
                act.activation(pooled[:, GC * k:GC * k + GC, 0:S], u_pad[:, GC * k:GC * k + GC, PAD:PAD + S],
                               ACT.Copy).then_inc(pool_hi, 1)
            for g in range(3):
                split_to(U_GW + 2 * (g + 1) + RING - 1)
                act.wait_ge(units_done, U_GW + 2 * (g + 1))
                if g == 2:
                    act.wait_ge(pool_y_ready, 1)
                for b in range(4):
                    ins = act.activation(y_pool[g % 2][:, b, :], ps[:, bank_set(G_GW + g) + b, 0:S], ACT.Copy,
                                         scale=misc_col[:, 4 * g + b:4 * g + b + 1])
                ins.then_inc(halves, 1)
                split_to(U_GW + 2 * (g + 1) + RING)
                act.wait_ge(evacuated, G_GW + g + 1)
                act.activation(xy[:, 4 * g:4 * g + 4, 0:S], y_pool[g % 2][:], ACT.Copy).then_inc(pool_y_hi, 1)
            layer_norm(0)
            act.wait_ge(evacuated, G_V[1] + 1)
            act.dma_start(kv_scratch, kv_mem[1][:].rearrange("p a b -> p (a b)")).then_inc(kv_saved, 16)
            ffn(0)
            layer_norm(1)

            def latent_norm(n, e, g, gains):
                if n:
                    act.wait_ge(latent_ready, n)
                half_out(e, g, latent[:])
                act.wait_ge(evacuated, g + 1)
                act.activation(latent_sq[:], latent[:], ACT.Square).then_inc(lat_sq, 1)
                split_to(e + RING + 1)
                act.wait_ge(lat_var, n + 1)
                act.activation(std[:], var[:], ACT.Sqrt).then_inc(lat_std, 1)
                split_to(e + RING + 2)
                act.wait_ge(lat_normed, n + 1)
                for c in range(LC):
                    step.done(act.activation(latent[:, c, :], latent[:, c, :], ACT.Copy,
                                             scale=misc_col[:, gains + c:gains + c + 1]))
                step.wait()
                act.activation((qn_hl, kvn_hl)[n][:, :, 0:S], latent[:], ACT.Copy).then_inc(lat_hi, 1)

            def swap_halves(g, src, dst, quarters=range(4)):
                act.wait_ge(evacuated, g + 1)
                for q in quarters:
                    r, w = 32 * (q ^ 1), 32 * q
                    ins = act.activation(dst[w:w + 32, :, :], src[r:r + 32, :, :], ACT.Copy)
                ins.then_inc(swapped, 1)

            e = U_IN1
            latent_norm(0, e + UG, G_IN1, POOL_CHUNKS)
            latent_norm(1, e + 2 * UG, G_IN1 + 1, POOL_CHUNKS + LC)
            half_out(e + 2 * UG + 2, G_IN1 + 2, k_rope[:], 1)
            swap_halves(G_IN1 + 2, k_rope, k_swap)
            half_out(U_UQ, G_IN1 + 3, q_mem[1][:])
            for g in range(3):
                half_out(U_UQ + 2 * (g + 1), G_UQ + g, q_nope[:, 4 * g:4 * g + 4, :])
            half_out(U_QR + 2, G_QR, q_rope[:, 0:4, :])
            half_out(U_QR + 3, G_QR + 1, q_rope[:, 4:6, :], 2)
            for g in range(3):
                half_out(U_UK + 2 * (g + 1), G_UK + g, k_nope[:, 4 * g:4 * g + 4, :])
                if g < 2:
                    swap_halves(G_QR + 1, q_rope, q_swap, (2 * g, 2 * g + 1))
            split_to(U_UV + 2 + RING)
            attention(1, FIRST_STEPS)
            split_to(U_OUT[1] + RING)
            attention(1, LAST_STEPS[1])
            layer_norm(2)
            ffn(1)
            layer_norm(3)

        @block.vector
        def _(dve):
            step = Steps(dve, dve_step)

            def split(u, turn, turn16):
                s = u % RING
                dve.wait_ge(hi_ready, u + 1 + turn)
                dve.tensor_tensor(w_lo[:, s, :], raw[:, s, :], w_hi[:, s, :], ALU.subtract).then_inc(lo_ready, 1)

            split_to, skip_to = walk(dve, split)

            def add_half(e, g, h, dst, nb=4, ahead=RING):
                split_to(e + ahead)
                dve.wait_ge(halves, h + 1)
                dve.tensor_tensor(dst, dst, second_cols(g, nb), ALU.add).then_inc(evacuated, 1)

            def rows_out(e, g, dst):
                split_to(e + RING - 1)
                dve.wait_ge(units_done, e)
                b = bank_set(g)
                dve.tensor_copy(dst, ps[:, b:b + TB, :]).then_inc(evacuated, 1)

            for j in range(KC // 2):
                dve.wait_ge(mem_hi, j + 1)
                dve.tensor_tensor(mem_hl[:, 2 * j:2 * j + 2, S:2 * S], ps[:, j, :].rearrange("p (a b) -> p a b", a=2),
                                  mem_hl[:, 2 * j:2 * j + 2, 0:S], ALU.subtract).then_inc(mem_ready, 1)
                if j == 5:
                    split_to(1)
            split_to(RING)

            dve.wait_ge(pos_landed, 32)
            for q in range(4):
                step.done(dve.memset(sign[32 * q:32 * q + 32, :], -1.0 if q % 2 == 0 else 1.0))
            step.done(dve.tensor_copy(turns[:], pos_i[:]))
            step.wait()
            step.done(dve.tensor_scalar(angle[:], turns[:], freq[:, 0:1], None, ALU.mult))
            step.wait()
            step.done(dve.tensor_scalar(turns[:], angle[:], 1.0 / 6.283185307179586, MAGIC, ALU.mult, ALU.add))
            step.wait()
            step.done(dve.tensor_scalar(turns[:], turns[:], MAGIC, None, ALU.subtract))
            for part in TWO_PI_PARTS:
                step.wait()
                step.done(dve.scalar_tensor_tensor(out=angle[:], in0=turns[:], scalar=-part, in1=angle[:],
                                                   op0=ALU.mult, op1=ALU.add))
            step.wait()
            step.done(dve.tensor_scalar(angle[:], angle[:], 3.1415925, -3.1415925, ALU.min, ALU.max))
            step.wait()
            step.done(dve.scalar_tensor_tensor(out=turns[:], in0=angle[:], scalar=-1.0, in1=angle[:],
                                               op0=ALU.mult, op1=ALU.max))
            step.wait()
            dve.tensor_scalar(angle[:], angle[:], sign[:, 0:1], None, ALU.mult).then_inc(trig, 1)
            dve.tensor_scalar(turns[:], turns[:], -1.0, 1.5707964, ALU.mult, ALU.add).then_inc(trig, 1)

            def heads_of(t):
                return t.rearrange("p (a b) -> p a b", a=4)

            def memory_keys(l):
                add_half(U_K[l] + UG, G_K[l], H_K[l], heads_of(kv_mem[l][:, 0, :]), ahead=RING - 1)

            def memory_values(l):
                rows_out(U_V[l] + UG, G_V[l], kv_mem[l][:, 1, :].rearrange("p (a b) -> p a b", a=TB))

            memory_keys(0)
            split_to(U_V[0] + 4 + RING)
            for l in range(DEPTH):
                dve.wait_ge(params_turned, l + 1)
                dve.tensor_copy(conv_col[:, l, :, :].rearrange("p a b -> p (a b)"), ps[:, 6 + l, 0:8 * FC]) \
                    .then_inc(params_ready, 1)
            dve.wait_ge(params_turned, 3)
            dve.tensor_copy(ln_col[:].rearrange("p a b c -> p (a b c)"), ps[:, 3, 0:P]).then_inc(params_ready, 1)
            dve.tensor_copy(misc_col[:], ps[:, 3, P:P + POOL_CHUNKS + 2 * LC]).then_inc(params_ready, 1)
            memory_values(0)

            def x_lo(c, n, src):
                dve.tensor_tensor(xy[:, c:c + n, S:2 * S], src, xy[:, c:c + n, 0:S], ALU.subtract).then_inc(x_ready, 1)

            for j in range(KC // 2):
                dve.wait_ge(x_hi, j + 1)
                x_lo(2 * j, 2, ps[:, j % 4, :].rearrange("p (a b) -> p a b", a=2))

            def attention(l, steps):
                heads, h0 = HEADS[l], HEAD0[l]
                n = len(heads)
                for s in steps:
                    if s < n:
                        scale = MEM_SCALE if heads[s][0] == "mem" else MLA_SCALE
                        c = slice(2 * s, 2 * s + TB)
                        dve.wait_ge(scores_ready, h0 + s + 1)
                        scores = ps[:, head_bank(l, "scores", s), :].rearrange("p (a b) -> p a b", a=TB)
                        step.done(dve.tensor_reduce(soft[:, 0, c], scores, AX_X, ALU.max))
                        step.wait()
                        dve.tensor_scalar(soft[:, 1, c], soft[:, 0, c], -scale, None, ALU.mult).then_inc(neg_max, 1)
                    if 1 <= s <= n:
                        c = slice(2 * (s - 1), 2 * (s - 1) + TB)
                        dve.wait_ge(exps, h0 + s)
                        step.done(dve.reciprocal(soft[:, 3, c], soft[:, 2, c]))
                        step.wait()
                        for t in range(TB):
                            i = 2 * (s - 1) + t
                            ins = dve.tensor_scalar(probs[l][(s - 1) % 3][:, t, :], probs[l][(s - 1) % 3][:, t, :],
                                                    soft[:, 3, i:i + 1], None, ALU.mult)
                        ins.then_inc(probs_ready, 1)
                    if s >= 3:
                        h = s - 3
                        dve.wait_ge(y_hi, h0 + h + 1)
                        y = xy[:, y_chunk(l, h), :]
                        dve.tensor_tensor(y[:, S:2 * S], ps[:, head_bank(l, "out", h), 0:S], y[:, 0:S], ALU.subtract) \
                            .then_inc(y_ready, 1)

            def layer_norm(k):
                l, which, u0, n_units, g0, h0 = LN_AT[k]

                def chunks(g):
                    return res[:, 4 * g:4 * g + 4, :]

                alpha = dict(scalar=ALPHA, op0=ALU.mult)
                shift4 = wide(shift[:].unsqueeze(1), 4)
                for g in range(3):
                    split_to(u0 + (g + 1) * n_units + RING)
                    dve.wait_ge(halves, h0 + g + 1)
                    if g < 2:
                        step.done(dve.scalar_tensor_tensor(out=chunks(g), in0=chunks(g), in1=second_cols(g0 + g),
                                                           op1=ALU.add, **alpha))
                    else:
                        step.done(dve.tensor_tensor(chunks(g), chunks(g), second_cols(g0 + g), ALU.add))
                    step.wait()
                    dve.tensor_tensor(chunks(g), chunks(g), first_half[k][:], ALU.add).then_inc(evacuated, 1)
                    dve.wait_ge(evacuated, g0 + g + 1)
                    if g == 0:
                        step.done(dve.tensor_tensor(fold_b[:], res[:, 0:2, :], res[:, 2:4, :], ALU.add))
                        step.wait()
                        dve.tensor_tensor(fold_a[:], fold_b[:, 0, :], fold_b[:, 1, :], ALU.add).then_inc(col_sum, 1)
                    if g == 1:
                        dve.wait_ge(shift_ready, k + 1)
                        for gg in range(2):
                            dve.tensor_tensor(chunks(gg), chunks(gg), shift4, ALU.subtract).then_inc(shifted, 1)
                        split_to(u0 + 2 * n_units + RING + 1)
                        for gg in (2, 3):
                            step.done(dve.scalar_tensor_tensor(out=chunks(gg), in0=chunks(gg), in1=shift4,
                                                               op1=ALU.subtract, **alpha))
                        split_to(u0 + 2 * n_units + RING + 2)
                        dve.wait_ge(shifted, 4 * k + 2)
                        step.done(dve.tensor_tensor(sum_d[k][:], chunks(0), chunks(1), ALU.add))
                        step.wait()
                step.done(dve.tensor_tensor(sum_d[k][:], sum_d[k][:], chunks(2), ALU.add))
                step.wait()
                step.done(dve.tensor_tensor(fold_b[:], sum_d[k][:, 0:2, :], sum_d[k][:, 2:4, :], ALU.add))
                step.wait()
                dve.tensor_tensor(fold_a[:], fold_b[:, 0, :], fold_b[:, 1, :], ALU.add).then_inc(sums_ready, 1)
                dve.wait_ge(sums_ready, 2 * k + 1)
                dve.wait_ge(sq_used, 2 * k + 2)
                step.done(dve.tensor_tensor(fold_b[:], sum_dd[k][:, 0:2, :], sum_dd[k][:, 2:4, :], ALU.add))
                step.wait()
                dve.tensor_tensor(sum_dd[k][:, 0, :], fold_b[:, 0, :], fold_b[:, 1, :], ALU.add) \
                    .then_inc(sums_ready, 1)
                e = u0 + 4 * n_units
                split_to(e + RING - 1)
                dve.wait_ge(units_done, e)
                b3 = bank_set(g0 + 3)
                for h in range(2):
                    two = res[:, 12 + 2 * h:14 + 2 * h, :]
                    dve.tensor_tensor(two, two, ps[:, b3 + 2 * h:b3 + 2 * h + 2, 0:S], ALU.add).then_inc(shifted, 1)
                for h in range(2):
                    dve.wait_ge(shifted, 4 * k + 3 + h)
                    dve.tensor_tensor(sum_d[k][:, h, :], res[:, 12 + 2 * h, :], res[:, 13 + 2 * h, :],
                                      ALU.add).then_inc(tail_sum, 1)
                for h in range(2):
                    dve.wait_ge(squared, 5 * k + 4 + h)
                    dve.tensor_tensor(squares[k][:, 2 * h, :], squares[k][:, 2 * h, :], squares[k][:, 2 * h + 1, :],
                                      ALU.add).then_inc(tail_sum, 1)
                dve.sem_inc(evacuated, 1)
                b_d, b_dd = stat_banks(k)
                if k == 0:
                    split_to(e + RING + 1)
                dve.wait_ge(stat_done, 3 * k + 2)
                dve.tensor_scalar(mean[:], ps[:, b_d, 0:S], 1.0 / D, None, ALU.mult).then_inc(mean_ready, 1)
                dve.wait_ge(mean_ready, k + 1)
                step.done(dve.tensor_tensor(mean_sq[:], mean[:], mean[:], ALU.mult))
                step.wait()
                dve.wait_ge(stat_done, 3 * k + 3)
                dve.scalar_tensor_tensor(out=var[:], in0=ps[:, b_dd, 0:S], scalar=1.0 / D,
                                         in1=mean_sq[:], op0=ALU.mult, op1=ALU.subtract).then_inc(var_ready, 1)
                gain, bias = ln_col[:, 2 * which, l, :], ln_col[:, 2 * which + 1, l, :]

                for p in range(EARLY):
                    c = PIECES[p][0]
                    step.done(dve.tensor_tensor(res[:, c, :], res[:, c, :], mean[:], ALU.subtract))
                dve.wait_ge(std_ready, k + 1)
                step.done(dve.reciprocal(rstd[:], std[:]))
                step.wait()
                if k == 0:
                    split_to(U_NEXT[0] + RING + 2)
                def normalise(p):
                    c0, n = PIECES[p]
                    if p >= EARLY:
                        dve.wait_ge(centred, (NP - EARLY) * k + p - EARLY + 1)
                    if n == 1:
                        ins = dve.scalar_tensor_tensor(out=res[:, c0, :], in0=res[:, c0, :],
                                                       scalar=gain[:, c0:c0 + 1], in1=rstd[:],
                                                       op0=ALU.mult, op1=ALU.mult)
                    else:
                        piece = res[:, c0:c0 + n, :]
                        ins = dve.tensor_tensor(piece, piece, wide(rstd[:].unsqueeze(1), n), ALU.mult)
                    ins.then_inc(normed, 1)

                def remainder(p):
                    c0, n = PIECES[p]
                    dve.wait_ge(x_hi, KC // 2 + NP * k + p + 1)
                    if n == 1:
                        dve.scalar_tensor_tensor(out=xy[:, c0, S:2 * S], in0=res[:, c0, :],
                                                 scalar=bias[:, c0:c0 + 1], in1=xy[:, c0, 0:S],
                                                 op0=ALU.add, op1=ALU.subtract).then_inc(x_ready, 1)
                    else:
                        x_lo(c0, n, res[:, c0:c0 + n, :])
                    split_to(splits_after(k, p))

                def output(j):
                    dve.wait_ge(final_turned, j + 1)
                    dve.tensor_copy(out_rows[:, :, 2 * j * P:(2 * j + 2) * P],
                                    ps[:, j, :].rearrange("p (t b) -> p t b", t=TB)).then_inc(out_copied, 1)

                if k == 3:
                    for p in range(NP):
                        normalise(p)
                        if p > SINGLES:
                            output(p - SINGLES - 1)
                    for j in range(NP - SINGLES - 1, KC // 2):
                        output(j)
                    return

                for p in range(0, SINGLES, 2):
                    normalise(p)
                    normalise(p + 1)
                    if p + 2 == SINGLES:
                        normalise(SINGLES)
                    remainder(p)
                    remainder(p + 1)
                for p in range(SINGLES, NP):
                    if p + 1 < NP:
                        normalise(p + 1)
                    remainder(p)

            def ffn(l):
                u0 = U_UP[l]
                A = RING + 2
                split_to(u0 + A)
                dve.memset(h_pad[:, :, 0:1], 0.0)
                dve.memset(h_pad[:, :, S + 1:S + 2], 0.0).then_inc(pad_zero, 1)

                def convolve(dst, chunk, between=lambda: None):
                    def col(t, b):
                        return conv_col[:, l, t, bass.ds(chunk + b, 1)]

                    done = [step.done(dve.tensor_scalar(dst[:, b, :], h_pad[:, b, 1:S + 1], col(1, b), col(3, b),
                                                        ALU.mult, ALU.add)) for b in range(4)]
                    for t in (0, 2):
                        between()
                        for b in range(4):
                            step.wait(done[b])
                            done[b] = step.done(dve.scalar_tensor_tensor(
                                out=dst[:, b, :], in0=h_pad[:, b, t:t + S], scalar=col(t, b), in1=dst[:, b, :],
                                op0=ALU.mult, op1=ALU.add))

                with dve.Fori(0, FG) as i:
                    step.loop(i, 24)
                    reached = [A]

                    def ahead(n):
                        for j in range(reached[0], n):
                            split(u0 + j, i * (2 * UG), 0)
                        reached[0] = n

                    def hidden(half):
                        g = G_UP[l] + half
                        dve.wait_ge(halves, i * 2 + (H_UP[l] + half + 1))
                        dve.tensor_tensor(h_pad[:, :, 1:S + 1], h_pad[:, :, 1:S + 1], second_cols(g), ALU.add) \
                            .then_inc(evacuated, 1)
                        dve.wait_ge(evacuated, i * 2 + (g + 1))

                    ahead(UG + RING)
                    hidden(0)
                    convolve(gate, i * 4, lambda: ahead(reached[0] + 1))
                    step.wait()
                    dve.sem_inc(conv_gate, 1)
                    ahead(2 * UG + RING)
                    hidden(1)
                    convolve(val, i * 4 + FC, lambda: ahead(reached[0] + 1))
                    assert reached[0] == 2 * UG + A
                    dve.wait_ge(silu_done, i + (FG * l + 1))
                    step.wait()
                    dve.tensor_tensor(val[:], val[:], gate[:], ALU.mult).then_inc(product, 1)
                    dve.wait_ge(act_hi, i + (FG * l + 1))
                    a = act_hl[:, bass.ds(i * 4, 4), :]
                    dve.tensor_tensor(a[:, :, S:2 * S], val[:], a[:, :, 0:S], ALU.subtract).then_inc(act_ready, 1)
                step.end_loop(FG)
                skip_to(u0 + A + 2 * FG * UG)

            add_half(U_IN0 + UG, G_IN0, H_IN0, q_mem[0][:])
            for g in range(3):
                add_half(U_IN0 + (2 + g) * UG, G_IN0 + 1 + g, H_IN0 + 1 + g, u_pad[:, 4 * g:4 * g + 4, PAD:PAD + S])
            for k in range(len(WINDOWS)):
                if k == 2:
                    attention(0, FIRST_STEPS)
                if k == 3:
                    memory_keys(1)
                    attention(0, LAST_STEPS[0])
                split_to(min(U_K[1] + RING + 3 * k, U_GW + RING))
                u = u_pad[:, GC * k:GC * k + GC, PAD:PAD + S]
                dve.wait_ge(windowed, k + 1)
                dve.tensor_tensor(u, win[(k + 1) % 2][:, :, PAD:PAD + S], u, ALU.subtract).then_inc(pool_diff, 1)
                dve.wait_ge(pool_hi, k + 1)
                p = pooled[:, GC * k:GC * k + GC, :]
                dve.tensor_tensor(p[:, :, S:2 * S], u, p[:, :, 0:S], ALU.subtract).then_inc(pooled_ready, 1)
            for g in range(3):
                split_to(U_GW + 2 * (g + 1) + RING - 1)
                dve.wait_ge(halves, H_GW + g + 1)
                yp = y_pool[g % 2]
                for b in range(4):
                    ins = dve.scalar_tensor_tensor(out=yp[:, b, :], in0=ps[:, bank_set(G_GW + g) + b, S:2 * S],
                                                   scalar=misc_col[:, 4 * g + b:4 * g + b + 1], in1=yp[:, b, :],
                                                   op0=ALU.mult, op1=ALU.add)
                ins.then_inc(evacuated, 1)
                split_to(U_GW + 2 * (g + 1) + RING)
                dve.wait_ge(pool_y_hi, g + 1)
                y = xy[:, 4 * g:4 * g + 4, :]
                dve.tensor_tensor(y[:, :, S:2 * S], yp[:], y[:, :, 0:S], ALU.subtract).then_inc(pool_y_ready, 1)
            layer_norm(0)
            memory_values(1)
            ffn(0)
            layer_norm(1)

            def latent_norm(n, e, g, h):
                add_half(e, g, h, latent[:])
                dve.wait_ge(lat_sq, n + 1)
                sq = latent_sq
                step.done(dve.tensor_tensor(sq[:, 0:2, :], sq[:, 0:2, :], sq[:, 2:4, :], ALU.add))
                step.wait()
                dve.tensor_tensor(sq[:, 0, :], sq[:, 0, :], sq[:, 1, :], ALU.add).then_inc(lat_sum, 1)
                split_to(e + RING + 1)
                dve.wait_ge(lat_stat, n + 1)
                dve.tensor_scalar(var[:], ps[:, bank_set(g), 0:S], 1.0 / QL, RMS_EPS, ALU.mult, ALU.add) \
                    .then_inc(lat_var, 1)
                dve.wait_ge(lat_std, n + 1)
                step.done(dve.reciprocal(rstd[:], std[:]))
                step.wait()
                dve.tensor_tensor(latent[:], latent[:], wide(rstd[:].unsqueeze(1), LC), ALU.mult) \
                    .then_inc(lat_normed, 1)
                split_to(e + RING + 2)
                dve.wait_ge(lat_hi, n + 1)
                hl = (qn_hl, kvn_hl)[n]
                dve.tensor_tensor(hl[:, :, S:2 * S], latent[:], hl[:, :, 0:S], ALU.subtract).then_inc(latent_ready, 1)

            latent_norm(0, U_IN1 + UG, G_IN1, H_IN1)
            latent_norm(1, U_IN1 + 2 * UG, G_IN1 + 1, H_IN1 + 1)
            add_half(U_IN1 + 2 * UG + 2, G_IN1 + 2, H_IN1 + 2, k_rope[:], 1)
            dve.wait_ge(trig_done, 2)
            rotate(dve, step, 1, k_rope, k_swap, 1)
            add_half(U_UQ, G_IN1 + 3, H_IN1 + 3, q_mem[1][:])
            for g in range(3):
                add_half(U_UQ + 2 * (g + 1), G_UQ + g, H_UQ + g, q_nope[:, 4 * g:4 * g + 4, :])
            add_half(U_QR + 2, G_QR, H_QR, q_rope[:, 0:4, :])
            add_half(U_QR + 3, G_QR + 1, H_QR + 1, q_rope[:, 4:6, :], 2)
            for g in range(3):
                add_half(U_UK + 2 * (g + 1), G_UK + g, H_UK + g, k_nope[:, 4 * g:4 * g + 4, :])
            for g in range(3):
                rows_out(U_UV + 2 * (g + 1), G_UV + g, v_mla[:, :, 512 * g:512 * g + 512])
                if g == 0:
                    attention(1, FIRST_STEPS)
            split_to(U_OUT[1] + RING - 1)
            attention(1, LAST_STEPS[1][:1])
            split_to(U_OUT[1] + RING)
            attention(1, LAST_STEPS[1][1:])
            layer_norm(2)
            ffn(1)
            layer_norm(3)

        @block.gpsimd
        def _(pool):
            step = Steps(pool, pool_step)
            step.done(pool.memset(ident[:], 0.0))
            step.wait()
            step.done(pool.affine_select(out=ident[:], in_=ident[:], compare_op=ALU.not_equal, fill=1.0, base=0,
                                         pattern=[[-1, P]], channel_multiplier=1))
            step.wait()
            pool.memset(ones[:], 1.0).then_inc(consts_ready, 1)
            pool.memset(eps[:], LN_EPS)
            for k, w in enumerate(WINDOWS):
                h = w // 2
                pool.memset(inv_count[:, k, h:S - h + 1], 1.0 / w)
                for t in range(h):
                    pool.memset(inv_count[:, k, t:t + 1], 1.0 / (t + h))
                for t in range(S - h + 1, S):
                    pool.memset(inv_count[:, k, t:t + 1], 1.0 / (S - t + h))

            pool.wait_ge(mem_turned, KC // 2)
            pool.memset(u_pad[:, :, 0:PAD], 0.0)
            pool.memset(u_pad[:, :, PAD + S:], 0.0).then_inc(pads_ready, 1)
            pool.wait_ge(pads_ready, 1)
            for k, w in enumerate(WINDOWS):
                pool.wait_ge(evacuated, G_IN0 + 1 + (1, 2, 3, 3)[k])
                src = u_pad[:, GC * k:GC * k + GC, :]
                n = 0
                for m in range(k + 1):
                    back, forth = (1, 0) if m == 0 else (2 ** (m - 1), 2 ** (m - 1))
                    reach = w // 2 - 2 ** m
                    a, b = PAD - reach, PAD + S + reach
                    dst = win[(k - m) % 2][:, :, a:b]
                    if k >= 1 and m < 2:
                        pool.wait_ge(pool_diff, k)
                    step.done(pool.tensor_tensor(dst, src[:, :, a - back:b - back],
                                                 src[:, :, a + forth:b + forth], ALU.add))
                    step.wait()
                    src = win[(k - m) % 2]
                assert src is win[0]
                pool.tensor_tensor(win[(k + 1) % 2][:, :, PAD:PAD + S], src[:, :, PAD:PAD + S],
                                   wide(inv_count[:, k:k + 1, :], GC), ALU.mult).then_inc(windowed, 1)

            for k in range(4):
                if k == 2:
                    pool.wait_ge(rope_ready, 1)
                    rotate(pool, step, 3, q_rope, q_swap, MLA_HEADS // 2)
                for g in range(1, 3):
                    pool.wait_ge(squared, 5 * k + g + 1)
                    if g > 1:
                        pool.wait_ge(sq_used, 2 * k + g - 1)
                    pool.tensor_tensor(sum_dd[k][:], sum_dd[k][:], squares[k][:], ALU.add).then_inc(sq_used, 1)
                pool.wait_ge(mean_ready, k + 1)
                for c0, n in PIECES[EARLY:]:
                    piece = res[:, c0:c0 + n, :]
                    pool.tensor_tensor(piece, piece, wide(mean[:].unsqueeze(1), n), ALU.subtract).then_inc(centred, 1)

        @block.tensor
        def _(pe):
            def multiply(u, g, rhs, chunks, nb=4, width=512, first=False, last=False, turn=0, narrow=False):
                s, b0 = u % RING, bank_set(g)
                pe.wait_ge(lo_ready, u + 1 + turn)
                for c in range(chunks):
                    x_hl = rhs(c)
                    end = last and c == chunks - 1
                    for b in range(nb):
                        col = c * width + b * P
                        hi, lo = w_hi[:, s, col:col + P], w_lo[:, s, col:col + P]
                        bank = ps[:, b0 + b, :]
                        if narrow:
                            pe.matmul(bank[:, 0:S], hi, x_hl[:, 0:S], start=first and c == 0, stop=False)
                            pe.matmul(bank[:, 0:S], hi, x_hl[:, S:2 * S], start=False, stop=False)
                            ins = pe.matmul(bank[:, 0:S], lo, x_hl[:, 0:S], start=False, stop=end)
                        elif end:
                            pe.matmul(bank[:, S:2 * S], lo, x_hl[:, 0:S], start=False, stop=False)
                            ins = pe.matmul(bank, hi, x_hl, start=False, stop=True)
                        else:
                            pe.matmul(bank, hi, x_hl, start=first and c == 0, stop=False)
                            ins = pe.matmul(bank[:, S:2 * S], lo, x_hl[:, 0:S], start=False, stop=False)
                ins.then_inc(units_done, 1)

            def multiply_rows(u, g, lhs, chunks, first=False, last=False):
                s, b0 = u % RING, bank_set(g)
                pe.wait_ge(lo_ready, u + 1)
                for c in range(chunks):
                    x_hl = lhs(c)
                    hi, lo = w_hi[:, s, c * 512:(c + 1) * 512], w_lo[:, s, c * 512:(c + 1) * 512]
                    for t in range(TB):
                        x_hi_, x_lo_ = x_hl[:, t * P:(t + 1) * P], x_hl[:, S + t * P:S + (t + 1) * P]
                        end = last and c == chunks - 1
                        pe.matmul(ps[:, b0 + t, :], x_hi_, hi, start=first and c == 0, stop=False)
                        pe.matmul(ps[:, b0 + t, :], x_lo_, hi, start=False, stop=False)
                        ins = pe.matmul(ps[:, b0 + t, :], x_hi_, lo, start=False, stop=end)
                ins.then_inc(units_done, 1)

            def banks_free(g, turn=0):
                pe.wait_ge(evacuated, g - 1 + turn)

            def xy_chunk(j):
                return lambda c: xy[:, 2 * j + c, :]

            def column_sums(bank, src):
                return pe.matmul(ps[:, bank, 0:S], ones[:], src, start=True, stop=True)

            pe.wait_ge(consts_ready, 1)
            for j in range(KC // 2):
                pe.wait_ge(mem_landed[j // 2], 16)
                for c in range(2):
                    for t in range(TB):
                        ins = pe.transpose(ps[:, j, c * S + t * P:c * S + (t + 1) * P],
                                           mem_rows[:, t, (2 * j + c) * P:(2 * j + c + 1) * P], ident[:])
                ins.then_inc(mem_turned, 1)
            def memory_group(u, g, kind, units=range(UG)):
                for j in units:
                    pe.wait_ge(mem_ready, j + 1)
                    (multiply, multiply_rows)[kind](u + j, g, lambda c: mem_hl[:, 2 * j + c, :], 2,
                                                    first=j == 0, last=j == UG - 1)

            pe.wait_ge(mem_ready, 4)
            memory_group(U_K[0], G_K[0], 0)
            pe.wait_ge(mem_ready, 8)
            memory_group(U_V[0], G_V[0], 1, range(4))
            pe.wait_ge(params_landed, 16 * (4 * DEPTH + 7))
            for l in range(DEPTH):
                for t in range(4):
                    ins = pe.transpose(ps[:, 6 + l, t * 2 * FC:(t + 1) * 2 * FC], conv_rows[:, l, t, :],
                                       ident[0:2 * FC, 0:2 * FC])
                ins.then_inc(params_turned, 1)
            n_misc = POOL_CHUNKS + 2 * LC
            pe.wait_ge(evacuated, G_K[0] + 1)
            pe.transpose(ps[:, 3, 0:P], ln_rows[:], ident[:])
            pe.transpose(ps[:, 3, P:P + n_misc], misc_rows[:], ident[0:n_misc, 0:n_misc]).then_inc(params_turned, 1)
            memory_group(U_V[0], G_V[0], 1, range(4, UG))

            pe.wait_ge(evacuated, 1)
            pe.wait_ge(x_landed, 16)
            for j in range(KC // 2):
                if j == 3:
                    pe.wait_ge(params_ready, 4)
                if j >= 4:
                    pe.wait_ge(x_ready, j - 3)
                for c in range(2):
                    for t in range(TB):
                        ins = pe.transpose(ps[:, j % 4, c * S + t * P:c * S + (t + 1) * P],
                                           x_rows[:, t, (2 * j + c) * P:(2 * j + c + 1) * P], ident[:])
                ins.then_inc(x_turned, 1)

            def attention(l, steps):
                heads, h0 = HEADS[l], HEAD0[l]
                n = len(heads)
                kv = (kv_mem[0], kv_back)[l]
                for s in steps:
                    if s < n:
                        kind, h = heads[s]
                        if kind == "mla" and h == 0:
                            pe.wait_ge(rope_ready, 2)
                        if s >= 3:
                            pe.wait_ge(exps, h0 + s - 2)
                        q = q_mem[l][:, h, :] if kind == "mem" else q_nope[:, h, :]
                        k = kv[:, 0, h * S:(h + 1) * S] if kind == "mem" else k_nope[:, h, :]
                        for t in range(TB):
                            bank = ps[:, head_bank(l, "scores", s), t * S:(t + 1) * S]
                            rot = kind == "mla"
                            ins = pe.matmul(bank, q[:, t * P:(t + 1) * P], k, start=True, stop=not rot)
                            if rot:
                                r = ROPE * (h % 2)
                                ins = pe.matmul(bank, q_rope[r:r + ROPE, h // 2, t * P:(t + 1) * P],
                                                k_rope[r:r + ROPE, 0, :], start=False, stop=True)
                        ins.then_inc(scores_ready, 1)
                    if s == 3:
                        pe.wait_ge(evacuated, (G_GW, G_OUT[1])[l])
                    if 2 <= s < n + 2:
                        h = s - 2
                        pe.wait_ge(probs_ready, h0 + h + 1)
                        if h >= 3:
                            pe.wait_ge(probs_t_ready, h0 + h - 2)
                        for m in range(TB):
                            for t in range(TB):
                                ins = pe.transpose(ps[:, head_bank(l, "turned", h), m * S + t * P:m * S + (t + 1) * P],
                                                   probs[l][h % 3][:, t, m * P:(m + 1) * P], ident[:])
                        ins.then_inc(probs_turned, 1)
                    if s >= 3:
                        n_, (kind, h) = s - 3, heads[s - 3]
                        pe.wait_ge(probs_t_ready, h0 + n_ + 1)
                        if n_ >= 2:
                            pe.wait_ge(y_ready, h0 + n_ - 1)
                        for m in range(TB):
                            v = kv[:, 1, m * 512 + h * HEAD:m * 512 + (h + 1) * HEAD] if kind == "mem" \
                                else v_mla[:, m, h * HEAD:(h + 1) * HEAD]
                            ins = pe.matmul(ps[:, head_bank(l, "out", n_), 0:S], v, probs_t[l][n_ % 2][:, m, :],
                                            start=m == 0, stop=m == TB - 1)
                        ins.then_inc(heads_out, 1)

            def early_sums(k):
                b_d, b_dd = stat_banks(k)
                pe.wait_ge(sums_ready, 2 * k + 2)
                pe.matmul(ps[:, b_d, 0:S], ones[:], fold_a[:], start=True, stop=False)
                pe.matmul(ps[:, b_dd, 0:S], ones[:], sum_dd[k][:, 0, :], start=True, stop=False)

            def last_sums(k):
                for i, (bank, rows_) in enumerate(zip(stat_banks(k), ((sum_d[k], (0, 1)), (squares[k], (0, 2))))):
                    for h in range(2):
                        pe.wait_ge(tail_sum, 4 * k + 2 * i + h + 1)
                        ins = pe.matmul(ps[:, bank, 0:S], ones[:], rows_[0][:, rows_[1][h], :], start=False, stop=h == 1)
                    ins.then_inc(stat_done, 1)

            def mix_out(l):
                k = 2 * l
                n_heads = HEAD0[l] + len(HEADS[l])
                for g in range(4):
                    gg = G_OUT[l] + g
                    banks_free(gg)
                    if l == 1 and g == 0:
                        pe.wait_ge(probs_t_ready, n_heads)
                    if l == 1 and g == 1:
                        pe.wait_ge(y_ready, n_heads)
                    for j in range(UG):
                        c = 2 * ((j + OUT_TURN) % UG)
                        if g == 0 and c < POOL_CHUNKS:
                            if l == 0:
                                pe.wait_ge(pool_y_ready, c // 4 + 1)
                            else:
                                pe.wait_ge(y_ready, HEAD0[1] + MEM_HEADS + c + 2)
                        elif g == 0:
                            pe.wait_ge(y_ready, HEAD0[l] + c - POOL_CHUNKS + 2)
                        if g == 1 and j == 4:
                            pe.wait_ge(col_sum, k + 1)
                            column_sums(stat_banks(k)[0], fold_a[:]).then_inc(stat_done, 1)
                        if g == 2 and j == 0:
                            pe.wait_ge(shift_ready, k + 1)
                        if g == 3 and j == 4:
                            early_sums(k)
                        multiply(U_OUT[l] + g * UG + j, gg, lambda cc: xy[:, c + cc, :], 2, first=j == 0,
                                 last=j == UG - 1, narrow=g == 3)
                if l == 0:
                    g = G_V[1]
                    banks_free(g)
                    for j in range(UG):
                        if j == 1:
                            last_sums(0)
                        multiply_rows(U_V[1] + j, g, lambda c: mem_hl[:, 2 * j + c, :], 2, first=j == 0,
                                      last=j == UG - 1)
                else:
                    last_sums(k)

            def ffn(l):
                k = 2 * l + 1
                with pe.Fori(0, FG) as i:
                    for h in range(2):
                        g = G_UP[l] + h
                        banks_free(g, i * 2)
                        if h == 0:
                            pe.wait_ge(var_ready, 2 * l + 1)
                        for j in range(UG):
                            if h == 0:
                                pe.wait_ge(x_ready, KC // 2 + NP * 2 * l + pieces_in(j))
                            multiply(U_UP[l] + h * UG + j, g, xy_chunk(j), 2, first=j == 0, last=j == UG - 1,
                                     turn=i * (2 * UG))
                flat = act_hl[:].rearrange("p a b -> p (a b)")
                loops = (DG - 6) // RING
                for g in range(4):
                    gg, u = G_DOWN[l] + g, U_DOWN[l] + g * DG
                    banks_free(gg)
                    if g == 2:
                        pe.wait_ge(shift_ready, k + 1)
                    for j in range(2):
                        pe.wait_ge(act_ready, FG * l + 1)
                        multiply(u + j, gg, lambda c: act_hl[:, 2 * j + c, :], 2, first=j == 0, narrow=g == 3)
                    pe.wait_ge(act_ready, FG * l + FG - 2)
                    with pe.Fori(0, loops) as i:
                        for j in range(RING):
                            multiply(u + 2 + j, gg,
                                     lambda c: flat[:, bass.ds(i * (2 * RING * 2 * S) + (4 + 2 * j + c) * 2 * S, 2 * S)],
                                     2, turn=i * RING, narrow=g == 3)
                    if g == 1:
                        pe.wait_ge(col_sum, k + 1)
                        column_sums(stat_banks(k)[0], fold_a[:]).then_inc(stat_done, 1)
                    if g == 3:
                        early_sums(k)
                    pe.wait_ge(act_ready, FG * l + FG)
                    for j in range(DG - RING, DG):
                        multiply(u + j, gg, lambda c: act_hl[:, 2 * j + c, :], 2, last=j == DG - 1,
                                 narrow=g == 3)
                last_sums(k)

            for g in range(4):
                banks_free(G_IN0 + g)
                for j in range(UG):
                    if g == 0:
                        pe.wait_ge(x_ready, j + 1)
                        if j == 0:
                            pe.wait_ge(x_ready, 8)
                    multiply(U_IN0 + g * UG + j, G_IN0 + g, xy_chunk(j), 2, first=j == 0, last=j == UG - 1)
            banks_free(G_K[1])
            memory_group(U_K[1], G_K[1], 0, range(4))
            pe.wait_ge(evacuated, G_K[1])
            attention(0, FIRST_STEPS)
            memory_group(U_K[1], G_K[1], 0, range(4, UG))
            attention(0, LAST_STEPS[0])
            pe.wait_ge(probs_t_ready, HEAD0[1])
            for r in range(6):
                u, g = U_GW + r, G_GW + r // 2
                s = u % RING
                if r == 2:
                    pe.wait_ge(y_ready, HEAD0[1])
                if r % 2 == 0:
                    banks_free(g)
                pe.wait_ge(lo_ready, u + 1)
                for h in range(2):
                    w, b = divmod(2 * r + h, GC)
                    pe.wait_ge(pooled_ready, w + 1)
                    bank = ps[:, bank_set(g) + 2 * (r % 2) + h, :]
                    for c in range(GC):
                        col = (h * GC + c) * P
                        pc = pooled[:, GC * w + c, :]
                        hi, lo = w_hi[:, s, col:col + P], w_lo[:, s, col:col + P]
                        if c == GC - 1:
                            pe.matmul(bank[:, S:2 * S], lo, pc[:, 0:S], start=False, stop=False)
                            ins = pe.matmul(bank, hi, pc, start=False, stop=True)
                        else:
                            pe.matmul(bank, hi, pc, start=c == 0, stop=False)
                            pe.matmul(bank[:, S:2 * S], lo, pc[:, 0:S], start=False, stop=False)
                ins.then_inc(units_done, 1)
            mix_out(0)
            ffn(0)

            g = G_IN1
            pe.wait_ge(var_ready, 2)
            for n in range(2):
                banks_free(g + n)
                for j in range(UG):
                    if n == 1 and j == 2:
                        pe.wait_ge(lat_sum, 1)
                        column_sums(bank_set(g), latent_sq[:, 0, :]).then_inc(lat_stat, 1)
                    pe.wait_ge(x_ready, KC // 2 + NP + pieces_in(j))
                    multiply(U_IN1 + n * UG + j, g + n, xy_chunk(j), 2, first=j == 0, last=j == UG - 1)
            pe.wait_ge(lat_var, 1)
            banks_free(g + 2)
            for r in range(2):
                multiply(U_IN1 + 2 * UG + r, g + 2, lambda c: xy[:, 8 * r + c, :], 8, nb=1, width=P,
                         first=r == 0, last=r == 1)
            pe.wait_ge(lat_sum, 2)
            column_sums(bank_set(g + 1), latent_sq[:, 0, :]).then_inc(lat_stat, 1)
            pe.wait_ge(lat_var, 2)
            banks_free(g + 3)
            for j in range(UG):
                multiply(U_IN1 + 2 * UG + 2 + j, g + 3, xy_chunk(j), 2, first=j == 0, last=j == UG - 1)
            pe.wait_ge(latent_ready, 1)
            for n in range(3):
                banks_free(G_UQ + n)
                for j in range(2):
                    multiply(U_UQ + 2 * n + j, G_UQ + n, lambda c: qn_hl[:, 2 * j + c, :], 2, first=j == 0, last=j == 1)
            for r in range(3):
                gg = G_QR + r // 2
                if r != 1:
                    banks_free(gg)
                s, b0 = (U_QR + r) % RING, bank_set(gg) + 2 * (r % 2)
                pe.wait_ge(lo_ready, U_QR + r + 1)
                for b in range(2):
                    for c in range(LC):
                        col = c * 256 + b * P
                        hi, lo = w_hi[:, s, col:col + P], w_lo[:, s, col:col + P]
                        bank, xc = ps[:, b0 + b, :], qn_hl[:, c, :]
                        if c == LC - 1:
                            pe.matmul(bank[:, S:2 * S], lo, xc[:, 0:S], start=False, stop=False)
                            ins = pe.matmul(bank, hi, xc, start=False, stop=True)
                        else:
                            pe.matmul(bank, hi, xc, start=c == 0, stop=False)
                            pe.matmul(bank[:, S:2 * S], lo, xc[:, 0:S], start=False, stop=False)
                ins.then_inc(units_done, 1)
            pe.wait_ge(latent_ready, 2)
            for n in range(3):
                banks_free(G_UK + n)
                for j in range(2):
                    multiply(U_UK + 2 * n + j, G_UK + n, lambda c: kvn_hl[:, 2 * j + c, :], 2, first=j == 0, last=j == 1)
            for n in range(3):
                if n == 1:
                    pe.wait_ge(evacuated, G_UV)
                    pe.wait_ge(kv_loaded, 16)
                    attention(1, FIRST_STEPS)
                banks_free(G_UV + n)
                for j in range(2):
                    multiply_rows(U_UV + 2 * n + j, G_UV + n, lambda c: kvn_hl[:, 2 * j + c, :], 2,
                                  first=j == 0, last=j == 1)
            pe.wait_ge(evacuated, G_UV + 2)
            attention(1, LAST_STEPS[1])
            mix_out(1)
            ffn(1)
            pe.wait_ge(var_ready, 4)
            pe.wait_ge(evacuated, G_DOWN[1] + 4)
            for j in range(KC // 2):
                pe.wait_ge(affine, NP * 3 + pieces_in(j))
                for t in range(TB):
                    for c in range(2):
                        ins = pe.transpose(ps[:, j, t * 2 * P + c * P:t * 2 * P + (c + 1) * P],
                                           res[:, 2 * j + c, t * P:(t + 1) * P], ident[:])
                ins.then_inc(final_turned, 1)


LN_EPS = 1e-5
RMS_EPS = 1e-6
_INS = ["x", "mem", "positions", "pool_w_in", "pool_group_w", "pool_scale", "pool_w_out", "mla_w_in", "mla_q_norm_g",
        "mla_kv_norm_g", "mla_w_uq", "mla_w_uk", "mla_w_uv", "mla_w_out", "mem_w_kv", "ln1_g", "ln1_b", "ln2_g",
        "ln2_b", "ffn_w_up", "ffn_conv_w", "ffn_conv_b", "ffn_w_down"]


def kernel(**inputs):
    import numpy as _np
    import concourse.bacc as _bacc
    from concourse import mybir as _mybir
    from concourse.bass_utils import run_bass_kernel_spmd as _run

    nc = _bacc.Bacc("TRN2", target_bir_lowering=False, num_devices=1)
    arrays, args = {}, []
    for name in _INS:
        a = _np.ascontiguousarray(inputs[name])
        arrays[f"in_{name}_dram"] = a
        args.append(nc.dram_tensor(f"in_{name}_dram", a.shape, _mybir.dt.from_np(a.dtype), kind="ExternalInput").ap())
    half = ROPE // 2
    freqs = _np.float32(10000.0) ** (-_np.arange(0, ROPE, 2, dtype=_np.float32) / _np.float32(ROPE))
    arrays["rotary_freq"] = _np.ascontiguousarray(_np.tile(freqs, P // half).reshape(P, 1).astype(_np.float32))
    args.append(nc.dram_tensor("rotary_freq", (P, 1), _mybir.dt.float32, kind="ExternalInput").ap())
    shape = inputs["x"].shape
    args.append(nc.dram_tensor("out_0_dram", shape, _mybir.dt.float32, kind="ExternalOutput").ap())
    encoder_trunk(nc, *args)
    r = _run(nc, [arrays], core_ids=[0])
    return r.results[0]["out_0_dram"]
```
